# Optimizing a Trainium2 kernel written in Bass

```python
import jax, jax.numpy as jnp
from jax import lax
import numpy as np
import math

D_MODEL = 1024
BATCH = 1
SEQ = 256
DEPTH = 1

HEAD_DIM = 64
NSA_HEADS = 8
NSA_KV_GROUPS = 2
NSA_HPG = NSA_HEADS // NSA_KV_GROUPS
NSA_WIDTH = NSA_HEADS * HEAD_DIM
NSA_KV_WIDTH = NSA_KV_GROUPS * HEAD_DIM
CMP_LEN = 32
CMP_STRIDE = 16
CMP_HIDDEN = 2 * HEAD_DIM
SLC_BLOCK = 64
SLC_TOPN = 16
WINDOW = 512
MOBA_HEADS = 8
MOBA_WIDTH = MOBA_HEADS * HEAD_DIM
MOBA_BLOCK = 256
MOBA_TOPK = 3
TOTAL_HEADS = NSA_HEADS + MOBA_HEADS
Q_CHUNK = 32
RMS_EPS = 1e-6
COL_WIDTHS = (NSA_WIDTH, 6 * NSA_KV_WIDTH, 3 * NSA_HEADS, NSA_WIDTH, 3 * MOBA_WIDTH, MOBA_WIDTH, 2 * D_MODEL)
IN_COLS = NSA_WIDTH + 6 * NSA_KV_WIDTH + 3 * NSA_HEADS + NSA_WIDTH + 3 * MOBA_WIDTH + MOBA_WIDTH + 2 * D_MODEL


def rms_norm(x, g):
    xf = x.astype(jnp.float32)
    y = xf * lax.rsqrt(jnp.mean(xf * xf, axis=-1, keepdims=True) + RMS_EPS)
    return (y * g.astype(jnp.float32)).astype(x.dtype)

def alibi_slopes(n):
    return jnp.asarray((2.0 ** (-8.0 * np.arange(1, n + 1) / n)).astype(np.float32))

def masked_softmax(s, mask):
    s = jnp.where(mask, s, -jnp.inf)
    m = jnp.max(s, axis=-1, keepdims=True)
    m = jnp.where(jnp.isfinite(m), m, 0.0)
    p = jnp.where(mask, jnp.exp(s - m), 0.0)
    return p / jnp.maximum(jnp.sum(p, axis=-1, keepdims=True), 1e-30)

def cmp_to_slc_matrix(n_cmp, n_slc):
    cs = np.arange(n_cmp) * CMP_STRIDE
    ce = cs + CMP_LEN - 1
    ss = np.arange(n_slc) * SLC_BLOCK
    se = ss + SLC_BLOCK - 1
    return ((cs[:, None] <= se[None, :]) & (ce[:, None] >= ss[None, :])).astype(np.float32)

def compress(k, pe, w1, w2):
    S = k.shape[2]
    n_cmp = (S - CMP_LEN) // CMP_STRIDE + 1
    idx = np.arange(n_cmp)[:, None] * CMP_STRIDE + np.arange(CMP_LEN)[None, :]
    blocks = k[:, :, idx] + pe
    h = jax.nn.silu(jnp.einsum('bgnld,lde->bgne', blocks, w1))
    return jnp.einsum('bgne,ef->bgnf', h, w2)

def nsa_attention(q, kc, vc, ks, vs, kw, vw, gates, slopes):
    B, G, P, S, hd = q.shape
    n_cmp = kc.shape[2]
    n_slc = S // SLC_BLOCK
    k_sel = min(SLC_TOPN, n_slc)
    scale = hd ** -0.5
    cmp_end = jnp.asarray(np.arange(n_cmp) * CMP_STRIDE + CMP_LEN - 1, jnp.int32)
    overlap = jnp.asarray(cmp_to_slc_matrix(n_cmp, n_slc))
    ks_b = ks.reshape(B, G, n_slc, SLC_BLOCK, hd)
    vs_b = vs.reshape(B, G, n_slc, SLC_BLOCK, hd)
    kw_p = jnp.pad(kw, ((0, 0), (0, 0), (WINDOW, 0), (0, 0)))
    vw_p = jnp.pad(vw, ((0, 0), (0, 0), (WINDOW, 0), (0, 0)))
    bi = jnp.arange(B)[:, None, None, None]
    gi = jnp.arange(G)[None, :, None, None]
    blk = jnp.arange(n_slc)
    in_blk = jnp.arange(SLC_BLOCK)
    win_off = jnp.arange(WINDOW + Q_CHUNK) - WINDOW
    sl = slopes.astype(jnp.float32)[None, :, :, None, None]

    def chunk(ci):
        c0 = ci * Q_CHUNK
        t = c0 + jnp.arange(Q_CHUNK)
        qc = lax.dynamic_slice_in_dim(q, c0, Q_CHUNK, axis=3)
        g = lax.dynamic_slice_in_dim(gates, c0, Q_CHUNK, axis=4)
        dist = t[:, None] - cmp_end[None, :]
        s = jnp.einsum('bgpqd,bgnd->bgpqn', qc, kc).astype(jnp.float32) * scale - sl * dist.astype(jnp.float32)
        p_cmp = masked_softmax(s, dist >= 0)
        o_cmp = jnp.einsum('bgpqn,bgnd->bgpqd', p_cmp.astype(vc.dtype), vc)
        imp = jnp.einsum('bgpqn,nj->bgqj', p_cmp, overlap)
        cur = t // SLC_BLOCK
        causal_blk = blk[None, :] <= cur[:, None]
        forced = (blk[None, :] == 0) | (blk[None, :] == cur[:, None]) | (blk[None, :] == cur[:, None] - 1)
        imp = jnp.where(forced, jnp.inf, imp)
        imp = jnp.where(causal_blk, imp, -jnp.inf)
        _, sel = lax.top_k(imp, k_sel)
        kg = ks_b[bi, gi, sel]
        vg = vs_b[bi, gi, sel]
        pos = (sel[..., None] * SLC_BLOCK + in_blk).reshape(B, G, 1, Q_CHUNK, k_sel * SLC_BLOCK)
        dist = t[:, None] - pos
        s = jnp.einsum('bgpqd,bgqkld->bgpqkl', qc, kg).reshape(B, G, P, Q_CHUNK, k_sel * SLC_BLOCK)
        s = s.astype(jnp.float32) * scale - sl * dist.astype(jnp.float32)
        p = masked_softmax(s, dist >= 0).astype(vg.dtype).reshape(B, G, P, Q_CHUNK, k_sel, SLC_BLOCK)
        o_slc = jnp.einsum('bgpqkl,bgqkld->bgpqd', p, vg)
        kwin = lax.dynamic_slice_in_dim(kw_p, c0, WINDOW + Q_CHUNK, axis=2)
        vwin = lax.dynamic_slice_in_dim(vw_p, c0, WINDOW + Q_CHUNK, axis=2)
        posw = c0 + win_off
        dist = t[:, None] - posw[None, :]
        mask = (posw[None, :] >= 0) & (dist >= 0) & (dist < WINDOW)
        s = jnp.einsum('bgpqd,bgkd->bgpqk', qc, kwin).astype(jnp.float32) * scale - sl * dist.astype(jnp.float32)
        p = masked_softmax(s, mask).astype(vwin.dtype)
        o_win = jnp.einsum('bgpqk,bgkd->bgpqd', p, vwin)
        return g[0][..., None] * o_cmp + g[1][..., None] * o_slc + g[2][..., None] * o_win

    out = lax.map(chunk, jnp.arange(S // Q_CHUNK))
    return out.transpose(1, 0, 4, 2, 3, 5).reshape(B, S, G * P * hd)

def moba_attention(q, k, v, slopes):
    B, H, S, hd = q.shape
    nb = -(-S // MOBA_BLOCK)
    pad = nb * MOBA_BLOCK - S
    kb = jnp.pad(k, ((0, 0), (0, 0), (0, pad), (0, 0))).reshape(B, H, nb, MOBA_BLOCK, hd)
    vb = jnp.pad(v, ((0, 0), (0, 0), (0, pad), (0, 0))).reshape(B, H, nb, MOBA_BLOCK, hd)
    kbar = jnp.mean(kb.astype(jnp.float32), axis=3)
    k_sel = min(MOBA_TOPK, nb)
    scale = hd ** -0.5
    bi = jnp.arange(B)[:, None, None, None]
    hi = jnp.arange(H)[None, :, None, None]
    offs = jnp.arange(MOBA_BLOCK)
    blocks = jnp.arange(nb)
    sl = slopes.astype(jnp.float32)[None, :, None, None]

    def chunk(ci):
        c0 = ci * Q_CHUNK
        t = c0 + jnp.arange(Q_CHUNK)
        cur = c0 // MOBA_BLOCK
        qc = lax.dynamic_slice_in_dim(q, c0, Q_CHUNK, axis=2)
        gate = jnp.einsum('bhqd,bhnd->bhqn', qc.astype(jnp.float32), kbar)
        gate = jnp.where(blocks < cur, gate, -jnp.inf)
        _, sel = lax.top_k(gate, k_sel)
        valid = sel < cur
        kg = kb[bi, hi, sel]
        vg = vb[bi, hi, sel]
        ko = lax.dynamic_index_in_dim(kb, cur, axis=2, keepdims=False)
        vo = lax.dynamic_index_in_dim(vb, cur, axis=2, keepdims=False)
        n_sel = k_sel * MOBA_BLOCK
        s_sel = jnp.einsum('bhqd,bhqkld->bhqkl', qc, kg).reshape(B, H, Q_CHUNK, n_sel)
        s_own = jnp.einsum('bhqd,bhld->bhql', qc, ko)
        s = jnp.concatenate([s_sel, s_own], axis=-1).astype(jnp.float32) * scale
        pos_sel = (sel[..., None] * MOBA_BLOCK + offs).reshape(B, H, Q_CHUNK, n_sel)
        pos_own = jnp.broadcast_to(cur * MOBA_BLOCK + offs, (B, H, Q_CHUNK, MOBA_BLOCK))
        pos = jnp.concatenate([pos_sel, pos_own], axis=-1)
        dist = t[:, None] - pos
        mask_sel = jnp.broadcast_to(valid[..., None], (B, H, Q_CHUNK, k_sel, MOBA_BLOCK)).reshape(B, H, Q_CHUNK, n_sel)
        mask = jnp.concatenate([mask_sel, dist[..., n_sel:] >= 0], axis=-1)
        s = s - sl * dist.astype(jnp.float32)
        p = masked_softmax(s, mask).astype(v.dtype)
        p_sel = p[..., :n_sel].reshape(B, H, Q_CHUNK, k_sel, MOBA_BLOCK)
        p_own = p[..., n_sel:]
        return jnp.einsum('bhqkl,bhqkld->bhqd', p_sel, vg) + jnp.einsum('bhql,bhld->bhqd', p_own, vo)

    out = lax.map(chunk, jnp.arange(S // Q_CHUNK))
    return out.transpose(1, 0, 3, 2, 4).reshape(B, S, H * hd)

def hybrid_layer(x, norm_pre, w_in, pe_k, w1_k, w2_k, pe_v, w1_v, w2_v, w_a, w_b, w_o, norm_post):
    B, S, _ = x.shape
    G, P, hd = NSA_KV_GROUPS, NSA_HPG, HEAD_DIM
    u = rms_norm(x, norm_pre)
    proj = u @ w_in
    splits = [int(c) for c in np.cumsum(COL_WIDTHS)[:-1]]
    q_a, kv_a, g_a, z_a, qkv_b, z_b, merge = jnp.split(proj, splits, axis=-1)
    slopes = alibi_slopes(TOTAL_HEADS)
    q_a = q_a.reshape(B, S, G, P, hd).transpose(0, 2, 3, 1, 4)
    kv_a = kv_a.reshape(B, S, 6, G, hd).transpose(2, 0, 3, 1, 4)
    kc = compress(kv_a[0], pe_k, w1_k, w2_k)
    vc = compress(kv_a[1], pe_v, w1_v, w2_v)
    gates_a = jax.nn.sigmoid(g_a).reshape(B, S, 3, G, P).transpose(2, 0, 3, 4, 1)
    o_a = nsa_attention(q_a, kc, vc, kv_a[2], kv_a[3], kv_a[4], kv_a[5], gates_a,
                        slopes[0::2].reshape(G, P))
    y_a = o_a * jax.nn.silu(z_a)
    qkv_b = qkv_b.reshape(B, S, 3, MOBA_HEADS, hd).transpose(2, 0, 3, 1, 4)
    o_b = moba_attention(qkv_b[0], qkv_b[1], qkv_b[2], slopes[1::2])
    y_b = o_b * jax.nn.silu(z_b)
    gate_a, gate_b = jnp.split(merge, 2, axis=-1)
    m = jax.nn.sigmoid(gate_a) * (y_a @ w_a) + jax.nn.sigmoid(gate_b) * (y_b @ w_b)
    return x + rms_norm(m @ w_o, norm_post)

def first_inputs(seed: int = 0) -> dict:
    key = jax.random.key(seed)
    ks = jax.random.split(key, 13)

    def nrm(k, shape, s):
        return jax.random.normal(k, shape, jnp.float32) * s

    return {
        'x': nrm(ks[0], (BATCH, SEQ, D_MODEL), 1.0),
        'norm_pre': 1.0 + nrm(ks[1], (DEPTH, D_MODEL), 0.1),
        'w_in': nrm(ks[2], (DEPTH, D_MODEL, IN_COLS), D_MODEL ** -0.5),
        'cmp_pe_k': nrm(ks[3], (DEPTH, CMP_LEN, HEAD_DIM), 0.1),
        'cmp_w1_k': nrm(ks[4], (DEPTH, CMP_LEN, HEAD_DIM, CMP_HIDDEN), (CMP_LEN * HEAD_DIM) ** -0.5),
        'cmp_w2_k': nrm(ks[5], (DEPTH, CMP_HIDDEN, HEAD_DIM), CMP_HIDDEN ** -0.5),
        'cmp_pe_v': nrm(ks[6], (DEPTH, CMP_LEN, HEAD_DIM), 0.1),
        'cmp_w1_v': nrm(ks[7], (DEPTH, CMP_LEN, HEAD_DIM, CMP_HIDDEN), (CMP_LEN * HEAD_DIM) ** -0.5),
        'cmp_w2_v': nrm(ks[8], (DEPTH, CMP_HIDDEN, HEAD_DIM), CMP_HIDDEN ** -0.5),
        'w_branch_a': nrm(ks[9], (DEPTH, NSA_WIDTH, D_MODEL), NSA_WIDTH ** -0.5),
        'w_branch_b': nrm(ks[10], (DEPTH, MOBA_WIDTH, D_MODEL), MOBA_WIDTH ** -0.5),
        'w_o': nrm(ks[11], (DEPTH, D_MODEL, D_MODEL), D_MODEL ** -0.5),
        'norm_post': 1.0 + nrm(ks[12], (DEPTH, D_MODEL), 0.1),
    }

def first_block(x, norm_pre, w_in, cmp_pe_k, cmp_w1_k, cmp_w2_k, cmp_pe_v, cmp_w1_v, cmp_w2_v,
              w_branch_a, w_branch_b, w_o, norm_post):
    h = x
    for l in range(DEPTH):
        h = hybrid_layer(h, norm_pre[l], w_in[l], cmp_pe_k[l], cmp_w1_k[l], cmp_w2_k[l],
                         cmp_pe_v[l], cmp_w1_v[l], cmp_w2_v[l], w_branch_a[l], w_branch_b[l],
                         w_o[l], norm_post[l])
    return h


GRID_W = 64
CTX_LEN = 256

H_A = 8
KV_A = 2
G_A = H_A // KV_A
DH_A = 64
WINDOW_2 = 128
BLOCK = 128
BAND = BLOCK + 2 * WINDOW_2

H_B = 8
NOPE_B = 64
ROPE_B = 32
V_B = 64
Q_RANK = 384
KV_RANK = 256
MLA_SCALE = (NOPE_B + ROPE_B) ** -0.5

W_QA = H_A * DH_A
W_KA = KV_A * DH_A
W_VA = KV_A * DH_A
IN_WIDTHS = (W_QA, W_KA, W_VA, Q_RANK, KV_RANK, ROPE_B)
IN_DIM = sum(IN_WIDTHS)
SPLIT_POINTS = tuple(int(v) for v in np.cumsum(IN_WIDTHS)[:-1])
MIX_DIM = H_A * DH_A + H_B * V_B

N_EXPERTS = 16
CAP_FACTOR = 2
D_FF = 512

ROPE_BASE = 10000.0
EPS = 1e-6


def rmsnorm(x, w):
    xf = x.astype(jnp.float32)
    y = xf * lax.rsqrt(jnp.mean(xf * xf, axis=-1, keepdims=True) + EPS)
    return (y * w.astype(jnp.float32)).astype(x.dtype)

def modulate(h, shift, scale):
    return h * (1 + scale) + shift

def axial_rope(x, rows, cols):
    d = x.shape[-1]
    da = d // 2
    nf = da // 2
    inv = ROPE_BASE ** (-jnp.arange(nf, dtype=jnp.float32) / nf)

    def rot(xa, pos):
        ang = pos.astype(jnp.float32)[:, None] * inv[None, :]
        cos = jnp.cos(ang)[None, :, None, :]
        sin = jnp.sin(ang)[None, :, None, :]
        x1, x2 = xa[..., :nf], xa[..., nf:]
        return jnp.concatenate([x1 * cos - x2 * sin, x1 * sin + x2 * cos], axis=-1)

    xf = x.astype(jnp.float32)
    out = jnp.concatenate([rot(xf[..., :da], rows), rot(xf[..., da:], cols)], axis=-1)
    return out.astype(x.dtype)

def gqa_sink_attend(qb, keys, vals, bias, sink_g):
    s = jnp.einsum('bqkgd,bskd->bkgqs', qb, keys, preferred_element_type=jnp.float32) * (DH_A ** -0.5)
    if bias is not None:
        s = s + bias
    b, q = qb.shape[0], qb.shape[1]
    s_sink = jnp.broadcast_to(sink_g.astype(jnp.float32)[None, :, :, None, None], (b, KV_A, G_A, q, 1))
    p = jax.nn.softmax(jnp.concatenate([s, s_sink], axis=-1), axis=-1)[..., :-1]
    o = jnp.einsum('bkgqs,bskd->bqkgd', p.astype(vals.dtype), vals)
    return o.reshape(b, q, H_A * DH_A)

def window_attention_latent(q, k, v, kc, vc, sink_g):
    b, s_len = q.shape[:2]
    lc = kc.shape[1]
    nb = s_len // BLOCK
    qg = q.reshape(b, s_len, KV_A, G_A, DH_A)
    pad = ((0, 0), (WINDOW_2, WINDOW_2), (0, 0), (0, 0))
    kp = jnp.pad(k, pad)
    vp = jnp.pad(v, pad)
    ctx_bias = jnp.zeros((BLOCK, lc), jnp.float32)

    def block(i):
        start = i * BLOCK
        qb = lax.dynamic_slice_in_dim(qg, start, BLOCK, axis=1)
        kb = lax.dynamic_slice_in_dim(kp, start, BAND, axis=1)
        vb = lax.dynamic_slice_in_dim(vp, start, BAND, axis=1)
        tq = start + jnp.arange(BLOCK)
        ts = start - WINDOW_2 + jnp.arange(BAND)
        valid = (jnp.abs(tq[:, None] - ts[None, :]) <= WINDOW_2) & (ts[None, :] >= 0) & (ts[None, :] < s_len)
        band_bias = jnp.where(valid, 0.0, -jnp.inf).astype(jnp.float32)
        keys = jnp.concatenate([kc, kb], axis=1)
        vals = jnp.concatenate([vc, vb], axis=1)
        bias = jnp.concatenate([ctx_bias, band_bias], axis=1)
        return gqa_sink_attend(qb, keys, vals, bias, sink_g)

    out = lax.map(block, jnp.arange(nb))
    return jnp.transpose(out, (1, 0, 2, 3)).reshape(b, s_len, H_A * DH_A)

def mla_attend(qn, qr, kn, kr, v):
    s = (jnp.einsum('bqhd,bkhd->bhqk', qn, kn, preferred_element_type=jnp.float32)
         + jnp.einsum('bqhr,bkr->bhqk', qr, kr, preferred_element_type=jnp.float32)) * MLA_SCALE
    p = jax.nn.softmax(s, axis=-1)
    o = jnp.einsum('bhqk,bkhd->bqhd', p.astype(v.dtype), v)
    return o.reshape(qn.shape[0], qn.shape[1], H_B * V_B)

def mla_latent(qn, qr, kn, kr, v):
    b, s_len = qn.shape[:2]
    nb = s_len // BLOCK

    def block(i):
        start = i * BLOCK
        qnb = lax.dynamic_slice_in_dim(qn, start, BLOCK, axis=1)
        qrb = lax.dynamic_slice_in_dim(qr, start, BLOCK, axis=1)
        return mla_attend(qnb, qrb, kn, kr, v)

    out = lax.map(block, jnp.arange(nb))
    return jnp.transpose(out, (1, 0, 2, 3)).reshape(b, s_len, H_B * V_B)

def project_groups(t, w_in, q_norm, kv_norm, w_q_up, w_kv_up):
    bt, n = t.shape[:2]
    p = jnp.einsum('bsd,de->bse', t, w_in)
    qa, ka, va, cq, ckv, kr = jnp.split(p, SPLIT_POINTS, axis=-1)
    qa = qa.reshape(bt, n, H_A, DH_A)
    ka = ka.reshape(bt, n, KV_A, DH_A)
    va = va.reshape(bt, n, KV_A, DH_A)
    qb = jnp.einsum('bsr,re->bse', rmsnorm(cq, q_norm), w_q_up).reshape(bt, n, H_B, NOPE_B + ROPE_B)
    kvb = jnp.einsum('bsr,re->bse', rmsnorm(ckv, kv_norm), w_kv_up).reshape(bt, n, H_B, NOPE_B + V_B)
    return (qa, ka, va, qb[..., :NOPE_B], qb[..., NOPE_B:], kr,
            kvb[..., :NOPE_B], kvb[..., NOPE_B:])

def token_mixers(h, hc, rows, cols, w_in, sink, q_norm, kv_norm, w_q_up, w_kv_up, w_out, with_ctx_out):
    sink_g = sink.reshape(KV_A, G_A)
    qa, ka, va, qbn, qbr, kr, kbn, vb = project_groups(h, w_in, q_norm, kv_norm, w_q_up, w_kv_up)
    qa_c, ka_c, va_c, qbn_c, qbr_c, kr_c, kbn_c, vb_c = project_groups(hc, w_in, q_norm, kv_norm, w_q_up, w_kv_up)
    qa = axial_rope(qa, rows, cols)
    ka = axial_rope(ka, rows, cols)
    qbr = axial_rope(qbr, rows, cols)
    kr = axial_rope(kr[:, :, None, :], rows, cols)[:, :, 0, :]
    o_a = window_attention_latent(qa, ka, va, ka_c, va_c, sink_g)
    o_b = mla_latent(qbn, qbr,
                     jnp.concatenate([kbn_c, kbn], axis=1),
                     jnp.concatenate([kr_c, kr], axis=1),
                     jnp.concatenate([vb_c, vb], axis=1))
    out = jnp.einsum('bse,ed->bsd', jnp.concatenate([o_a, o_b], axis=-1), w_out)
    if not with_ctx_out:
        return out, None
    lc = hc.shape[1]
    o_a_c = gqa_sink_attend(qa_c.reshape(hc.shape[0], lc, KV_A, G_A, DH_A), ka_c, va_c, None, sink_g)
    o_b_c = mla_attend(qbn_c, qbr_c, kbn_c, kr_c, vb_c)
    out_c = jnp.einsum('bse,ed->bsd', jnp.concatenate([o_a_c, o_b_c], axis=-1), w_out)
    return out, out_c

def ec_moe(h, w_router, w_gate, w_up, w_down):
    n = h.shape[1]
    cap = CAP_FACTOR * n // N_EXPERTS
    aff = jax.nn.softmax(jnp.einsum('bnd,de->bne', h, w_router, preferred_element_type=jnp.float32), axis=-1)
    vals, idx = lax.top_k(jnp.swapaxes(aff, 1, 2), cap)

    def per_sample(hs, idx_s, val_s):
        xs = hs[idx_s]
        a = jnp.einsum('ecd,edf->ecf', xs, w_gate)
        u = jnp.einsum('ecd,edf->ecf', xs, w_up)
        y = jnp.einsum('ecf,efd->ecd', jax.nn.silu(a) * u, w_down) * val_s[..., None].astype(hs.dtype)
        return jnp.zeros_like(hs).at[idx_s.reshape(-1)].add(y.reshape(-1, hs.shape[-1]).astype(hs.dtype))

    return jax.vmap(per_sample)(h, idx, vals)

def second_inputs(seed: int = 0) -> dict:
    key = jax.random.key(seed)
    ks = jax.random.split(key, 20)
    f32 = jnp.float32
    L = DEPTH

    def nrm(k, shape, scale):
        return jax.random.normal(k, shape, f32) * scale

    return {
        "x": nrm(ks[0], (BATCH, SEQ, D_MODEL), 1.0),
        "c": nrm(ks[1], (BATCH, D_MODEL), 1.0),
        "ctx": nrm(ks[2], (BATCH, CTX_LEN, D_MODEL), 1.0),
        "c_ctx": nrm(ks[3], (D_MODEL,), 1.0),
        "w_mod": nrm(ks[4], (L, D_MODEL, 6 * D_MODEL), 0.5 * D_MODEL ** -0.5),
        "b_mod": nrm(ks[5], (L, 6 * D_MODEL), 0.01),
        "norm_attn": 1.0 + nrm(ks[6], (L, D_MODEL), 0.02),
        "norm_ffn": 1.0 + nrm(ks[7], (L, D_MODEL), 0.02),
        "w_in": nrm(ks[8], (L, D_MODEL, IN_DIM), D_MODEL ** -0.5),
        "sink": nrm(ks[9], (L, H_A), 0.5),
        "q_norm": 1.0 + nrm(ks[10], (L, Q_RANK), 0.02),
        "kv_norm": 1.0 + nrm(ks[11], (L, KV_RANK), 0.02),
        "w_q_up": nrm(ks[12], (L, Q_RANK, H_B * (NOPE_B + ROPE_B)), Q_RANK ** -0.5),
        "w_kv_up": nrm(ks[13], (L, KV_RANK, H_B * (NOPE_B + V_B)), KV_RANK ** -0.5),
        "w_out": nrm(ks[14], (L, MIX_DIM, D_MODEL), MIX_DIM ** -0.5),
        "w_router": nrm(ks[15], (L, D_MODEL, N_EXPERTS), D_MODEL ** -0.5),
        "w_gate": nrm(ks[16], (L, N_EXPERTS, D_MODEL, D_FF), D_MODEL ** -0.5),
        "w_up": nrm(ks[17], (L, N_EXPERTS, D_MODEL, D_FF), D_MODEL ** -0.5),
        "w_down": nrm(ks[18], (L, N_EXPERTS, D_FF, D_MODEL), D_FF ** -0.5),
        "norm_final": 1.0 + nrm(ks[19], (D_MODEL,), 0.02),
    }

def second_block(x, c, ctx, c_ctx, w_mod, b_mod, norm_attn, norm_ffn, w_in, sink, q_norm, kv_norm,
              w_q_up, w_kv_up, w_out, w_router, w_gate, w_up, w_down, norm_final):
    n_lat = x.shape[1]
    ROWS = n_lat // GRID_W
    rows = jnp.repeat(jnp.arange(ROWS, dtype=jnp.int32), GRID_W)
    cols = jnp.tile(jnp.arange(GRID_W, dtype=jnp.int32), ROWS)
    xc = ctx
    for l in range(DEPTH):
        last = l == DEPTH - 1
        mod = jnp.einsum('bd,de->be', jax.nn.silu(c), w_mod[l]) + b_mod[l]
        mod_c = jnp.einsum('d,de->e', jax.nn.silu(c_ctx), w_mod[l]) + b_mod[l]
        sh_a, sc_a, g_a, sh_f, sc_f, g_f = [m[:, None, :] for m in jnp.split(mod, 6, axis=-1)]
        csh_a, csc_a, cg_a, csh_f, csc_f, cg_f = jnp.split(mod_c, 6, axis=-1)

        h = modulate(rmsnorm(x, norm_attn[l]), sh_a, sc_a)
        hc = modulate(rmsnorm(xc, norm_attn[l]), csh_a, csc_a)
        mix, mix_c = token_mixers(h, hc, rows, cols, w_in[l], sink[l], q_norm[l], kv_norm[l],
                                  w_q_up[l], w_kv_up[l], w_out[l], not last)
        x = x + g_a * mix
        h2 = modulate(rmsnorm(x, norm_ffn[l]), sh_f, sc_f)
        x = x + g_f * ec_moe(h2, w_router[l], w_gate[l], w_up[l], w_down[l])

        if not last:
            xc = xc + cg_a * mix_c
            h2c = modulate(rmsnorm(xc, norm_ffn[l]), csh_f, csc_f)
            xc = xc + cg_f * ec_moe(h2c, w_router[l], w_gate[l], w_up[l], w_down[l])
    return rmsnorm(x, norm_final)


def setup_inputs(seed=0):
    out = dict(first_inputs(seed))
    for name, value in second_inputs(seed + 1).items():
        if name != "x":
            out[name + "_2"] = value
    return out


def reference(
    x, norm_pre, w_in, cmp_pe_k, cmp_w1_k, cmp_w2_k, cmp_pe_v, cmp_w1_v, cmp_w2_v, w_branch_a,
    w_branch_b, w_o, norm_post, c_2, ctx_2, c_ctx_2, w_mod_2, b_mod_2, norm_attn_2, norm_ffn_2,
    w_in_2, sink_2, q_norm_2, kv_norm_2, w_q_up_2, w_kv_up_2, w_out_2, w_router_2, w_gate_2,
    w_up_2, w_down_2, norm_final_2,
):
    x = first_block(
        x, norm_pre, w_in, cmp_pe_k, cmp_w1_k, cmp_w2_k, cmp_pe_v, cmp_w1_v, cmp_w2_v,
        w_branch_a, w_branch_b, w_o, norm_post,
    )
    return second_block(
        x, c_2, ctx_2, c_ctx_2, w_mod_2, b_mod_2, norm_attn_2, norm_ffn_2, w_in_2, sink_2,
        q_norm_2, kv_norm_2, w_q_up_2, w_kv_up_2, w_out_2, w_router_2, w_gate_2, w_up_2,
        w_down_2, norm_final_2,
    )


_drawn_inputs = setup_inputs


def setup_inputs(seed=0):
    import zlib

    import numpy as np

    out = dict(_drawn_inputs(seed))
    spreads = {}
    factors = {'cmp_pe_k': 8.0,
     'ctx_2': 4.127,
     'b_mod_2': 8.0,
     'norm_attn_2': 8.0,
     'norm_ffn_2': 8.0,
     'sink_2': 8.0,
     'q_norm_2': 8.0,
     'kv_norm_2': 8.0,
     'w_q_up_2': 4.202}
    for name, (base, spread) in spreads.items():
        noise = np.random.default_rng([zlib.crc32(name.encode()), seed]).standard_normal(out[name].shape)
        drawn = base * np.exp(spread * noise) if base else spread * noise
        out[name] = __import__('jax').numpy.asarray(drawn.astype(out[name].dtype))
    for name, factor in factors.items():
        out[name] = (out[name] * factor).astype(out[name].dtype)
    return out
```

```python
from contextlib import ExitStack

import numpy as np

import concourse.bass as bass
from concourse import mybir

F32 = mybir.dt.float32
ALU = mybir.AluOpType
ACT = mybir.ActivationFunctionType
AX_X = mybir.AxisListType.X

P = 128
S = 256
TOK = S // P
D = 1024
KC = D // P
HD = 64
EPS = 1e-6
FAR = 1e30
SLOT = 4096
RING = 4

N_CMP = 15
CMPW = 16
LP = 16
CAUSAL = P + S

XP = 1440
KA, VA, CKV, CQ, KR = 512, 640, 768, 1024, 1408
CP = 544
QR, KVR = 384, 256
HB, NOPE, ROPE, QK = 8, 64, 32, 96
MLA_SCALE = float(QK) ** -0.5
E = 16
CAP = 32
FF = 512
EG = 4
NG = E // EG

STREAM = (["W0", "W1", "W2", "W3", "M0", "WC", "W4", "M1", "W5", "M2", "W6", "M3", "W7", "M4", "W8", "M5",
           "W9", "M6", "WA", "M7", "W10", "M8", "W11", "M9", "C0", "WB", "M10", "M11", "C1", "WO0", "WO1", "KU0",
           "X0", "X1", "X2", "QU", "KU1", "OUT0", "OUT1"]
          + [f"{m}{g}.{i}" for g in range(NG) for m in ("G", "U", "D") for i in range(4)])
N_DENSE = STREAM.index("G0.0")
EXTRA = {4: "queries and keys", 5: "MLA's keys", 6: "projections", 7: "values"}
EXPERT_CYCLE = [3, 0, 4, 5, 6, 7, 1, 2]
BUFFER = [n % RING for n in range(N_DENSE)] + [EXPERT_CYCLE[n % 8] for n in range(len(STREAM) - N_DENSE)]
TURN = [BUFFER[:n + 1].count(BUFFER[n]) for n in range(len(STREAM))]

DENSE = ["xT00", "xT01", "xT10", "xT11", "qa0", "qa1", "kvc", "kvs", "kvw", "ga",
         "qb0", "qb1", "cH", "kb0", "kb1", "cT", "vb0", "cK", "vb1", "cS", "za0", "za1", "cP", "zb0", "zb1",
         "cO0", "cO1", "gA00", "gA10", "yaT0", "yaT1", "modT0", "gA01", "gA11", "wa00", "wa01", "wa10", "wa11",
         "ybT0", "ybT1", "gB00", "gB10", "cxT00", "cxT01", "cxT10", "cxT11", "gB01", "gB11", "ck0", "ck1",
         "wb00", "wb01", "wb10", "wb11", "cc0", "cc1", "mT00", "mT01", "mT10", "mT11", "modT1",
         "wo00", "wo01", "wo10", "wo11", "clT", "ckv00", "ckv01", "ckv10", "ckv11", "hT00", "hT01",
         "bG0", "bG1", "modT2", "bF0", "bF1", "kc0", "kc1", "kc2", "kc3", "hT10", "hT11",
         "xa00", "xa01", "xa02", "xa10", "xa11", "xa12",
         "qwT0", "lq0", "lk0", "qu00", "qu01", "xkv00", "xkv01",
         "qwT1", "kwT", "lq1", "lk1", "qu10", "qu11", "xkv10", "xkv11",
         "qm0", "qm1", "qm2", "qm3", "kx0", "kx1", "kx2", "kx3"]
TAIL = (["oT00", "oT10", "oT01", "oT11", "ou00", "ou01", "ou10", "ou11",
         "rT00", "rT01", "rT10", "rT11", "lg", "afT", "slT"]
        + [f"gx{c}" for c in range(KC)] + ["ohT0", "ohT1"])
OT_ROUND = 20
GROUPS = DENSE + TAIL
BANK_OF = {name: n % 2 for n, name in enumerate(GROUPS)}
USE_OF = {name: n // 2 + 1 for n, name in enumerate(GROUPS)}

MOD_AFTER = {"qb1": 0, "kb1": 1, "vb1": 2, "za1": 3, "zb1": 4, "gA10": 5, "gA11": 6, "wa11": 7,
             "gB10": 8, "gB11": 9, "wb01": 10, "wb11": 11}

LAST_USE = {"W0": "qa1", "W1": "kvs", "W2": "ga", "W3": "qb1", "W4": "kb1", "W5": "vb1", "W6": "za1", "W7": "zb1",
            "W8": "gA10", "W9": "gA11", "W10": "gB10", "W11": "gB11", "WA": "wa11", "WB": "wb11", "WC": "cH",
            "C0": "ck1", "C1": "cc1", "KU0": "ckv11", "WO0": "wo10", "WO1": "wo11", "X0": "xa10", "X1": "xa11",
            "X2": "xa12", "QU": "qu11", "KU1": "xkv11", "OUT0": "ou10", "OUT1": "ou11"}

NSA, WIN, MOBA = range(3)
UNITS = [(NSA, j) for j in range(4)] + [(WIN, j) for j in range(4)] + [(MOBA, j) for j in range(4)]
ROUND_AFTER = {name: r for r, name in enumerate(
    ["qb0", "qb1", "kb0", "kb1", "vb0", "vb1", "za0", "za1", "zb0", "zb1", "gA00", "gA10", "gA01", "gA11"])}


def schedule():
    out = []
    for name in DENSE:
        out.append(("dense", name))
        if name in MOD_AFTER:
            out.append(("mod", MOD_AFTER[name]))
        if name in ROUND_AFTER:
            r = ROUND_AFTER[name]
            if r < len(UNITS):
                out.append(("score", r))
            if 0 <= r - 1 < len(UNITS):
                out.append(("turn", r - 1))
            if 0 <= r - 2:
                out.append(("pv", r - 2))
        if name == "cO1":
            out.append(("ya", 0))
        if name == "gA11":
            out.append(("yb", 0))
        if name == "wa11":
            out.append(("context", 0))
    return out


SCHEDULE = schedule()


def alibi(n):
    return [float(np.float32(2.0 ** (-8.0 * k / n))) for k in range(1, n + 1)]


def build(nc, A, out):
    ctx = ExitStack()
    with ctx:
        def sem(name):
            return ctx.enter_context(nc.semaphore(name))

        def sb(name, cols):
            return ctx.enter_context(nc.sbuf_tensor(name, [P, cols], F32))

        ring = sb("ring", RING * SLOT)
        x_sb = sb("x_sb", TOK * D)
        tz = sb("tz", 4096)
        turned = tz[:, 0:2048]
        zz = tz[:, 2048:4096]
        rows = sb("rows", TOK * D)
        tabs = sb("tabs", 4096)
        mo = sb("mo", 4096)
        qk = sb("qk", 5120)
        vvc = sb("vvc", 6656)
        vv = vvc[:, 0:1536]
        vc = vvc[:, 1536:6656]
        sp = sb("sp", 1536)
        pt = sb("pt", 1536)
        lat = sb("lat", 1792)
        ident = sb("ident", P)
        modr = sb("modr", 1536)
        rope = sb("rope", 384)
        small = sb("small", 1400)

        used = {}

        def view(tensor, start, cols, pattern=None, **sizes):
            v = tensor[:, start:start + cols]
            return v.rearrange(pattern, **sizes) if pattern else v

        def tiny(cols):
            a = used.get("small", 0)
            used["small"] = a + cols
            assert a + cols <= 1400
            return small[:, a:a + cols]

        def slot(name):
            b = BUFFER[STREAM.index(name)]
            if b < RING:
                return ring[:, b * SLOT:(b + 1) * SLOT]
            return {4: qk, 5: tabs, 6: mo, 7: vvc}[b][:, 0:SLOT]

        xn = x_sb[:, :].rearrange("p (t d) -> p t d", t=TOK)
        rn = rows[:, :].rearrange("p (t d) -> p t d", t=TOK)
        uT = turned[:, :].rearrange("p (c s) -> p c s", c=KC)
        table = view(tabs, 0, 8 * CAUSAL, "p (h k) -> p h k", h=8)
        eg = view(mo, 0, 2048, "p (t d) -> p t d", t=TOK)
        oa = view(mo, 2048, 1024, "p (t d) -> p t d", t=TOK)
        ob = view(mo, 3072, 1024, "p (t d) -> p t d", t=TOK)
        qaT = view(qk, 0, 1024, "p (j s) -> p j s", j=4)
        ksD = view(qk, 1024, 512, "p (g s) -> p g s", g=2)
        kwD = view(qk, 1536, 512, "p (g s) -> p g s", g=2)
        qbT = view(qk, 2048, 1024, "p (j s) -> p j s", j=4)
        kbD = view(qk, 3072, 2048, "p (j g s) -> p j g s", j=4, g=2)
        za = view(zz, 0, 1024, "p (t d) -> p t d", t=TOK)
        zb = view(zz, 1024, 1024, "p (t d) -> p t d", t=TOK)
        vS = view(vv, 0, 256, "p (t d) -> p t d", t=TOK)
        vW = view(vv, 256, 256, "p (t d) -> p t d", t=TOK)
        vB = view(vv, 512, 1024, "p (t d) -> p t d", t=TOK)
        kvT = view(vc, 0, 512, "p (i s) -> p i s", i=2)
        kv2 = view(vc, 512, 1024, "p (i g s) -> p i g s", i=2, g=2)
        blk = view(vc, 1536, 960, "p (i l n) -> p i l n", i=2, l=LP)
        cE = view(vc, 2496, 256)
        cH = view(vc, 2752, 256)
        hkT = view(vc, 3008, 30)
        hvR = view(vc, 3072, 256, "p (g h n) -> p g h n", g=2, h=4)
        w2k = view(vc, 3328, 128)
        w2v = view(vc, 3456, 64)
        kcD = view(vc, 3520, 32, "p (g n) -> p g n", g=2)
        vcD = view(vc, 3552, 512, "p (g d) -> p g d", g=2)
        cB = view(vc, 4064, 256)
        cM = view(vc, 4320, 256)
        cS = view(vc, 4576, 256)
        cP = view(vc, 512, 512, "p (i h n) -> p i h n", i=4, h=4)
        cPT = view(vc, 1024, 512, "p (i q) -> p i q", i=4)
        pe = view(vc, 4832, 32, "p (i l) -> p i l", i=2)
        spn = sp[:, :].rearrange("p (u b k) -> p u b k", u=2, b=2)
        ptn = pt[:, :].rearrange("p (u b k) -> p u b k", u=2, b=2)
        yT = view(lat, 0, 1024, "p (c s) -> p c s", c=4)
        post = view(vc, 2048, 1024)

        hcT = zz[:, :].rearrange("p (c s) -> p c s", c=KC)
        cn = view(vc, 0, 2048, "p (t d) -> p t d", t=TOK)
        px = view(mo, 0, TOK * XP, "p (t d) -> p t d", t=TOK)
        pc = view(mo, TOK * XP, TOK * CP, "p (t d) -> p t d", t=TOK)
        kcat = view(qk, 0, 3072, "p (t h d) -> p t h d", t=2 * TOK, h=HB)
        qcat = view(qk, 3072, 1536, "p (t h d) -> p t h d", t=TOK, h=HB)
        kP = view(vv, 0, 1024, "p (g s) -> p g s", g=2)
        rt = view(sp, 0, 1280, "p (i d) -> p i d", i=2)
        gG = view(vc, 3072, 1024)
        gF = view(vc, 4096, 1024)
        vm = view(vc, 0, 2048, "p (t h d) -> p t h d", t=2 * TOK, h=HB)
        qwT = view(pt, 0, 1024, "p (j s) -> p j s", j=4)
        xv = view(vv, 1024, 256)
        lqT = view(lat, 0, 768, "p (c s) -> p c s", c=3)
        lkT = view(lat, 768, 512, "p (c s) -> p c s", c=2)
        lcT = view(lat, 1280, 512, "p (c s) -> p c s", c=2)
        qmT = turned[:, :].rearrange("p (h s) -> p h s", h=HB)
        kmT = tabs[:, :].rearrange("p (h s) -> p h s", h=HB)
        wB = view(modr, 0, 1024, "p (t k) -> p t k", t=TOK)
        oT0 = view(pt, 0, 1024, "p (c s) -> p c s", c=4)
        o2 = zz[:, :].rearrange("p (t d) -> p t d", t=TOK)
        sp3 = sp[:, :].rearrange("p (u k) -> p u k", u=3)
        pt2 = view(mo, 0, 1024, "p (u k) -> p u k", u=2)
        mod = modr[:, :].rearrange("p (r n) -> p r n", r=3)
        pick = view(lat, 0, 512, "p (j q) -> p j q", j=4)

        nfin = gG
        xsT = tz[:, :].rearrange("p (c s) -> p c s", c=KC)
        oh = view(modr, 0, 1024, "p (t s) -> p t s", t=TOK)
        ohv = view(lat, 768, 1024, "p (t s) -> p t s", t=TOK)
        ohT = view(qk, 4096, 1024, "p (g s) -> p g s", g=NG)
        hE = view(sp, 0, 512)
        hA = view(sp, 512, 512)
        hT = view(sp, 1024, 512)
        yE = view(pt, 0, 1024)

        gcol = tiny(KC)
        nat = tiny(KC)
        nff = tiny(KC)
        bmod = tiny(48)
        modc = tiny(96)
        mc = modc.rearrange("p (v q) -> p v q", v=2)
        qn = tiny(3)
        kvn = tiny(2)
        sink = tiny(8)
        iota = tiny(CAP)
        wr = tiny(KC * E).rearrange("p (c e) -> p c e", c=KC)
        cc = tiny(2 * KC)
        ccE = tiny(2 * KC)
        csil = tiny(KC * 32).rearrange("p (c v) -> p c v", c=KC)
        gates = tiny(48).rearrange("p (t i) -> p t i", t=TOK)
        ss = tiny(16)
        rs = tiny(16)
        half = tiny(4)
        mx = tiny(8).rearrange("p (u i) -> p u i", u=2)
        nm = tiny(8).rearrange("p (u i) -> p u i", u=2)
        sums = tiny(48).rearrange("p (u i) -> p u i", u=12)
        rc = tiny(48).rearrange("p (u i) -> p u i", u=12)
        cst = tiny(48).rearrange("p (i n) -> p i n", i=3)
        mx2 = tiny(32)
        nm2 = tiny(32)
        sm2 = tiny(32)
        sk2 = tiny(32)
        rc2 = tiny(32)
        scl = tiny(4 * KC).rearrange("p (i c) -> p i c", i=4)
        aff = tiny(32).rearrange("p (t e) -> p t e", t=TOK)
        slt = tiny(32).rearrange("p (t e) -> p t e", t=TOK)
        rst = tiny(8)
        affT = view(pt, 1024, 256)
        work = view(pt, 1280, 256)
        top8 = tiny(8)
        msk = view(lat, 0, 256)
        cum = view(lat, 256, 256)
        zer = view(lat, 512, 256)

        bank = [ctx.enter_context(nc.psum_tensor(f"bank{i}", [P, 512], F32)) for i in range(8)]
        DB = bank[0:2]
        MB = bank[2]
        SB = bank[3:5]
        TB = bank[5:7]
        VB = bank[7]
        OB = (VB, MB)

        slot_in = [sem(f"slot_in{i}") for i in range(RING + len(EXTRA))]
        mod_used = sem("mod_used")
        e_used = sem("e_used")
        d_ready = [sem(f"d_ready{i}") for i in range(2)]
        d_free = [sem(f"d_free{i}") for i in range(2)]
        x_in = [sem(f"x_in{t}") for t in range(TOK)]
        early_in = sem("early_in")
        const_in = sem("const_in")
        nsa_table_in = sem("nsa_table_in")
        moba_table_in = sem("moba_table_in")
        ctx_in = sem("ctx_in")
        post_in = sem("post_in")
        wmask_in = sem("wmask_in")
        bg_in = sem("bg_in")
        bf_in = sem("bf_in")
        fin_in = sem("fin_in")
        out_done = sem("out_done")
        kv2_in = sem("kv2_in")
        zeroed = sem("zeroed")
        picked = sem("picked")
        kp_zeroed = sem("kp_zeroed")
        squares = sem("squares")
        means = sem("means")
        roots = sem("roots")
        normed = sem("normed")
        tanhs = sem("tanhs")
        cond_tanh = sem("cond_tanh")
        cond_ready = sem("cond_ready")
        mod_kept = sem("mod_kept")
        scores = sem("scores")
        masked = sem("masked")
        maxed = sem("maxed")
        exps = sem("exps")
        turns = sem("turns")
        turned_a = sem("turned_a")
        turned_b = sem("turned_b")
        pvs = sem("pvs")
        outs = sem("outs")
        blocks_ready = sem("blocks_ready")
        c_act = sem("c_act")
        c_vec = sem("c_vec")
        ya_ready = sem("ya_ready")
        yb_ready = sem("yb_ready")
        m_ready = sem("m_ready")
        x1_ready = sem("x1_ready")
        roped = sem("roped")
        lat_ready = sem("lat_ready")
        cat_ready = sem("cat_ready")
        u_scores = sem("u_scores")
        u_masked = sem("u_masked")
        u_neg = sem("u_neg")
        u_exp = sem("u_exp")
        u_turn = sem("u_turn")
        u_turned_a = sem("u_turned_a")
        u_turned_v = sem("u_turned_v")
        u_pv = sem("u_pv")
        u_out = sem("u_out")
        u_sink = sem("u_sink")
        x2_ready = sem("x2_ready")
        logit_max = sem("logit_max")
        logit_exp = sem("logit_exp")
        aff_ready = sem("aff_ready")
        slots_ready = sem("slots_ready")
        oh_ready = sem("oh_ready")
        e_tanh = sem("e_tanh")
        e_h = sem("e_h")
        e_turn = sem("e_turn")
        e_hT = sem("e_hT")
        e_y = sem("e_y")
        e_y2 = sem("e_y2")
        e_out = sem("e_out")
        f_in = sem("f_in")
        y_ready = sem("y_ready")
        dve_step = sem("dve_step")
        act_step = sem("act_step")
        pool_step = sem("pool_step")

        def D_(name):
            return DB[BANK_OF[name]]

        def filled(eng, name):
            eng.wait_ge(d_ready[BANK_OF[name]], USE_OF[name])

        def kept(eng, name):
            eng.wait_ge(d_free[BANK_OF[name]], USE_OF[name])

        def released(eng, name):
            if name in LAST_USE:
                filled(eng, LAST_USE[name])
            elif name[0] == "M":
                eng.wait_ge(mod_used, int(name[1:]) + 1)
            else:
                group, part = name[1:].split(".")
                eng.wait_ge(e_used, 12 * int(group) + 4 * "GUD".index(name[0]) + int(part) + 1)

        def experts_done(eng, stage, g):
            released(eng, f"{stage}{g}.3")

        def leave(ins, name):
            ins.then_inc(d_free[BANK_OF[name]], 1)

        def bc(t, n):
            return t.rearrange("p (k n) -> p k n", n=1).to_broadcast([P, t.shape[1], n])

        def over(t, n):
            return t.rearrange("p (n k) -> p n k", n=1).to_broadcast([P, n, t.shape[1]])

        def mla_turned(name):
            i = 2 * int(name[2])
            return {"qm": qmT, "kx": kmT[:, :, S:2 * S], "kc": kmT[:, :, 0:S]}[name[:2]][0:QK, i:i + 2, :]

        block = ctx.enter_context(nc.Block())

        @block.sync
        def _(eng):
            stream = A["stream"]
            for t in range(TOK):
                eng.dma_start(xn[:, t, :], A["x"][t * P:(t + 1) * P, :]).then_inc(x_in[t], 16)
            for n, name in enumerate(STREAM):
                b = BUFFER[n]
                before = [k for k in range(n) if BUFFER[k] == b]
                if before:
                    released(eng, STREAM[before[-1]])
                elif b == 4:
                    filled(eng, "kx2")
                    filled(eng, "kx3")
                elif b == 5:
                    eng.wait_ge(u_scores, 32)
                elif b >= 6:
                    eng.wait_ge(u_pv, 32)
                eng.dma_start(slot(name), stream[n, :, :]).then_inc(slot_in[b], 16)
                if name == "W2":
                    eng.dma_start(tabs[:, 0:8 * CAUSAL], A["nsa_table"]).then_inc(nsa_table_in, 16)
                if name == "W9":
                    kept(eng, "cO1")
                    eng.dma_start(cn, A["ctx"].rearrange("(t p) d -> p t d", p=P)).then_inc(ctx_in, 16)
                    eng.dma_start(post, A["norm_post"].to_broadcast([P, D])).then_inc(post_in, 16)
                    eng.dma_start(gG, A["b_mod"][:, 2 * D:3 * D].to_broadcast([P, D])).then_inc(bg_in, 16)
                    eng.dma_start(gF, A["b_mod"][:, 5 * D:6 * D].to_broadcast([P, D])).then_inc(bf_in, 16)
            for t in range(TOK):
                eng.wait_ge(y_ready, t + 1)
                eng.dma_start(out[t * P:(t + 1) * P, :], xn[:, t, :]).then_inc(out_done, 16)
            eng.wait_ge(out_done, 16 * TOK)

        @block.scalar
        def _(eng):
            act = nc.scalar
            steps = [0]

            def own(ins):
                steps[0] += 1
                ins.then_inc(act_step, 1)
                eng.wait_ge(act_step, steps[0])

            eng.dma_start(ident[:, :], A["ident"]).then_inc(early_in, 16)
            eng.dma_start(gcol, A["norm_pre"]).then_inc(early_in, 16)
            def copy(dst, src, name=None, scale=1.0):
                ins = act.activation(dst, src, ACT.Copy, scale=scale)
                if name:
                    leave(ins, name)
                return ins

            n_sq = [0]

            def sum_squares(src, k, junk):
                if n_sq[0]:
                    eng.wait_ge(squares, n_sq[0])
                act.activation(junk, src, ACT.Square, accum_out=ss[:, k:k + 1]).then_inc(squares, 1)
                n_sq[0] += 1

            for t in range(TOK):
                eng.wait_ge(x_in[t], 16)
                sum_squares(xn[:, t, :], t, pt[:, 0:D])
            n_const = 0
            for dst, name in ((w2k, "w2k"), (w2v, "w2v"), (cB, "cmp_bias"), (cM, "cmp_mask"), (view(vc, 4832, 32), "pe"),
                              (rope[:, :], "rope"), (nat, "norm_attn"), (nff, "norm_ffn"), (bmod, "b_mod_cols"),
                              (qn, "q_norm"), (kvn, "kv_norm"), (iota, "iota"), (cc, "cond"),
                              (wr.rearrange("p c e -> p (c e)"), "w_router")):
                eng.dma_start(dst, A[name]).then_inc(const_in, 16)
                n_const += 1
            eng.dma_start(sink, A["sink"].to_broadcast([P, 8])).then_inc(const_in, 16)

            def turned_mod(name, dst, add, mult):
                filled(eng, name)
                t = int(name[-2])
                for c in range(4):
                    k = 4 + c
                    ins = act.activation(dst[:, k, t * P:(t + 1) * P], D_(name)[:, c * P:(c + 1) * P], ACT.Identity,
                                         bias=add[:, k:k + 1], scale=mult[:, k:k + 1])
                leave(ins, name)

            for kind, n in SCHEDULE:
                if kind == "score":
                    u = n
                    eng.wait_ge(maxed, u + 1)
                    for b in range(2):
                        for q in range(TOK):
                            k = spn[:, u % 2, b, P * q:P + S * q]
                            ins = act.activation(k, k, ACT.Exp, bias=nm[:, u % 2, 2 * b + q:2 * b + q + 1],
                                                 accum_out=sums[:, u, 2 * b + q:2 * b + q + 1])
                    ins.then_inc(exps, 1)
                elif kind == "turn":
                    u = n
                    eng.wait_ge(turns, u + 1)
                    if u >= 2:
                        eng.wait_ge(pvs, u - 1)
                    copy(ptn[:, u % 2, 0, :], TB[0][:, 0:CAUSAL]).then_inc(turned_a, 1)
                elif kind == "dense":
                    name = n
                    if name in ("qa0", "qa1", "qb0", "qb1"):
                        filled(eng, name)
                        i = int(name[2])
                        dst = qaT if name[1] == "a" else qbT
                        copy(dst[:, 2 * i:2 * i + 2, :], D_(name)[:, :].rearrange("p (j s) -> p j s", j=2), name, HD ** -0.5)
                    elif name in ("vb0", "vb1"):
                        filled(eng, name)
                        copy(vB[:, int(name[2]), :], D_(name)[:, :], name)
                    elif name == "ga":
                        filled(eng, name)
                        leave(act.activation(gates, D_(name)[:, 0:48].rearrange("p (t i) -> p t i", t=TOK), ACT.Tanh,
                                             scale=0.5), name)
                        eng.wait_ge(const_in, 16 * (n_const + 1))
                        act.activation(ccE, cc, ACT.Tanh, scale=0.5).then_inc(cond_tanh, 1)
                    elif name == "kvs":
                        kept(eng, "kvc")
                        for g in range(2):
                            src = kvT[64 * g:64 * g + 64, :, :]
                            eng.dma_start(kv2[0:64, :, g, :], src).then_inc(kv2_in, 16)
                            eng.dma_start(kv2[64:128, :, g, 0:S - 1], src[:, :, 1:S]).then_inc(kv2_in, 16)
                    elif name in ("za0", "za1", "zb0", "zb1"):
                        filled(eng, name)
                        dst = za if name[1] == "a" else zb
                        act.activation(dst[:, int(name[2]), :], D_(name)[:, :], ACT.Tanh, scale=0.5)\
                           .then_inc(tanhs, 1)
                    elif name[:2] in ("gA", "gB"):
                        filled(eng, name)
                        t, h = int(name[2]), int(name[3])
                        if name[:2] == "gB":
                            kept(eng, f"wa{t}{h}")
                        leave(act.activation(eg[:, t, 512 * h:512 * h + 512], D_(name)[:, :], ACT.Tanh, scale=0.5), name)
                    elif name == "cH":
                        filled(eng, name)
                        act.activation(cE[0:30, :], D_(name)[0:30, 0:256], ACT.Tanh, scale=0.5).then_inc(c_act, 1)
                    elif name == "cS":
                        eng.wait_ge(c_vec, 2)
                        act.activation(cS, cS, ACT.Exp).then_inc(c_act, 1)
                    elif name == "cP":
                        filled(eng, name)
                        copy(cPT, D_(name)[:, :].rearrange("p (i q) -> p i q", i=4), name)
                    elif name[:3] in ("yaT", "ybT"):
                        filled(eng, name)
                        t = int(name[3])
                        copy(yT[:, :, t * P:(t + 1) * P], D_(name)[:, :].rearrange("p (c s) -> p c s", c=4), name, 0.5)
                    elif name[:2] == "mT":
                        filled(eng, name)
                        t, h = int(name[2]), int(name[3])
                        copy(uT[:, 4 * h:4 * h + 4, t * P:(t + 1) * P],
                             D_(name)[:, :].rearrange("p (c s) -> p c s", c=4), name, 0.5)
                    elif name in ("cxT01", "cxT11"):
                        turned_mod(name, hcT, mc[:, 1, 0:8], scl[:, 1, :])
                    elif name in ("hT01", "hT11"):
                        turned_mod(name, uT, mc[:, 0, 0:8], scl[:, 0, :])
                    elif name in ("ck0", "ck1"):
                        filled(eng, name)
                        copy(pc[:, int(name[2]), 0:256], D_(name)[:, 0:256], name)
                    elif name in ("cc0", "cc1"):
                        filled(eng, name)
                        t = int(name[2])
                        copy(pc[:, t, 256:544], D_(name)[:, 0:288], name)
                        kept(eng, name)
                        sum_squares(pc[:, t, 256:512], 6 + t, pt[:, 0:256])
                    elif name[:2] == "wo":
                        filled(eng, name)
                        t, h = int(name[2]), int(name[3])
                        copy(rn[:, t, 512 * h:512 * h + 512], D_(name)[:, :], name)
                        if h == 1:
                            kept(eng, f"wo{t}0")
                            kept(eng, name)
                            sum_squares(rn[:, t, :], 4 + t, sp[:, 0:D])
                            eng.wait_ge(x1_ready, t + 1)
                            sum_squares(xn[:, t, :], 8 + t, sp[:, 0:D])
                    elif name == "bF1":
                        kept(eng, "modT2")
                        kept(eng, "bG0")
                        kept(eng, "bG1")
                        eng.dma_start(modr[:, 0:1024], A["window_mask"]).then_inc(wmask_in, 16)
                    elif name[:2] == "xa":
                        filled(eng, name)
                        t, h = int(name[2]), int(name[3])
                        w = 512 if h < 2 else 416
                        copy(px[:, t, 512 * h:512 * h + w], D_(name)[:, 0:w], name)
                        if h == 2:
                            kept(eng, name)
                            kept(eng, f"xa{t}1")
                            sum_squares(px[:, t, CQ:CQ + QR], 10 + 2 * t, pt[:, 1024:1024 + QR])
                            sum_squares(px[:, t, CKV:CKV + KVR], 11 + 2 * t, pt[:, 1024:1024 + KVR])
                    elif name in ("qwT0", "qwT1"):
                        filled(eng, name)
                        t = int(name[3])
                        copy(qwT[:, :, t * P:(t + 1) * P], D_(name)[:, :].rearrange("p (j s) -> p j s", j=4), name,
                             HD ** -0.5)
                    elif name[:2] == "qu":
                        filled(eng, name)
                        t, h = int(name[2]), int(name[3])
                        w = 480 if h == 0 else 288
                        copy(qcat[:, t, :, :].rearrange("p h d -> p (h d)")[:, 480 * h:480 * h + w], D_(name)[:, 0:w], name)
                    elif name[:3] in ("ckv", "xkv"):
                        filled(eng, name)
                        t, h = int(name[3]), int(name[4])
                        tk = t if name[0] == "c" else TOK + t
                        src = D_(name)[:, :].rearrange("p (h d) -> p h d", h=4)
                        copy(kcat[:, tk, 4 * h:4 * h + 4, 0:NOPE], src[:, :, 0:64])
                        leave(copy(vm[:, tk, 4 * h:4 * h + 4, :], src[:, :, 64:128]), name)
                    elif name[:2] in ("qm", "kx", "kc") and int(name[2]) % 2 == 0:
                        filled(eng, name)
                        copy(mla_turned(name), D_(name)[0:QK, :].rearrange("p (h s) -> p h s", h=2), name)

            def soften(u):
                eng.wait_ge(u_neg, u + 1)
                if u < 16:
                    act.activation(sp3[:, u % 3, :], sp3[:, u % 3, :], ACT.Exp, bias=nm2[:, u:u + 1],
                                   accum_out=sm2[:, u:u + 1]).then_inc(u_exp, 1)
                    h = (u // 2) % 2 * 4 + u // 4
                    act.activation(sk2[:, u:u + 1], sink[:, h:h + 1], ACT.Exp, bias=nm2[:, u:u + 1]).then_inc(u_sink, 1)
                else:
                    eng.wait_ge(u_turn, u - 2)
                    act.activation(sp3[:, u % 3, :], SB[u % 2][:, :], ACT.Exp, bias=nm2[:, u:u + 1], scale=MLA_SCALE,
                                   accum_out=sm2[:, u:u + 1]).then_inc(u_exp, 1)

            def turned_out(name):
                filled(eng, name)
                t, h = int(name[2]), int(name[3])
                copy(uT[:, 4 * h:4 * h + 4, t * P:(t + 1) * P] if h else oT0[:, :, t * P:(t + 1) * P],
                     D_(name)[:, :].rearrange("p (c s) -> p c s", c=4), name)

            for r in range(34):
                if r < 32:
                    soften(r)
                if 1 <= r <= 32 and (r - 1) % 2 == 0:
                    u = r - 1
                    eng.wait_ge(u_turn, u + 1)
                    if u >= 2:
                        eng.wait_ge(u_pv, u - 1)
                    copy(pt2[:, 0, :], TB[0][:, :]).then_inc(u_turned_a, 1)
                if r in (OT_ROUND, OT_ROUND + 1):
                    turned_out(f"oT{r - OT_ROUND}0")

            for name in TAIL:
                if name in ("oT01", "oT11"):
                    turned_out(name)
                elif name == "ou01" or name == "ou11":
                    t = int(name[2])
                    eng.wait_ge(x2_ready, t + 1)
                    sum_squares(xn[:, t, :], 14 + t, sp[:, 0:D])
                elif name in ("rT01", "rT11"):
                    turned_mod(name, uT, mc[:, 0, 24:32], scl[:, 2, :])
                    if name == "rT11":
                        eng.dma_start(nfin, A["norm_final"].to_broadcast([P, D])).then_inc(fin_in, 16)
                elif name == "lg":
                    eng.wait_ge(logit_max, 1)
                    act.activation(aff, aff, ACT.Exp).then_inc(logit_exp, 1)
                elif name[:2] == "gx" and int(name[2]) % 2 == 0:
                    c = int(name[2])
                    filled(eng, name)
                    leave(act.activation(xsT[:, c, :], D_(name)[:, :], ACT.Identity, bias=mc[:, 0, 24 + c:25 + c],
                                         scale=scl[:, 2, c:c + 1]), name)
                elif name[:3] == "ohT":
                    filled(eng, name)
                    i = int(name[3])
                    copy(ohT[:, 2 * i:2 * i + 2, :], D_(name)[:, :].rearrange("p (g s) -> p g s", g=2), name)

            for g in range(NG):
                experts_done(eng, "G", g)
                if g:
                    eng.wait_ge(e_h, g)
                act.activation(hE, bank[0][:, :], ACT.Tanh, scale=0.5).then_inc(e_tanh, 1)
                eng.wait_ge(e_turn, g + 1)
                copy(hT, bank[0][:, :], scale=0.5).then_inc(e_hT, 1)
                experts_done(eng, "D", g)
                if g:
                    eng.wait_ge(e_out, g)
                copy(yE[:, 0:512], bank[2][:, :]).then_inc(e_y, 1)
            for t in range(TOK):
                eng.wait_ge(f_in, t + 1)
                sum_squares(xn[:, t, :], t, sp[:, 0:D])

        @block.gpsimd
        def _(eng):
            pool = nc.gpsimd
            pool.memset(half[:, 2:3], -0.5)
            pool.memset(qk[:, 1024:2048], 0.0)
            pool.memset(qk[:, 3072:5120], 0.0)
            pool.memset(csil, 0.0)
            pool.memset(view(vc, 3072, 256), 0.0)
            pool.memset(view(vc, 3520, 544), 0.0).then_inc(zeroed, 1)
            eng.wait_ge(zeroed, 1)
            for n, (k, w) in enumerate([(0, 1), (1, 1), (2, 2), (6, 2), (4, 1), (8, 1), (5, 1), (9, 1), (10, 2), (12, 2),
                                        (14, 1), (15, 1), (0, 1), (1, 1)]):
                eng.wait_ge(means, n + 1)
                pool.tensor_tensor(rs[:, k:k + w], ss[:, k:k + w], half[:, 2:3].to_broadcast([P, w]), ALU.pow)\
                    .then_inc(roots, 1)
                if n == 1:
                    eng.wait_ge(blocks_ready, 2)
                    pool.memset(view(vc, 512, 512), 0.0).then_inc(zeroed, 1)
                    eng.wait_ge(masked, 8)
                    eng.dma_start(tabs[:, 0:8 * CAUSAL], A["moba_table"]).then_inc(moba_table_in, 16)
                if n == 3:
                    kept(eng, "wb11")
                    pool.memset(lat[:, 0:512], 0.0).then_inc(pool_step, 1)
                    eng.wait_ge(pool_step, 1)
                    for j in range(4):
                        pool.memset(pick[32 * j:32 * j + 1, j, :], 1.0).then_inc(picked, 1)
                        eng.wait_ge(picked, j + 1)
                    pool.memset(vv[:, 0:1024], 0.0).then_inc(kp_zeroed, 1)

        @block.tensor
        def _(eng):
            pe_ = nc.tensor

            def loaded(name):
                n = STREAM.index(name)
                eng.wait_ge(slot_in[BUFFER[n]], 16 * TURN[n])

            def begin(name):
                if USE_OF[name] >= 2:
                    eng.wait_ge(d_free[BANK_OF[name]], USE_OF[name] - 1)
                return D_(name)

            def turn(dst, src, n=P, m=P):
                return pe_.transpose(dst, src, ident[0:n, 0:n])

            def turn_tiles(name, src, cols=P):
                o = begin(name)
                for c in range(4):
                    ins = turn(o[:, c * P:(c + 1) * P], src[:, c * P:(c + 1) * P])
                ins.then_inc(d_ready[BANK_OF[name]], 1)

            def product(o, lhs, rhs, chunks):
                for c in range(chunks):
                    ins = pe_.matmul(o, lhs(c), rhs(c), start=(c == 0), stop=(c == chunks - 1))
                return ins

            def turned_product(name, w, col, dst=0, src=None):
                return product(D_(name)[:, dst:dst + S], lambda c: w[:, c, col:col + P],
                               lambda c: (src or uT)[:, c, :], KC)

            def rows_product(name, w, col, width, t, src, dst=0, chunks=KC):
                return product(D_(name)[:, dst:dst + width], lambda c: src[:, c, t * P:(t + 1) * P],
                               lambda c: w[:, c, col:col + width], chunks)

            def weights(name, chunks, width):
                return slot(name)[:, 0:chunks * width].rearrange("p (c n) -> p c n", c=chunks)

            def done(ins, name):
                ins.then_inc(d_ready[BANK_OF[name]], 1)

            def dense(name):
                if name[:2] == "xT":
                    t, h = int(name[2]), int(name[3])
                    if name == "xT00":
                        eng.wait_ge(early_in, 32)
                    eng.wait_ge(normed, t + 1)
                    turn_tiles(name, rn[:, t, 512 * h:512 * h + 512])
                elif name in ("qa0", "qa1", "qb0", "qb1", "kb0", "kb1"):
                    i = int(name[2])
                    sl = {"qa": "W0", "qb": "W3", "kb": "W4"}[name[:2]]
                    if i == 0:
                        loaded(sl)
                        if name == "qa0":
                            for x in ("xT00", "xT01", "xT10", "xT11"):
                                kept(eng, x)
                    begin(name)
                    w = weights(sl, KC, 512)
                    turned_product(name, w, 256 * i, 0)
                    done(turned_product(name, w, 256 * i + P, S), name)
                elif name == "kvc":
                    loaded("W1")
                    begin(name)
                    w = weights("W1", KC, 512)
                    turned_product(name, w, 0, 0)
                    done(turned_product(name, w, P, S), name)
                elif name in ("kvs", "kvw"):
                    if name == "kvw":
                        loaded("W2")
                    begin(name)
                    w, col = (weights("W1", KC, 512), 256) if name == "kvs" else (weights("W2", KC, 280), 0)
                    turned_product(name, w, col, 0)
                    rows_product(name, w, col + P, P, 0, uT, S)
                    done(rows_product(name, w, col + P, P, 1, uT, S + P), name)
                elif name == "ga":
                    begin(name)
                    w = weights("W2", KC, 280)
                    rows_product(name, w, 256, 24, 0, uT, 0)
                    done(rows_product(name, w, 256, 24, 1, uT, 24), name)
                elif name[:2] in ("vb", "za", "zb", "gA", "gB"):
                    t = int(name[2])
                    sl = {"vb": "W5", "za": "W6", "zb": "W7", "gA": "W8", "gB": "W10"}[name[:2]]
                    if name[:2] in ("gA", "gB") and name[3] == "1":
                        sl = {"gA": "W9", "gB": "W11"}[name[:2]]
                    if t == 0:
                        loaded(sl)
                    begin(name)
                    done(rows_product(name, weights(sl, KC, 512), 0, 512, t, uT), name)
                elif name == "cH":
                    loaded("WC")
                    eng.wait_ge(blocks_ready, 2)
                    begin(name)
                    w = slot("WC").rearrange("p (i l e) -> p i l e", i=2, l=LP)
                    for i in range(2):
                        ins = product(D_(name)[0:30, i * P:(i + 1) * P], lambda c: blk[:, i, c, :],
                                      lambda c: w[:, i, c, :], LP)
                    done(ins, name)
                elif name == "cT":
                    eng.wait_ge(c_vec, 1)
                    begin(name)
                    for i in range(2):
                        ins = turn(D_(name)[:, 32 * i:32 * i + 30], cH[0:30, i * P:(i + 1) * P], 30)
                    done(ins, name)
                elif name == "cK":
                    kept(eng, "cT")
                    begin(name)
                    pe_.matmul(D_(name)[:, 0:30], w2k, hkT, start=True, stop=True)
                    for g in range(2):
                        ins = pe_.matmul(D_(name)[:, 64 + 64 * g:128 + 64 * g],
                                         hvR[:, g, :, :].rearrange("p h n -> p (h n)"), w2v, start=True, stop=True)
                    done(ins, name)
                elif name == "cS":
                    kept(eng, "cK")
                    begin(name)
                    for q in range(TOK):
                        for j in range(4):
                            a = (q * 4 + j) * 32
                            ins = pe_.matmul(D_(name)[:, a:a + 32], qaT[:, j, q * P:(q + 1) * P],
                                             kcD.rearrange("p g n -> p (g n)"), start=True, stop=True)
                    done(ins, name)
                elif name == "cP":
                    eng.wait_ge(c_vec, 3)
                    begin(name)
                    for i in range(4):
                        ins = turn(D_(name)[:, i * P:(i + 1) * P], cP[:, i, :, :].rearrange("p h n -> p (h n)"))
                    done(ins, name)
                elif name in ("cO0", "cO1"):
                    kept(eng, "cP")
                    q = int(name[2])
                    begin(name)
                    for g in range(2):
                        ins = pe_.matmul(D_(name)[:, 256 * g:256 * g + 256], cPT[:, 2 * q + g, :], vcD[:, g, :],
                                         start=True, stop=True)
                    done(ins, name)
                elif name[:3] in ("yaT", "ybT"):
                    eng.wait_ge(ya_ready if name[1] == "a" else yb_ready, 1)
                    turn_tiles(name, (oa if name[1] == "a" else ob)[:, int(name[3]), :])
                elif name[:2] in ("wa", "wb"):
                    t, h = int(name[2]), int(name[3])
                    if (t, h) == (0, 0):
                        loaded("WA" if name[1] == "a" else "WB")
                        for i in range(2):
                            kept(eng, f"y{name[1]}T{i}")
                    begin(name)
                    w = weights("WA" if name[1] == "a" else "WB", 4, D)
                    done(rows_product(name, w, 512 * h, 512, t, yT, 0, 4), name)
                elif name[:2] == "mT":
                    t, h = int(name[2]), int(name[3])
                    if h == 0:
                        eng.wait_ge(m_ready, 2 * t + 2)
                    turn_tiles(name, rn[:, t, 512 * h:512 * h + 512])
                elif name[:4] == "modT":
                    r = int(name[4])
                    eng.wait_ge(mod_kept, r + 1)
                    turn_tiles(name, mod[:, r, :])
                elif name[:3] == "cxT":
                    t, h = int(name[3]), int(name[4])
                    eng.wait_ge(normed, 3 + t)
                    turn_tiles(name, cn[:, t, 512 * h:512 * h + 512])
                elif name in ("ck0", "ck1", "cc0", "cc1"):
                    t = int(name[2])
                    if t == 0:
                        loaded("C0" if name[1] == "k" else "C1")
                        for x in ("cxT00", "cxT01", "cxT10", "cxT11"):
                            kept(eng, x)
                    begin(name)
                    width = 256 if name[1] == "k" else 288
                    w = weights("C0" if name[1] == "k" else "C1", KC, width)
                    done(rows_product(name, w, 0, width, t, hcT), name)
                elif name == "clT":
                    eng.wait_ge(lat_ready, 1)
                    begin(name)
                    for c in range(2):
                        for t in range(TOK):
                            ins = turn(D_(name)[:, c * S + t * P:c * S + (t + 1) * P], pc[:, t, 256 + c * P:256 + (c + 1) * P])
                    done(ins, name)
                elif name[:3] in ("ckv", "xkv"):
                    t, h = int(name[3]), int(name[4])
                    sl = "KU0" if name[0] == "c" else "KU1"
                    if (t, h) == (0, 0):
                        loaded(sl)
                        if name[0] == "c":
                            kept(eng, "clT")
                    if h == 0 and name[0] == "x":
                        kept(eng, f"lk{t}")
                    begin(name)
                    done(rows_product(name, weights(sl, 2, D), 512 * h, 512, t, lcT if name[0] == "c" else lkT, 0, 2),
                         name)
                elif name[:2] == "wo":
                    t, h = int(name[2]), int(name[3])
                    if t == 0:
                        loaded(f"WO{h}")
                    if h == 0:
                        for i in range(2):
                            kept(eng, f"mT{t}{i}")
                    begin(name)
                    done(rows_product(name, weights(f"WO{h}", KC, 512), 0, 512, t, uT), name)
                elif name[:2] in ("bG", "bF"):
                    h = int(name[2])
                    eng.wait_ge(picked, 4)
                    begin(name)
                    r, j = (1, h) if name[1] == "G" else (2, 2 + h)
                    done(pe_.matmul(D_(name)[:, :], pick[:, j, :], mod[:, r, :], start=True, stop=True), name)
                elif name[:2] == "hT":
                    t, h = int(name[2]), int(name[3])
                    eng.wait_ge(normed, 5 + t)
                    turn_tiles(name, rn[:, t, 512 * h:512 * h + 512])
                elif name[:2] == "xa":
                    t, h = int(name[2]), int(name[3])
                    if t == 0:
                        loaded(f"X{h}")
                    if h == 0:
                        for i in range(2):
                            kept(eng, f"hT{t}{i}")
                    begin(name)
                    width = 512 if h < 2 else 416
                    done(rows_product(name, weights(f"X{h}", KC, width), 0, width, t, uT), name)
                elif name in ("qwT0", "qwT1"):
                    t = int(name[3])
                    eng.wait_ge(roped, t + 1)
                    turn_tiles(name, px[:, t, 0:512])
                elif name == "kwT":
                    begin(name)
                    for i in range(4):
                        src = pc[:, i, 0:P] if i < 2 else px[:, i - 2, KA:KA + P]
                        ins = turn(D_(name)[:, i * P:(i + 1) * P], src)
                    done(ins, name)
                elif name[:2] in ("lq", "lk"):
                    t = int(name[2])
                    eng.wait_ge(lat_ready, t + 2)
                    begin(name)
                    base, n = (CQ, 3) if name[1] == "q" else (CKV, 2)
                    for c in range(n):
                        ins = turn(D_(name)[:, c * P:(c + 1) * P], px[:, t, base + c * P:base + (c + 1) * P])
                    done(ins, name)
                elif name[:2] == "qu":
                    t, h = int(name[2]), int(name[3])
                    if (t, h) == (0, 0):
                        loaded("QU")
                    if h == 0:
                        kept(eng, f"lq{t}")
                    begin(name)
                    width = 480 if h == 0 else 288
                    done(rows_product(name, weights("QU", 3, 768), 480 * h, width, t, lqT, 0, 3), name)
                elif name[:2] in ("qm", "kx", "kc"):
                    i = int(name[2])
                    if name == "qm0":
                        eng.wait_ge(cat_ready, 3)
                    if name == "kx0":
                        kept(eng, "xkv10")
                        kept(eng, "xkv11")
                    if name == "kc0":
                        kept(eng, "ckv10")
                        kept(eng, "ckv11")
                        eng.wait_ge(cat_ready, 1)
                    src, t0 = {"qm": (qcat, 0), "kx": (kcat, TOK), "kc": (kcat, 0)}[name[:2]]
                    begin(name)
                    for b in range(2):
                        for t in range(TOK):
                            ins = turn(D_(name)[0:QK, b * S + t * P:b * S + (t + 1) * P], src[:, t0 + t, 2 * i + b, :])
                    done(ins, name)

            def mod_slot(n):
                loaded(f"M{n}")
                if n == 0:
                    eng.wait_ge(cond_ready, 1)
                if n % 4 == 0 and n:
                    eng.wait_ge(mod_kept, n // 4)
                w = slot(f"M{n}").rearrange("p (k n) -> p k n", k=2)
                for k in range(2):
                    for j in range(4):
                        c = n % 4 * 2 + k
                        ins = pe_.matmul(MB[32 * j:32 * j + 32, :], csil[:, c, :], w[:, k, 512 * j:512 * j + 512],
                                         start=(c == 0), stop=(c == KC - 1), tile_position=(0, 32 * j))
                ins.then_inc(mod_used, 1)

            def operands(u):
                kind, j = UNITS[u]
                q = qbT if kind == MOBA else qaT
                k = {NSA: ksD, WIN: kwD, MOBA: kbD[:, j, :, :]}[kind]
                return q[:, j, :], k

            for kind, n in SCHEDULE:
                if kind == "dense":
                    dense(n)
                elif kind == "mod":
                    mod_slot(n)
                elif kind == "score":
                    q, k = operands(n)
                    if n == 0:
                        kept(eng, "kvs")
                        kept(eng, "qa0")
                        kept(eng, "qa1")
                    if n == 4:
                        kept(eng, "kvw")
                    if n == 8:
                        for x in ("qb0", "qb1", "kb0", "kb1"):
                            kept(eng, x)
                    if n:
                        eng.wait_ge(masked, n)
                    pe_.matmul(SB[0][:, :], q[:, P:S], k.rearrange("p g s -> p (g s)"), start=True, stop=True)
                    pe_.matmul(SB[1][:, 0:S].rearrange("p (g s) -> p g s", g=2), q[:, 0:P], k[:, :, 0:P],
                               start=True, stop=True).then_inc(scores, 1)
                elif kind == "turn":
                    u = n
                    eng.wait_ge(exps, u + 1)
                    if u:
                        eng.wait_ge(turned_a, u)
                        eng.wait_ge(turned_b, u)
                    for b in range(2):
                        for i in range(3):
                            ins = turn(TB[b][:, i * P:(i + 1) * P], spn[:, u % 2, b, i * P:(i + 1) * P])
                    ins.then_inc(turns, 1)
                elif kind == "pv":
                    u = n
                    typ, j = UNITS[u]
                    v = {NSA: vS, WIN: vW, MOBA: vB}[typ]
                    eng.wait_ge(turned_a, u + 1)
                    eng.wait_ge(turned_b, u + 1)
                    if u == 0:
                        kept(eng, "kvs")
                    if u == 4:
                        kept(eng, "kvw")
                    if u == 8:
                        kept(eng, "vb0")
                        kept(eng, "vb1")
                    if u:
                        eng.wait_ge(outs, u)
                    for b in range(2):
                        c = HD * b if typ != MOBA else HD * (2 * j + b)
                        o = VB[:, 128 * b:128 * b + 128]
                        pr = ptn[:, u % 2, b, :]
                        pe_.matmul(o[:, 0:64], pr[:, 0:P], v[:, 0, c:c + HD], start=True, stop=True)
                        pe_.matmul(o[:, 64:128], pr[:, P:2 * P], v[:, 0, c:c + HD], start=True, stop=False)
                        ins = pe_.matmul(o[:, 64:128], pr[:, 2 * P:3 * P], v[:, 1, c:c + HD], start=False, stop=True)
                    ins.then_inc(pvs, 1)

            def unit_scores(u):
                q = u % 2
                if u == 0:
                    for x in ("qwT0", "qwT1", "kwT"):
                        kept(eng, x)
                if u == 16:
                    for x in ("qm2", "qm3", "kx2", "kx3"):
                        kept(eng, x)
                if u == 0:
                    eng.wait_ge(masked, len(UNITS))
                if u >= 2:
                    eng.wait_ge(u_masked, min(u - 1, 16))
                    if u >= 18:
                        eng.wait_ge(u_exp, u - 1)
                o = SB[u % 2][:, :]
                if u < 16:
                    j, b = u // 4, u // 2 % 2
                    ins = pe_.matmul(o, qwT[:, j, q * P:(q + 1) * P], kP[:, b, :], start=True, stop=True)
                else:
                    h = (u - 16) // 2
                    ins = pe_.matmul(o, qmT[0:QK, h, q * P:(q + 1) * P], kmT[0:QK, h, :], start=True, stop=True)
                ins.then_inc(u_scores, 1)

            def unit_turn(u):
                eng.wait_ge(u_exp, u + 1)
                if u == 0:
                    eng.wait_ge(turned_a, len(UNITS))
                if u == 1:
                    eng.wait_ge(turned_b, len(UNITS))
                if u >= 2:
                    eng.wait_ge(u_turned_a if u % 2 == 0 else u_turned_v, u // 2)
                for i in range(4):
                    ins = turn(TB[u % 2][:, i * P:(i + 1) * P], sp3[:, u % 3, i * P:(i + 1) * P])
                ins.then_inc(u_turn, 1)

            def unit_pv(u):
                eng.wait_ge(u_turned_a if u % 2 == 0 else u_turned_v, u // 2 + 1)
                if u >= 2:
                    eng.wait_ge(u_out, u - 1)
                else:
                    eng.wait_ge(outs, len(UNITS))
                o = OB[u % 2][:, 0:HD]
                for i in range(4):
                    if u < 16:
                        b = u // 2 % 2
                        v = (pc[:, i, P + HD * b:P + HD * (b + 1)] if i < 2 else
                             xv[:, (i - 2) * P + HD * b:(i - 2) * P + HD * (b + 1)])
                    else:
                        v = vm[:, i, (u - 16) // 2, :]
                    ins = pe_.matmul(o, pt2[:, u % 2, i * P:(i + 1) * P], v, start=(i == 0), stop=(i == 3))
                ins.then_inc(u_pv, 1)

            def tail(name):
                if name[:2] == "oT":
                    t, h = int(name[2]), int(name[3])
                    eng.wait_ge(u_out, 16 * (h + 1))
                    turn_tiles(name, o2[:, t, 512 * h:512 * h + 512])
                elif name[:2] == "ou":
                    t, h = int(name[2]), int(name[3])
                    if t == 0:
                        loaded(f"OUT{h}")
                    if h == 0:
                        for i in range(2):
                            kept(eng, f"oT{t}{i}")
                    begin(name)
                    w = weights(f"OUT{h}", KC, 512)
                    done(product(D_(name)[:, :], lambda c: (oT0 if c < 4 else uT)[:, c, t * P:(t + 1) * P],
                                 lambda c: w[:, c, :], KC), name)
                elif name[:2] == "rT":
                    t, h = int(name[2]), int(name[3])
                    eng.wait_ge(normed, 7 + t)
                    turn_tiles(name, rn[:, t, 512 * h:512 * h + 512])
                elif name == "lg":
                    for x in ("rT00", "rT01", "rT10", "rT11"):
                        kept(eng, x)
                    begin(name)
                    for t in range(TOK):
                        ins = product(D_(name)[:, t * E:(t + 1) * E], lambda c: uT[:, c, t * P:(t + 1) * P],
                                      lambda c: wr[:, c, :], KC)
                    done(ins, name)
                elif name == "afT":
                    eng.wait_ge(aff_ready, 1)
                    begin(name)
                    for t in range(TOK):
                        ins = turn(D_(name)[0:E, t * P:(t + 1) * P], aff[:, t, :])
                    done(ins, name)
                elif name == "slT":
                    eng.wait_ge(slots_ready, 1)
                    begin(name)
                    for t in range(TOK):
                        ins = turn(D_(name)[:, t * E:(t + 1) * E], cum[0:E, t * P:(t + 1) * P], E)
                    done(ins, name)
                elif name[:2] == "gx":
                    c = int(name[2])
                    if c == 0:
                        eng.wait_ge(oh_ready, 1)
                    begin(name)
                    for t in range(TOK):
                        ins = pe_.matmul(D_(name)[:, :], rn[:, t, c * P:(c + 1) * P], oh[:, t, :],
                                         start=(t == 0), stop=(t == TOK - 1))
                    done(ins, name)
                elif name[:3] == "ohT":
                    i = int(name[3])
                    if i == 0:
                        eng.wait_ge(oh_ready, 2)
                    begin(name)
                    for g in range(2):
                        for t in range(TOK):
                            a = (2 * i + g) * P
                            ins = turn(D_(name)[:, g * S + t * P:g * S + (t + 1) * P], ohv[:, t, a:a + P])
                    done(ins, name)

            for r in range(34):
                if r < 32:
                    unit_scores(r)
                if 1 <= r <= 32:
                    unit_turn(r - 1)
                if r >= 2:
                    unit_pv(r - 2)
                if r in (OT_ROUND, OT_ROUND + 1):
                    tail(f"oT{r - OT_ROUND}0")

            for name in TAIL[2:]:
                tail(name)

            for c in range(KC):
                kept(eng, f"gx{c}")
            kept(eng, "ohT0")
            kept(eng, "ohT1")
            for g in range(NG):
                for m, b in (("G", 0), ("U", 1)):
                    if g:
                        eng.wait_ge(e_hT if b == 0 else e_h, g)
                    for i in range(4):
                        loaded(f"{m}{g}.{i}")
                        w = slot(f"{m}{g}.{i}").rearrange("p (e k n) -> p e k n", e=EG, k=2)
                        for k in range(2):
                            c = 2 * i + k
                            for e in range(EG):
                                a = (EG * g + e) * CAP
                                ins = pe_.matmul(bank[b][32 * e:32 * e + 32, :], xsT[:, c, a:a + CAP], w[:, e, k, :],
                                                 start=(c == 0), stop=(c == KC - 1), tile_position=(0, 32 * e))
                        ins.then_inc(e_used, 1)
                eng.wait_ge(e_h, g + 1)
                for i in range(4):
                    ins = turn(bank[0][:, i * P:(i + 1) * P], hA[:, i * P:(i + 1) * P])
                ins.then_inc(e_turn, 1)
                eng.wait_ge(e_hT, g + 1)
                if g:
                    eng.wait_ge(e_y, g)
                    eng.wait_ge(e_y2, g)
                for i in range(4):
                    loaded(f"D{g}.{i}")
                    w = slot(f"D{g}.{i}").rearrange("p (e n) -> p e n", e=EG)
                    for h in range(2):
                        for e in range(EG):
                            ins = pe_.matmul(bank[2 + h][32 * e:32 * e + 32, :], hT[:, i * P + 32 * e:i * P + 32 * e + 32],
                                             w[:, e, 512 * h:512 * h + 512], start=(i == 0), stop=(i == 3),
                                             tile_position=(0, 32 * e))
                    ins.then_inc(e_used, 1)
                eng.wait_ge(e_y, g + 1)
                eng.wait_ge(e_y2, g + 1)
                for t in range(TOK):
                    for h in range(2):
                        ins = pe_.matmul(bank[4 + 2 * t + h][:, :], ohT[:, g, t * P:(t + 1) * P],
                                         yE[:, 512 * h:512 * h + 512], start=(g == 0), stop=(g == NG - 1))
                    if t == TOK - 1 or g == NG - 1:
                        ins.then_inc(e_out, 1)

        @block.vector
        def _(eng):
            dve = nc.vector
            steps = [0]
            n_mean = [0]
            n_norm = [0]

            def own(ins):
                steps[0] += 1
                ins.then_inc(dve_step, 1)
                eng.wait_ge(dve_step, steps[0])

            def mean_root(k, w, width, n_squares):
                eng.wait_ge(squares, n_squares)
                dve.tensor_scalar(ss[:, k:k + w], ss[:, k:k + w], 1.0 / width, EPS, ALU.mult, ALU.add).then_inc(means, 1)
                n_mean[0] += 1
                eng.wait_ge(roots, n_mean[0])

            def turned_mod(name, dst, add, mult):
                filled(eng, name)
                t, h = int(name[-2]), int(name[-1])
                for c in range(4):
                    k = 4 * h + c
                    o, i = dst[:, k, t * P:(t + 1) * P], D_(name)[:, c * P:(c + 1) * P]
                    if add is None:
                        ins = dve.tensor_scalar(o, i, mult[:, k:k + 1], None, ALU.mult)
                    else:
                        ins = dve.tensor_scalar(o, i, mult[:, k:k + 1], add[:, k:k + 1], ALU.mult, ALU.add)
                leave(ins, name)

            def normalise(t, k, n_squares):
                mean_root(k + t, 1, D, n_squares)
                dve.tensor_scalar(rn[:, t, :], xn[:, t, :], rs[:, k + t:k + t + 1], None, ALU.mult).then_inc(normed, 1)

            def block1_norm(t):
                mean_root(4 + t, 1, D, 5 + 2 * t)
                eng.wait_ge(post_in, 16)
                own(dve.scalar_tensor_tensor(rn[:, t, :], rn[:, t, :], rs[:, 4 + t:5 + t], post, ALU.mult, ALU.mult))
                dve.tensor_tensor(xn[:, t, :], xn[:, t, :], rn[:, t, :], ALU.add).then_inc(x1_ready, 1)
                eng.wait_ge(x1_ready, t + 1)

            def rotate(x, t, heads, n, at):
                w = 4 * n
                cos = rope[:, at + t * w:at + (t + 1) * w]
                sin = rope[:, at + (TOK + t) * w:at + (TOK + t + 1) * w]
                a, b = (rt[:, i, 0:heads * w].rearrange("p (h d) -> p h d", h=heads) for i in range(2))
                dve.tensor_tensor(a, x, over(cos, heads), ALU.mult)
                b5 = rt[:, 1, 0:heads * w].rearrange("p (h a f n) -> p h a f n", h=heads, a=2, f=2)
                s4 = sin.rearrange("p (h a f n) -> p h a f n", h=1, a=2, f=2)
                x5 = x.rearrange("p h (a f n) -> p h a f n", a=2, f=2)
                for f in range(2):
                    ins = dve.tensor_tensor(b5[:, :, :, f, :], x5[:, :, :, 1 - f, :],
                                            s4[:, :, :, f, :].to_broadcast([P, heads, 2, n]), ALU.mult)
                own(ins)
                return dve.tensor_tensor(x, a, b, ALU.add)

            def late_x(t):
                kept(eng, f"xa{t}1")
                kept(eng, f"xa{t}2")
                rotate(px[:, t, 0:640].rearrange("p (h d) -> p h d", d=HD), t, 10, 16, 0).then_inc(roped, 1)
                eng.wait_ge(roped, t + 1)
                own(rotate(px[:, t, KR:KR + ROPE].rearrange("p (h d) -> p h d", h=1), t, 1, 8, 256))
                own(dve.tensor_copy(kcat[:, TOK + t, :, NOPE:QK], over(px[:, t, KR:KR + ROPE], HB)))
                i = 10 + 2 * t
                eng.wait_ge(squares, i)
                dve.tensor_scalar(ss[:, i:i + 1], ss[:, i:i + 1], 1.0 / QR, EPS, ALU.mult, ALU.add)
                dve.tensor_scalar(ss[:, i + 1:i + 2], ss[:, i + 1:i + 2], 1.0 / KVR, EPS, ALU.mult, ALU.add)\
                   .then_inc(means, 1)
                n_mean[0] += 1
                eng.wait_ge(roots, n_mean[0])
                dve.tensor_scalar(px[:, t, CQ:CQ + QR], px[:, t, CQ:CQ + QR], rs[:, i:i + 1], None, ALU.mult)
                dve.tensor_scalar(px[:, t, CKV:CKV + KVR], px[:, t, CKV:CKV + KVR], rs[:, i + 1:i + 2], None, ALU.mult)\
                   .then_inc(lat_ready, 1)

            def rope_q(t):
                kept(eng, f"qu{t}0")
                kept(eng, f"qu{t}1")
                rotate(qcat[:, t, :, NOPE:QK], t, HB, 8, 256).then_inc(cat_ready, 1)
                eng.wait_ge(cat_ready, t + 2)

            def spread_keys(name, src, dst):
                dve.tensor_copy(dst[0:64, 0], src[0:64])
                return dve.tensor_copy(dst[64:128, 1], src[64:128])

            for t in range(TOK):
                normalise(t, 0, t + 1)

            def unit_mask(u):
                kind, j = UNITS[u]
                eng.wait_ge(scores, u + 1)
                if u == 0:
                    eng.wait_ge(nsa_table_in, 16)
                if u == 8:
                    eng.wait_ge(moba_table_in, 16)
                if u >= 2:
                    eng.wait_ge(turns, u - 1)
                for b in range(2):
                    h = j + 4 * b if kind != MOBA else 2 * j + b
                    for q in range(TOK):
                        w = P if q == 0 else S
                        src = SB[1 - q][:, b * w:(b + 1) * w]
                        ins = dve.tensor_tensor_reduce(spn[:, u % 2, b, P * q:P * q + w], src,
                                                       table[:, h, P * q:P * q + w], 1.0, -3e38, ALU.add, ALU.max,
                                                       mx[:, u % 2, 2 * b + q:2 * b + q + 1])
                ins.then_inc(masked, 1)
                eng.wait_ge(masked, u + 1)
                dve.tensor_scalar(nm[:, u % 2, :], mx[:, u % 2, :], -1.0, None, ALU.mult).then_inc(maxed, 1)

            def unit_out(u):
                kind, j = UNITS[u]
                eng.wait_ge(pvs, u + 1)
                own(dve.reciprocal(rc[:, u, :], sums[:, u, :]))
                if kind != MOBA:
                    i = 8 * (kind + 1) + j
                    own(dve.tensor_tensor(rc[:, u, :].rearrange("p (b q) -> p b q", b=2),
                                          rc[:, u, :].rearrange("p (b q) -> p b q", b=2),
                                          gates[:, :, i:i + 5:4].rearrange("p q b -> p b q"), ALU.mult))
                for b in range(2):
                    h = j + 4 * b if kind != MOBA else 2 * j + b
                    for q in range(TOK):
                        o = VB[:, 128 * b + 64 * q:128 * b + 64 * q + 64]
                        r = rc[:, u, 2 * b + q:2 * b + q + 1]
                        dst = (ob if kind == MOBA else oa)[:, q, HD * h:HD * h + HD]
                        if kind == WIN:
                            ins = dve.scalar_tensor_tensor(dst, o, r, dst, ALU.mult, ALU.add)
                        else:
                            ins = dve.tensor_scalar(dst, o, r, None, ALU.mult)
                ins.then_inc(outs, 1)

            for kind, n in SCHEDULE:
                if kind == "score":
                    unit_mask(n)
                elif kind == "turn":
                    u = n
                    eng.wait_ge(turns, u + 1)
                    if u >= 2:
                        eng.wait_ge(pvs, u - 1)
                    dve.tensor_copy(ptn[:, u % 2, 1, :], TB[1][:, 0:CAUSAL]).then_inc(turned_b, 1)
                elif kind == "pv":
                    unit_out(n)
                elif kind == "mod":
                    if n % 4 == 3:
                        eng.wait_ge(mod_used, n + 1)
                        dve.tensor_copy(mod[:, n // 4, :], MB[:, :]).then_inc(mod_kept, 1)
                elif kind == "ya":
                    eng.wait_ge(outs, 8)
                    kept(eng, "cO1")
                    dve.tensor_tensor(mo[:, 2048:3072], mo[:, 2048:3072], zz[:, 0:1024], ALU.mult).then_inc(ya_ready, 1)
                elif kind == "yb":
                    eng.wait_ge(outs, 12)
                    dve.tensor_tensor(mo[:, 3072:4096], mo[:, 3072:4096], zz[:, 1024:2048], ALU.mult).then_inc(yb_ready, 1)
                elif kind == "context":
                    eng.wait_ge(ctx_in, 16)
                    for t in range(TOK):
                        own(dve.tensor_tensor_reduce(pt[:, 0:D], cn[:, t, :], cn[:, t, :], 1.0, 0.0, ALU.mult,
                                                     ALU.add, ss[:, 2 + t:3 + t]))
                    mean_root(2, 2, D, 2)
                    for t in range(TOK):
                        dve.tensor_scalar(cn[:, t, :], cn[:, t, :], rs[:, 2 + t:3 + t], None, ALU.mult)\
                           .then_inc(normed, 1)
                elif kind == "dense":
                    name = n
                    if name[:2] == "xT":
                        if name == "xT00":
                            eng.wait_ge(early_in, 32)
                        filled(eng, name)
                        t, h = int(name[2]), int(name[3])
                        leave(dve.tensor_tensor(uT[:, 4 * h:4 * h + 4, t * P:(t + 1) * P],
                                                D_(name)[:, :].rearrange("p (c s) -> p c s", c=4),
                                                bc(gcol[:, 4 * h:4 * h + 4], P), ALU.mult), name)
                    elif name == "kvc":
                        filled(eng, name)
                        leave(dve.tensor_copy(kvT, D_(name)[:, :].rearrange("p (i s) -> p i s", i=2)), name)
                    elif name in ("kvs", "kvw"):
                        filled(eng, name)
                        k, v = (ksD, vS) if name == "kvs" else (kwD, vW)
                        spread_keys(name, D_(name)[:, 0:S], k)
                        leave(dve.tensor_copy(v, D_(name)[:, S:2 * S].rearrange("p (t d) -> p t d", t=TOK)), name)
                    elif name == "ga":
                        kept(eng, name)
                        own(dve.tensor_scalar(gates, gates, 0.5, 0.5, ALU.mult, ALU.add))
                        eng.wait_ge(kv2_in, 16 * 4)
                        eng.wait_ge(const_in, 16 * 15)
                        for i in range(2):
                            for a in range(2):
                                src = kv2[:, i, :, :].rearrange("p g (n l r) -> p g n l r", l=8, r=2)
                                src = src[:, :, a:a + N_CMP, :, 0].rearrange("p g n l -> p l g n")
                                dst = blk[:, i, 8 * a:8 * a + 8, :].rearrange("p l (g n) -> p l g n", g=2)
                                pos = pe[:, i, 8 * a:8 * a + 8].rearrange("p (l g n) -> p l g n", g=1, n=1)
                                ins = dve.tensor_tensor(dst, src, pos.to_broadcast([P, 8, 2, N_CMP]), ALU.add)
                            ins.then_inc(blocks_ready, 1)
                        eng.wait_ge(cond_tanh, 1)
                        eng.wait_ge(zeroed, 1)
                        own(dve.scalar_tensor_tensor(ccE, ccE, 1.0, cc, ALU.add, ALU.mult))
                        dve.tensor_scalar(csil[:, :, 0:2], ccE.rearrange("p (c v) -> p c v", c=KC), 0.5, None, ALU.mult)\
                           .then_inc(cond_ready, 1)
                    elif name in ("kb0", "kb1"):
                        filled(eng, name)
                        i = int(name[2])
                        src = D_(name)[:, :].rearrange("p (j s) -> p j s", j=2)
                        dve.tensor_copy(kbD[0:64, 2 * i:2 * i + 2, 0, :], src[0:64])
                        leave(dve.tensor_copy(kbD[64:128, 2 * i:2 * i + 2, 1, :], src[64:128]), name)
                    elif name in ("za0", "za1", "zb0", "zb1"):
                        k = {"za0": 1, "za1": 2, "zb0": 3, "zb1": 4}[name]
                        eng.wait_ge(tanhs, k)
                        z = (za if name[1] == "a" else zb)[:, int(name[2]), :]
                        leave(dve.scalar_tensor_tensor(z, z, 1.0, D_(name)[:, :], ALU.add, ALU.mult), name)
                    elif name == "cH":
                        eng.wait_ge(c_act, 1)
                        leave(dve.scalar_tensor_tensor(cH[0:30, :], cE[0:30, :], 1.0, D_(name)[0:30, 0:256], ALU.add,
                                                       ALU.mult), name)
                        kept(eng, name)
                        dve.tensor_scalar(cH[0:30, :], cH[0:30, :], 0.5, None, ALU.mult).then_inc(c_vec, 1)
                    elif name == "cT":
                        filled(eng, name)
                        dve.tensor_copy(hkT, D_(name)[:, 0:30])
                        for g in range(2):
                            ins = dve.tensor_copy(hvR[:, g, :, 0:15],
                                                  D_(name)[:, 32 + 15 * g:47 + 15 * g].rearrange("p (a n) -> p a n", a=1)
                                                  .to_broadcast([P, 4, 15]))
                        leave(ins, name)
                    elif name == "cK":
                        filled(eng, name)
                        for g in range(2):
                            dve.tensor_copy(kcD[64 * g:64 * g + 64, g, 0:15], D_(name)[64 * g:64 * g + 64, 15 * g:15 * g + 15])
                        for g in range(2):
                            for h in range(4):
                                ins = dve.tensor_copy(vcD[32 * h:32 * h + 32, g, 64 * h:64 * h + 64],
                                                      D_(name)[32 * h:32 * h + 32, 64 + 64 * g:128 + 64 * g])
                        leave(ins, name)
                    elif name == "cS":
                        filled(eng, name)
                        leave(dve.tensor_tensor(cS, D_(name)[:, 0:256], cB, ALU.add), name)
                        kept(eng, name)
                        s3 = cS.rearrange("p (i n) -> p i n", n=CMPW)
                        own(dve.tensor_reduce(cst[:, 0, :], s3, AX_X, ALU.max))
                        dve.tensor_tensor(s3, s3, bc(cst[:, 0, :], CMPW), ALU.subtract).then_inc(c_vec, 1)
                        eng.wait_ge(c_act, 2)
                        own(dve.tensor_tensor(cS, cS, cM, ALU.mult))
                        own(dve.tensor_reduce(cst[:, 0, :], s3, AX_X, ALU.add))
                        own(dve.tensor_scalar(cst[:, 0, :], cst[:, 0, :], 1e-30, None, ALU.max))
                        own(dve.reciprocal(cst[:, 1, :], cst[:, 0, :]))
                        for q in range(TOK):
                            ins = dve.tensor_tensor(cst[:, 0, 8 * q:8 * q + 8].rearrange("p (j g) -> p j g", g=2),
                                                    cst[:, 1, 8 * q:8 * q + 8].rearrange("p (j g) -> p j g", g=2),
                                                    gates[:, q, 0:8].rearrange("p (g j) -> p j g", g=2), ALU.mult)
                        own(ins)
                        own(dve.tensor_tensor(s3, s3, bc(cst[:, 0, :], CMPW), ALU.mult))
                        eng.wait_ge(zeroed, 2)
                        s5 = cS.rearrange("p (q j g n) -> p q j g n", q=2, j=4, g=2)
                        for q in range(TOK):
                            for g in range(2):
                                ins = dve.tensor_copy(cP[:, 2 * q + g, :, 0:CMPW], s5[:, q, :, g, :])
                        ins.then_inc(c_vec, 1)
                    elif name in ("cO0", "cO1"):
                        q = int(name[2])
                        filled(eng, name)
                        eng.wait_ge(outs, 8)
                        leave(dve.tensor_tensor(oa[:, q, :], oa[:, q, :], D_(name)[:, :], ALU.add), name)
                    elif name[:2] == "wa":
                        t, h = int(name[2]), int(name[3])
                        filled(eng, name)
                        kept(eng, f"gA{t}{h}")
                        leave(dve.scalar_tensor_tensor(rn[:, t, 512 * h:512 * h + 512], eg[:, t, 512 * h:512 * h + 512], 1.0,
                                                       D_(name)[:, :], ALU.add, ALU.mult), name)
                    elif name[:2] == "wb":
                        t, h = int(name[2]), int(name[3])
                        filled(eng, name)
                        kept(eng, f"gB{t}{h}")
                        e = eg[:, t, 512 * h:512 * h + 512]
                        leave(dve.scalar_tensor_tensor(e, e, 1.0, D_(name)[:, :], ALU.add, ALU.mult), name)
                        kept(eng, name)
                        m = rn[:, t, 512 * h:512 * h + 512]
                        dve.tensor_tensor(m, m, e, ALU.add).then_inc(m_ready, 1)
                    elif name[:4] == "modT":
                        r = int(name[4])
                        filled(eng, name)
                        src = D_(name)[:, :].rearrange("p (b j v) -> p v j b", b=4, j=4)
                        for v in range(2):
                            ins = dve.tensor_copy(mc[:, v, 16 * r:16 * r + 16].rearrange("p (j b) -> p j b", j=4), src[:, v, :, :])
                        leave(ins, name)
                        kept(eng, name)
                        for v in range(2):
                            m = mc[:, v, 16 * r:16 * r + 16]
                            ins = dve.tensor_tensor(m, m, bmod[:, 16 * r:16 * r + 16], ALU.add)
                        own(ins)
                        if r == 0:
                            for v in range(2):
                                ins = dve.scalar_tensor_tensor(scl[:, v, :], mc[:, v, 8:16], 1.0, nat, ALU.add, ALU.mult)
                            own(ins)
                        if r == 2:
                            own(dve.scalar_tensor_tensor(scl[:, 2, :], mc[:, 0, 32:40], 1.0, nff, ALU.add, ALU.mult))
                    elif name in ("cxT00", "cxT10"):
                        turned_mod(name, hcT, mc[:, 1, 0:8], scl[:, 1, :])
                    elif name == "cc1":
                        mean_root(6, 2, KVR, 4)
                        for t in range(TOK):
                            ins = dve.tensor_scalar(pc[:, t, 256:512], pc[:, t, 256:512], rs[:, 6 + t:7 + t], None, ALU.mult)
                        ins.then_inc(lat_ready, 1)
                    elif name == "clT":
                        filled(eng, name)
                        for c in range(2):
                            ins = dve.tensor_scalar(lcT[:, c, :], D_(name)[:, c * S:(c + 1) * S], kvn[:, c:c + 1], None, ALU.mult)
                        leave(ins, name)
                        for t in range(TOK):
                            ins = dve.tensor_copy(kcat[:, t, :, NOPE:QK], over(pc[:, t, 512:544], HB))
                        ins.then_inc(cat_ready, 1)
                    elif name[:2] == "wo" and name[3] == "1":
                        t = int(name[2])
                        block1_norm(t)
                        normalise(t, 8, 6 + 2 * t)
                    elif name[:2] in ("bG", "bF"):
                        h = int(name[2])
                        filled(eng, name)
                        dst = (gG if name[1] == "G" else gF)[:, 512 * h:512 * h + 512]
                        eng.wait_ge(bg_in if name[1] == "G" else bf_in, 16)
                        leave(dve.tensor_tensor(dst, D_(name)[:, :], dst, ALU.add), name)
                    elif name in ("hT00", "hT10"):
                        turned_mod(name, uT, mc[:, 0, 0:8], scl[:, 0, :])
                    elif name in ("xa02", "xa12"):
                        late_x(int(name[2]))
                    elif name == "kwT":
                        filled(eng, name)
                        eng.wait_ge(kp_zeroed, 1)
                        leave(spread_keys(name, D_(name)[:, :], kP), name)
                        dve.tensor_copy(xv.rearrange("p (t d) -> p t d", t=TOK), px[:, :, VA:VA + P])
                    elif name[:2] in ("lq", "lk"):
                        filled(eng, name)
                        t = int(name[2])
                        dst, w, n_ = (lqT, qn, 3) if name[1] == "q" else (lkT, kvn, 2)
                        leave(dve.tensor_tensor(dst[:, :, t * P:(t + 1) * P],
                                                D_(name)[:, 0:n_ * P].rearrange("p (c s) -> p c s", c=n_), bc(w, P),
                                                ALU.mult), name)
                    elif name in ("qu01", "qu11"):
                        rope_q(int(name[2]))
                    elif name[:2] in ("qm", "kx", "kc") and int(name[2]) % 2 == 1:
                        filled(eng, name)
                        leave(dve.tensor_copy(mla_turned(name), D_(name)[0:QK, :].rearrange("p (h s) -> p h s", h=2)),
                              name)

            def unit_mask2(u):
                q = u % 2
                eng.wait_ge(u_scores, u + 1)
                if u == 0:
                    eng.wait_ge(wmask_in, 16)
                if u < 16:
                    if u >= 3:
                        eng.wait_ge(u_turn, u - 2)
                    h = u // 2 % 2 * 4 + u // 4
                    dve.tensor_tensor_reduce(sp3[:, u % 3, :], SB[u % 2][:, :], wB[:, q, :], 1.0, -3e38, ALU.add, ALU.max,
                                             mx2[:, u:u + 1]).then_inc(u_masked, 1)
                    eng.wait_ge(u_masked, u + 1)
                    dve.tensor_scalar(nm2[:, u:u + 1], mx2[:, u:u + 1], sink[:, h:h + 1], -1.0, ALU.max, ALU.mult)\
                       .then_inc(u_neg, 1)
                else:
                    own(dve.tensor_reduce(mx2[:, u:u + 1], SB[u % 2][:, :], AX_X, ALU.max))
                    dve.tensor_scalar(nm2[:, u:u + 1], mx2[:, u:u + 1], -MLA_SCALE, None, ALU.mult).then_inc(u_neg, 1)

            def unit_out2(u):
                q = u % 2
                eng.wait_ge(u_pv, u + 1)
                if u < 16:
                    eng.wait_ge(u_sink, u + 1)
                    own(dve.tensor_tensor(sm2[:, u:u + 1], sm2[:, u:u + 1], sk2[:, u:u + 1], ALU.add))
                    col = HD * (u // 2 % 2 * 4 + u // 4)
                else:
                    col = 512 + HD * ((u - 16) // 2)
                own(dve.reciprocal(rc2[:, u:u + 1], sm2[:, u:u + 1]))
                dve.tensor_scalar(o2[:, q, col:col + HD], OB[u % 2][:, 0:HD], rc2[:, u:u + 1], None, ALU.mult)\
                   .then_inc(u_out, 1)

            for r in range(34):
                if r < 32:
                    unit_mask2(r)
                if 1 <= r <= 32 and (r - 1) % 2 == 1:
                    u = r - 1
                    eng.wait_ge(u_turn, u + 1)
                    if u >= 2:
                        eng.wait_ge(u_pv, u - 1)
                    dve.tensor_copy(pt2[:, 1, :], TB[1][:, :]).then_inc(u_turned_v, 1)
                if r >= 2:
                    unit_out2(r - 2)

            for name in TAIL:
                if name[:2] == "ou":
                    t, h = int(name[2]), int(name[3])
                    filled(eng, name)
                    r = rn[:, t, 512 * h:512 * h + 512]
                    x = xn[:, t, 512 * h:512 * h + 512]
                    leave(dve.tensor_tensor(r, D_(name)[:, :], gG[:, 512 * h:512 * h + 512], ALU.mult), name)
                    kept(eng, name)
                    ins = dve.tensor_tensor(x, x, r, ALU.add)
                    if h == 1:
                        ins.then_inc(x2_ready, 1)
                        normalise(t, 14, 13 + t)
                elif name in ("rT00", "rT10"):
                    turned_mod(name, uT, mc[:, 0, 24:32], scl[:, 2, :])
                elif name == "lg":
                    filled(eng, name)
                    lg = D_(name)[:, 0:2 * E].rearrange("p (t e) -> p t e", t=TOK)
                    own(dve.tensor_reduce(rst[:, 0:2], lg, AX_X, ALU.max))
                    leave(dve.tensor_tensor(aff, lg, bc(rst[:, 0:2], E), ALU.subtract), name)
                    kept(eng, name)
                    dve.tensor_scalar(rst[:, 6:7], rst[:, 0:1], 1.0, None, ALU.mult).then_inc(logit_max, 1)
                    eng.wait_ge(logit_exp, 1)
                    own(dve.tensor_reduce(rst[:, 2:4], aff, AX_X, ALU.add))
                    own(dve.reciprocal(rst[:, 4:6], rst[:, 2:4]))
                    dve.tensor_tensor(aff, aff, bc(rst[:, 4:6], E), ALU.mult).then_inc(aff_ready, 1)
                elif name == "afT":
                    filled(eng, name)
                    leave(dve.tensor_copy(affT[0:E], D_(name)[0:E, 0:S]), name)
                    own(dve.memset(zer[0:E], 0.0))
                    kept(eng, name)
                    cur = affT
                    for i in range(CAP // 8):
                        own(dve.max(top8[0:E], cur[0:E]))
                        nxt = work if cur is affT else affT
                        own(dve.match_replace(nxt[0:E], top8[0:E], cur[0:E], -1.0))
                        cur = nxt
                    own(dve.tensor_scalar(msk[0:E], cur[0:E], 0.0, None, ALU.is_lt))
                    own(dve.tensor_tensor_scan(cum[0:E], msk[0:E], zer[0:E], 0.0, ALU.add, ALU.add))
                    dve.tensor_tensor(cum[0:E], cum[0:E], msk[0:E], ALU.mult).then_inc(slots_ready, 1)
                elif name == "slT":
                    filled(eng, name)
                    leave(dve.tensor_copy(slt, D_(name)[:, 0:2 * E].rearrange("p (t e) -> p t e", t=TOK)), name)
                    kept(eng, name)
                    for t in range(TOK):
                        ins = dve.tensor_tensor(oh[:, t, :].rearrange("p (e s) -> p e s", e=E), bc(slt[:, t, :], CAP),
                                                over(iota, E), ALU.is_equal)
                    ins.then_inc(oh_ready, 1)
                    eng.wait_ge(oh_ready, 1)
                    for t in range(TOK):
                        ins = dve.tensor_tensor(ohv[:, t, :].rearrange("p (e s) -> p e s", e=E),
                                                oh[:, t, :].rearrange("p (e s) -> p e s", e=E), bc(aff[:, t, :], CAP), ALU.mult)
                    ins.then_inc(oh_ready, 1)
                elif name[:2] == "gx" and int(name[2]) % 2 == 1:
                    c = int(name[2])
                    filled(eng, name)
                    leave(dve.tensor_scalar(xsT[:, c, :], D_(name)[:, :], scl[:, 2, c:c + 1], mc[:, 0, 24 + c:25 + c],
                                            ALU.mult, ALU.add), name)

            for g in range(NG):
                eng.wait_ge(e_tanh, g + 1)
                own(dve.scalar_tensor_tensor(hA, hE, 1.0, bank[0][:, :], ALU.add, ALU.mult))
                experts_done(eng, "U", g)
                dve.tensor_tensor(hA, hA, bank[1][:, :], ALU.mult).then_inc(e_h, 1)
                experts_done(eng, "D", g)
                if g:
                    eng.wait_ge(e_out, g)
                dve.tensor_copy(yE[:, 512:1024], bank[3][:, :]).then_inc(e_y2, 1)

            for t in range(TOK):
                eng.wait_ge(e_out, NG + t)
                for h in range(2):
                    r = rn[:, t, 512 * h:512 * h + 512]
                    own(dve.tensor_tensor(r, bank[4 + 2 * t + h][:, :], gF[:, 512 * h:512 * h + 512], ALU.mult))
                dve.tensor_tensor(xn[:, t, :], xn[:, t, :], rn[:, t, :], ALU.add).then_inc(f_in, 1)
            eng.wait_ge(fin_in, 16)
            for t in range(TOK):
                mean_root(t, 1, D, 15 + t)
                dve.scalar_tensor_tensor(xn[:, t, :], xn[:, t, :], rs[:, t:t + 1], nfin, ALU.mult, ALU.mult)\
                   .then_inc(y_ready, 1)


def shape_tables():
    q = np.arange(S)
    dist = (q[:, None] - q[None, :]).astype(np.float32)
    slopes = alibi(16)
    far = np.where(dist < 0, np.float32(FAR), dist)

    def table(sl):
        out = np.zeros((P, 8, CAUSAL), np.float32)
        for h in range(8):
            b = -np.float32(sl[h]) * far
            out[:, h, 0:P] = b[0:P, 0:P]
            out[:, h, P:CAUSAL] = b[P:S, :]
        return out.reshape(P, -1)

    end = np.arange(N_CMP) * 16 + 31
    cd = (q[:, None] - end[None, :]).astype(np.float32)
    bias = np.full((P, 2, 4, 2, CMPW), -FAR, np.float32)
    mask = np.zeros((P, 2, 4, 2, CMPW), np.float32)
    for t in range(2):
        for j in range(4):
            for g in range(2):
                d = cd[t * P:(t + 1) * P]
                bias[:, t, j, g, :N_CMP] = np.where(d >= 0, -np.float32(slopes[0::2][4 * g + j]) * d, -FAR)
                mask[:, t, j, g, :N_CMP] = d >= 0
    win = np.zeros((P, 2, 512), np.float32)
    for t in range(2):
        win[:, t, S:] = np.where(np.abs(dist[t * P:(t + 1) * P]) <= 128, 0.0, -FAR)

    def rotary(n):
        inv = 10000.0 ** (-np.arange(n, dtype=np.float32) / n)
        pos = np.stack([q // 64, q % 64], 1).astype(np.float32)
        ang = (pos[:, :, None] * inv[None, None, :]).astype(np.float32)
        c, s = np.cos(ang), np.sin(ang)
        cos = np.concatenate([c, c], 2).reshape(S, 4 * n)
        sin = np.concatenate([-s, s], 2).reshape(S, 4 * n)
        return [np.concatenate([m[0:P], m[P:S]], 1) for m in (cos, sin)]

    rope = np.concatenate(rotary(16) + rotary(8), 1).astype(np.float32)
    return {
        "ident": np.eye(P, dtype=np.float32), "nsa_table": table(slopes[0::2]), "moba_table": table(slopes[1::2]),
        "cmp_bias": bias.reshape(P, -1), "cmp_mask": mask.reshape(P, -1), "window_mask": win.reshape(P, -1),
        "rope": rope, "iota": np.tile(np.arange(1, CAP + 1, dtype=np.float32), (P, 1)),
    }


def chunks(w):
    return w.reshape(-1, P, w.shape[1]).transpose(1, 0, 2)


def stream_of(a):
    w = a["w_in"][0]
    pair = np.concatenate([np.arange(64) + 64 * h for j in range(4) for h in (j, 4 + j)])
    kv = lambda i: w[:, 512 + 128 * i:640 + 128 * i]
    parts = {"W0": w[:, pair], "W1": np.concatenate([kv(0), kv(1), kv(2), kv(3)], 1),
             "W2": np.concatenate([kv(4), kv(5), w[:, 1280:1304]], 1),
             "W6": w[:, 1304:1816], "W3": w[:, 1816:2328], "W4": w[:, 2328:2840], "W5": w[:, 2840:3352],
             "W7": w[:, 3352:3864]}
    for i in range(4):
        parts[f"W{8 + i}"] = w[:, 3864 + 512 * i:4376 + 512 * i]
    w2 = a["w_in_2"][0]
    ckv, kr = w2[:, 1152:1408], w2[:, 1408:1440]
    parts |= {"C0": w2[:, 512:768], "C1": np.concatenate([ckv, kr], 1), "X0": w2[:, pair],
              "X1": np.concatenate([w2[:, 512:768], ckv], 1), "X2": np.concatenate([w2[:, 768:1152], kr], 1),
              "WA": a["w_branch_a"][0], "WB": a["w_branch_b"][0], "QU": a["w_q_up_2"][0],
              "KU0": a["w_kv_up_2"][0], "KU1": a["w_kv_up_2"][0]}
    for i in range(2):
        parts[f"WO{i}"] = a["w_o"][0][:, 512 * i:512 * i + 512]
        parts[f"OUT{i}"] = a["w_out_2"][0][:, 512 * i:512 * i + 512]
    flat = {n: chunks(p).reshape(P, -1) for n, p in parts.items()}
    flat["WC"] = np.concatenate([chunks(a[f"cmp_w1_{k}"][0].reshape(-1, P)).reshape(P, -1) for k in "kv"], 1)
    wm = chunks(a["w_mod_2"][0])
    for n in range(12):
        flat[f"M{n}"] = wm[:, 2 * (n % 4):2 * (n % 4) + 2, 2048 * (n // 4):2048 * (n // 4) + 2048].reshape(P, -1)
    out = np.zeros((len(STREAM), P, SLOT), np.float32)
    for g in range(NG):
        for m, src in (("G", "w_gate_2"), ("U", "w_up_2"), ("D", "w_down_2")):
            e = a[src][0][EG * g:EG * g + EG]
            e = e.reshape(EG, -1, P, e.shape[2]).transpose(2, 0, 1, 3)
            for i in range(4):
                flat[f"{m}{g}.{i}"] = (e[:, :, 2 * i:2 * i + 2] if m != "D" else e[:, :, i]).reshape(P, -1)
    for n, name in enumerate(STREAM):
        out[n, :, :flat[name].shape[1]] = flat[name]
    return out


def host_arrays(a):
    col = lambda v: np.ascontiguousarray(v.reshape(-1, P).T)
    pe = np.concatenate([a[f"cmp_pe_{k}_"].reshape(LP, P).T for k in "kv"], 1)
    cond = np.stack([col(a["c_2"]), col(a["c_ctx_2"])], 2).reshape(P, -1)
    return {
        "stream": stream_of(a), "x": a["x"][0], "ctx": a["ctx_2"][0],
        "norm_pre": col(a["norm_pre"][0]), "norm_post": a["norm_post"], "norm_attn": col(a["norm_attn_2"][0]),
        "norm_ffn": col(a["norm_ffn_2"][0]), "norm_final": a["norm_final_2"].reshape(1, D),
        "b_mod": a["b_mod_2"], "b_mod_cols": col(a["b_mod_2"][0]), "q_norm": col(a["q_norm_2"][0]),
        "kv_norm": col(a["kv_norm_2"][0]), "sink": a["sink_2"], "cond": cond, "pe": pe,
        "w2k": np.concatenate([a["cmp_w2_k"][0]] * 2, 1), "w2v": a["cmp_w2_v"][0],
        "w_router": chunks(a["w_router_2"][0]).reshape(P, -1), **shape_tables(),
    }


def kernel(**inputs):
    import concourse.bacc as bacc
    from concourse.bass_utils import run_bass_kernel_spmd

    a = {k: np.asarray(v) for k, v in inputs.items()}
    a |= {f"cmp_pe_{k}_": a[f"cmp_pe_{k}"][0] for k in "kv"}
    nc = bacc.Bacc("TRN2", target_bir_lowering=False, num_devices=1)
    arrays, args = {}, {}
    for name, v in host_arrays(a).items():
        v = np.ascontiguousarray(v)
        arrays[f"in_{name}"] = v
        args[name] = nc.dram_tensor(f"in_{name}", v.shape, mybir.dt.from_np(v.dtype), kind="ExternalInput").ap()
    y = nc.dram_tensor("out_y", (S, D), F32, kind="ExternalOutput").ap()
    build(nc, args, y)
    got = run_bass_kernel_spmd(nc, [arrays], core_ids=[0])
    return got.results[0]["out_y"].reshape(1, S, D)
```

```python
from contextlib import ExitStack

import numpy as np

import concourse.bass as bass
from concourse import mybir

F32 = mybir.dt.float32
F32R = mybir.dt.float32r
ALU = mybir.AluOpType
ACT = mybir.ActivationFunctionType
AX_X = mybir.AxisListType.X

P = 128
S = 256
TOK = S // P
D = 1024
KC = D // P
HD = 64
EPS = 1e-6
FAR = 1e30
SLOT = 4096
SBUF_START = 16512
SBUF_END = 229344

N_CMP = 15
CMPW = 16
LP = 16
CAUSAL = P + S

XP = 1440
KA, VA, CKV, CQ, KR = 512, 640, 768, 1024, 1408
CP = 544
QR, KVR = 384, 256
HB, NOPE, ROPE, QK = 8, 64, 32, 96
MLA_SCALE = float(QK) ** -0.5
E = 16
CAP = 32
FF = 512
EG = 4
NG = E // EG

STREAM = (["W0", "W1", "W2", "W3", "W4", "M0", "WC", "W5", "M1", "W6", "M2", "W7", "M3", "W8", "M4", "W9", "M5",
           "WA", "M6", "W10", "M7", "W11", "M8", "WB", "M9", "C0", "M10", "WO0", "M11", "WO1", "C1", "KU0",
           "X0", "X1", "X2", "QU", "KU1", "OUT0", "OUT1"]
          + [f"{m}{g}.{i}" for g in range(NG) for m in ("G", "U", "D") for i in range(4)])
N_DENSE = STREAM.index("G0.0")
BUFFERS = 8
SECOND = STREAM.index("WA")
LATE = {"KU0": 0, "X0": 1, "X1": 2, "X2": 3, "QU": 0, "KU1": 1, "OUT0": 2, "OUT1": 3}
EXPERT_CYCLE = [0, 1, 4, 5, 6, 7, 2, 3]


def buffer_of(n):
    if n >= N_DENSE:
        return EXPERT_CYCLE[(n - N_DENSE) % len(EXPERT_CYCLE)]
    return n % 2 if n < SECOND else LATE.get(STREAM[n], (1, 4, 0)[(n - SECOND) % 3])


BUFFER = [buffer_of(n) for n in range(len(STREAM))]
TURN = [BUFFER[:n + 1].count(BUFFER[n]) for n in range(len(STREAM))]

SPLIT = [n for n in STREAM if n in ("WA", "WB", "WO0", "WO1") or n[0] == "W" and n[1:].isdigit()]
WIDTH = {"W2": 280}

DENSE = ["xT00", "xT01", "xT10", "xT11", "qa0", "qa1", "kvc", "kvs", "va0", "va1",
         "qb0", "qb1", "kb0", "cH", "kb1", "cT", "vb0", "cK", "vb1", "cS", "za0", "za1", "cP", "zb0", "zb1",
         "cO0", "cO1", "gA00", "gA10", "yaT0", "gA01", "yaT1", "gA11", "modT0", "wa00", "ybT0", "wa10", "ybT1",
         "wa01", "wa11", "gB00", "gB10", "cxT00", "cxT01", "cxT10", "cxT11", "gB01", "gB11",
         "wb00", "wb10", "ck0", "ck1", "wb01", "wb11", "mT00", "mT10", "mT01", "mT11", "modT1",
         "wo00", "wo10", "cc0", "cc1", "wo01", "clT", "wo11", "ckv00", "ckv01", "ckv10", "ckv11", "hT00", "hT01",
         "bG0", "bG1", "modT2", "bF0", "bF1", "kc0", "kc1", "kc2", "kc3", "hT10", "hT11",
         "xa00", "xa01", "xa02", "xa10", "qwT0", "xa11", "lq0", "lk0", "xa12",
         "qu00", "qu01", "xkv00", "xkv01",
         "qwT1", "kwT", "lq1", "lk1", "qu10", "qu11", "xkv10", "xkv11",
         "qm0", "qm1", "qm2", "qm3", "kx0", "kx1", "kx2", "kx3"]
TAIL = (["oT00", "oT10", "oT01", "oT11", "ou00", "ou01", "ou10", "rT00", "rT01", "ou11", "lg0",
          "rT10", "rT11", "lg1", "afT", "slT", "gx0", "gx1"])
OT_ROUND = 20
GROUPS = DENSE + TAIL
BANK_OF = {name: n % 2 for n, name in enumerate(GROUPS)}
USE_OF = {name: n // 2 + 1 for n, name in enumerate(GROUPS)}

MOD_AFTER = {"qb1": 0, "kb1": 1, "vb1": 2, "za1": 3, "zb1": 4, "gA10": 5, "gA11": 6, "wa11": 7,
             "gB10": 8, "gB11": 9, "ck1": 10, "modT1": 11}

LAST_USE = {"W0": "qa1", "W1": "kvs", "W2": "va1", "W3": "qb1", "W4": "kb1", "W5": "vb1", "W6": "za1", "W7": "zb1",
            "W8": "gA10", "W9": "gA11", "W10": "gB10", "W11": "gB11", "WA": "wa11", "WB": "wb11", "WC": "cH",
            "C0": "ck1", "C1": "cc1", "KU0": "ckv11", "WO0": "wo10", "WO1": "wo11", "X0": "xa10", "X1": "xa11",
            "X2": "xa12", "QU": "qu11", "KU1": "xkv11", "OUT0": "ou10", "OUT1": "ou11"}

NSA, WIN, MOBA = range(3)
UNITS = [(NSA, j) for j in range(4)] + [(WIN, j) for j in range(4)] + [(MOBA, j) for j in range(4)]
ROUND_AFTER = {name: r for r, name in enumerate(
    ["qb0", "qb1", "kb0", "kb1", "vb0", "vb1", "za0", "za1", "zb0", "zb1", "gA00", "gA10", "gA01", "gA11"])}


def schedule():
    out = []
    for name in DENSE:
        for k in range(1, len(SPLIT)):
            if LAST_USE[SPLIT[k - 1]] == name:
                out.append(("split", k))
        out.append(("dense", name))
        if name == "xT11":
            out.append(("split", 0))
        if name in MOD_AFTER:
            out.append(("mod", MOD_AFTER[name]))
        if name in ROUND_AFTER:
            r = ROUND_AFTER[name]
            if r < len(UNITS):
                out.append(("score", r))
            if 0 <= r - 1 < len(UNITS):
                out.append(("turn", r - 1))
            if 0 <= r - 2:
                out.append(("pv", r - 2))
        if name == "cO1":
            out.append(("ya", 0))
        if name == "gA11":
            out.append(("yb", 0))
        if name == "wa11":
            out.append(("context", 0))
    return out


SCHEDULE = schedule()


def alibi(n):
    return [float(np.float32(2.0 ** (-8.0 * k / n))) for k in range(1, n + 1)]


def build(nc, A, out):
    ctx = ExitStack()
    with ctx:
        def sem(name):
            return ctx.enter_context(nc.semaphore(name))

        placed = {}

        def sb(name, cols):
            start = max((a + 4 * n for a, n in placed.values()), default=SBUF_START)
            assert start + 4 * cols <= SBUF_END
            placed[name] = (start, cols)
            return nc.alloc_sbuf_tensor_at(name, [P, cols], F32, offset=start)

        def parts_at(name, where, start, cols):
            return nc.alloc_sbuf_tensor_at(name, [P, cols], F32R, offset=placed[where][0] + 4 * start)

        ring = sb("ring", 2 * SLOT)
        parts = sb("parts", 2 * SLOT)
        x_sb = sb("x_sb", TOK * D)
        tz = sb("tz", 4096)
        turned = tz[:, 0:2048]
        zz = tz[:, 2048:4096]
        rows = sb("rows", TOK * D)
        tabs = sb("tabs", 4096)
        mo = sb("mo", 4096)
        qk = sb("qk", 5120)
        vvc = sb("vvc", 6656)
        vv = vvc[:, 0:1536]
        vc = vvc[:, 1536:6656]
        sp = sb("sp", 1536)
        pt = sb("pt", 1536)
        lat = sb("lat", 1792)
        ident = sb("ident", P)
        modr = sb("modr", 1536)
        rope = sb("rope", 384)
        small = sb("small", 1400)

        used = {}

        def view(tensor, start, cols, pattern=None, **sizes):
            v = tensor[:, start:start + cols]
            return v.rearrange(pattern, **sizes) if pattern else v

        def tiny(cols):
            a = used.get("small", 0)
            used["small"] = a + cols
            assert a + cols <= 1400
            return small[:, a:a + cols]

        def slot(name):
            b = BUFFER[STREAM.index(name)]
            if b < 2:
                return ring[:, b * SLOT:(b + 1) * SLOT]
            if b < 4:
                return parts[:, (b - 2) * SLOT:(b - 1) * SLOT]
            return {4: qk, 5: tabs, 6: mo, 7: vvc}[b][:, 0:SLOT]

        weight_parts = parts_at("weight_parts", "parts", 0, 2 * SLOT)
        u_parts = parts_at("u_parts", "tz", 0, 2048)
        x_parts = parts_at("x_parts", "rows", 0, 2048)
        ml_parts = parts_at("ml_parts", "tabs", 2048, 2048)
        ya_parts = parts_at("ya_parts", "lat", 0, 1024)
        yb_parts = parts_at("yb_parts", "tabs", 3072, 1024)
        yal_parts = parts_at("yal_parts", "tabs", 2048, 1024)
        ybl_parts = parts_at("ybl_parts", "qk", 4096, 1024)

        xn = x_sb[:, :].rearrange("p (t d) -> p t d", t=TOK)
        rn = rows[:, :].rearrange("p (t d) -> p t d", t=TOK)
        uT = turned[:, :].rearrange("p (c s) -> p c s", c=KC)
        uhigh, xlow, mlow = (t_[:, :].rearrange("p (c s) -> p c s", c=KC) for t_ in (u_parts, x_parts, ml_parts))
        yaT, ybT, yalow, yblow = (t_[:, :].rearrange("p (c s) -> p c s", c=4)
                                  for t_ in (ya_parts, yb_parts, yal_parts, ybl_parts))
        xrow = view(mo, 0, 2048, "p (t d) -> p t d", t=TOK)
        mrow = view(tabs, 0, 2048, "p (t d) -> p t d", t=TOK)
        table = view(tabs, 0, 8 * CAUSAL, "p (h k) -> p h k", h=8)
        eg = view(mo, 0, 2048, "p (t d) -> p t d", t=TOK)
        oa = view(mo, 2048, 1024, "p (t d) -> p t d", t=TOK)
        ob = view(mo, 3072, 1024, "p (t d) -> p t d", t=TOK)
        qaT = view(qk, 0, 1024, "p (j s) -> p j s", j=4)
        ksD = view(qk, 1024, 512, "p (g s) -> p g s", g=2)
        kwD = view(qk, 1536, 512, "p (g s) -> p g s", g=2)
        qbT = view(qk, 2048, 1024, "p (j s) -> p j s", j=4)
        kbD = view(qk, 3072, 2048, "p (j g s) -> p j g s", j=4, g=2)
        za = view(zz, 0, 1024, "p (t d) -> p t d", t=TOK)
        zb = view(zz, 1024, 1024, "p (t d) -> p t d", t=TOK)
        vSW = view(vv, 0, 512, "p (t i d) -> p t i d", t=TOK, i=2)
        vS, vW = vSW[:, :, 0, :], vSW[:, :, 1, :]
        vB = view(vv, 512, 1024, "p (t d) -> p t d", t=TOK)
        kvT = view(vc, 0, 512, "p (i s) -> p i s", i=2)
        kv2 = view(vc, 512, 1024, "p (i g s) -> p i g s", i=2, g=2)
        blk = view(vc, 1536, 960, "p (i l n) -> p i l n", i=2, l=LP)
        cE = view(vc, 2496, 256)
        cH = view(vc, 2752, 256)
        hkT = view(vc, 3008, 30)
        hvR = view(vc, 3072, 256, "p (g h n) -> p g h n", g=2, h=4)
        w2k = view(vc, 3328, 128)
        w2v = view(vc, 3456, 64)
        kcD = view(vc, 3520, 32, "p (g n) -> p g n", g=2)
        vcD = view(vc, 3552, 512, "p (g d) -> p g d", g=2)
        cB = view(vc, 4064, 256)
        cM = view(vc, 4320, 256)
        cS = view(vc, 4576, 256)
        cP = view(vc, 512, 512, "p (i h n) -> p i h n", i=4, h=4)
        cPT = view(vc, 1024, 512, "p (i q) -> p i q", i=4)
        pe = view(vc, 4832, 32, "p (i l) -> p i l", i=2)
        spn = sp[:, :].rearrange("p (u b k) -> p u b k", u=2, b=2)
        ptn = pt[:, :].rearrange("p (u b k) -> p u b k", u=2, b=2)
        post = view(vc, 2048, 1024)

        hcT = zz[:, :].rearrange("p (c s) -> p c s", c=KC)
        cn = view(vc, 0, 2048, "p (t d) -> p t d", t=TOK)
        px = view(mo, 0, TOK * XP, "p (t d) -> p t d", t=TOK)
        pc = view(mo, TOK * XP, TOK * CP, "p (t d) -> p t d", t=TOK)
        kcat = view(qk, 0, 3072, "p (t h d) -> p t h d", t=2 * TOK, h=HB)
        qcat = view(qk, 3072, 1536, "p (t h d) -> p t h d", t=TOK, h=HB)
        kP = view(vv, 0, 1024, "p (g s) -> p g s", g=2)
        rt = view(sp, 0, 1280, "p (i d) -> p i d", i=2)
        gG = view(vc, 3072, 1024)
        gF = view(vc, 4096, 1024)
        vm = view(vc, 0, 2048, "p (t h d) -> p t h d", t=2 * TOK, h=HB)
        qwT = view(pt, 0, 1024, "p (j s) -> p j s", j=4)
        xv = view(vv, 1024, 256)
        lqT = view(lat, 0, 768, "p (c s) -> p c s", c=3)
        lkT = view(lat, 768, 512, "p (c s) -> p c s", c=2)
        lcT = view(lat, 1280, 512, "p (c s) -> p c s", c=2)
        qmT = turned[:, :].rearrange("p (h s) -> p h s", h=HB)
        kmT = tabs[:, :].rearrange("p (h s) -> p h s", h=HB)
        wB = view(modr, 0, 1024, "p (t k) -> p t k", t=TOK)
        oT0 = view(pt, 0, 1024, "p (c s) -> p c s", c=4)
        o2 = zz[:, :].rearrange("p (t d) -> p t d", t=TOK)
        sp3 = sp[:, :].rearrange("p (u k) -> p u k", u=3)
        pt2 = view(mo, 0, 1024, "p (u k) -> p u k", u=2)
        mod = modr[:, :].rearrange("p (r n) -> p r n", r=3)
        pick = view(lat, 0, 512, "p (j q) -> p j q", j=4)

        nfin = gG
        xsT = tz[:, :].rearrange("p (c s) -> p c s", c=KC)
        oh = view(modr, 0, 1024, "p (t s) -> p t s", t=TOK)
        ohv = view(lat, 768, 1024, "p (t s) -> p t s", t=TOK)
        ohT = view(qk, 4096, 1024, "p (g s) -> p g s", g=NG)
        hE = view(sp, 0, 512)
        hA = view(sp, 512, 512)
        hT = view(sp, 1024, 512)
        yE = view(pt, 0, 1024)

        gcol = tiny(KC)
        nat = tiny(KC)
        nff = tiny(KC)
        bmod = tiny(48)
        modc = tiny(96)
        mc = modc.rearrange("p (v q) -> p v q", v=2)
        qn = tiny(3)
        kvn = tiny(2)
        sink = tiny(8)
        iota = tiny(CAP)
        wr = tiny(KC * E).rearrange("p (c e) -> p c e", c=KC)
        cc = tiny(2 * KC)
        ccE = tiny(2 * KC)
        csil = tiny(KC * 32).rearrange("p (c v) -> p c v", c=KC)
        gates = tiny(48).rearrange("p (t i) -> p t i", t=TOK)
        ss = tiny(16)
        rs = tiny(16)
        half = tiny(4)
        mx = tiny(8).rearrange("p (u i) -> p u i", u=2)
        nm = tiny(8).rearrange("p (u i) -> p u i", u=2)
        sums = tiny(48).rearrange("p (u i) -> p u i", u=12)
        rc = tiny(48).rearrange("p (u i) -> p u i", u=12)
        cst = tiny(48).rearrange("p (i n) -> p i n", i=3)
        mx2 = tiny(32)
        nm2 = tiny(32)
        sm2 = tiny(32)
        sk2 = tiny(32)
        rc2 = tiny(32)
        scl = tiny(4 * KC).rearrange("p (i c) -> p i c", i=4)
        aff = tiny(32).rearrange("p (t e) -> p t e", t=TOK)
        slt = tiny(32).rearrange("p (t e) -> p t e", t=TOK)
        rst = tiny(8)
        affT = view(pt, 1024, 256)
        work = view(pt, 1280, 256)
        top8 = tiny(8)
        msk = view(lat, 0, 256)
        cum = view(lat, 256, 256)
        zer = view(lat, 512, 256)

        bank = [ctx.enter_context(nc.psum_tensor(f"bank{i}", [P, 512], F32)) for i in range(8)]
        DB = bank[0:2]
        MB = bank[2]
        SB = bank[3:5]
        TB = bank[5:7]
        VB = bank[7]
        OB = (VB, MB)

        slot_in = [sem(f"slot_in{i}") for i in range(BUFFERS)]
        mod_used = sem("mod_used")
        e_used = sem("e_used")
        d_ready = [sem(f"d_ready{i}") for i in range(2)]
        d_free = [sem(f"d_free{i}") for i in range(2)]
        x_in = [sem(f"x_in{t}") for t in range(TOK)]
        early_in = sem("early_in")
        const_in = sem("const_in")
        nsa_table_in = sem("nsa_table_in")
        moba_table_in = [sem(f"moba_table_in{i}") for i in range(2)]
        ctx_in = sem("ctx_in")
        post_in = sem("post_in")
        wmask_in = sem("wmask_in")
        bg_in = sem("bg_in")
        bf_in = sem("bf_in")
        fin_in = sem("fin_in")
        out_done = sem("out_done")
        kv2_in = sem("kv2_in")
        zeroed = sem("zeroed")
        picked = sem("picked")
        kp_zeroed = sem("kp_zeroed")
        split_a = sem("split_a")
        split_v = sem("split_v")
        part_used = sem("part_used")
        high_ready = sem("high_ready")
        squares = sem("squares")
        means = sem("means")
        roots = sem("roots")
        normed = sem("normed")
        tanhs = sem("tanhs")
        cond_tanh = sem("cond_tanh")
        cond_ready = sem("cond_ready")
        mod_kept = sem("mod_kept")
        scores = sem("scores")
        masked = sem("masked")
        maxed = sem("maxed")
        exps = sem("exps")
        turns = sem("turns")
        turned_a = sem("turned_a")
        turned_b = sem("turned_b")
        pvs = sem("pvs")
        outs = sem("outs")
        blocks_ready = sem("blocks_ready")
        c_act = sem("c_act")
        c_vec = sem("c_vec")
        ya_ready = sem("ya_ready")
        yb_ready = sem("yb_ready")
        m_ready = sem("m_ready")
        x1_ready = sem("x1_ready")
        roped = sem("roped")
        lat_ready = sem("lat_ready")
        cat_ready = sem("cat_ready")
        u_scores = sem("u_scores")
        u_masked = sem("u_masked")
        u_neg = sem("u_neg")
        u_exp = sem("u_exp")
        u_turn = sem("u_turn")
        u_turned_a = sem("u_turned_a")
        u_turned_v = sem("u_turned_v")
        u_pv = sem("u_pv")
        u_out = sem("u_out")
        u_sink = sem("u_sink")
        x2_ready = sem("x2_ready")
        logit_max = sem("logit_max")
        logit_exp = sem("logit_exp")
        aff_ready = sem("aff_ready")
        slots_ready = sem("slots_ready")
        oh_ready = sem("oh_ready")
        side_turn = sem("side_turn")
        side_a = sem("side_a")
        side_v = sem("side_v")
        e_tanh = sem("e_tanh")
        e_h = sem("e_h")
        e_turn = sem("e_turn")
        e_hT = sem("e_hT")
        e_y = sem("e_y")
        e_y2 = sem("e_y2")
        e_out = sem("e_out")
        f_in = sem("f_in")
        y_ready = sem("y_ready")
        dve_step = sem("dve_step")
        act_step = sem("act_step")
        pool_step = sem("pool_step")

        def D_(name):
            return DB[BANK_OF[name]]

        def filled(eng, name):
            eng.wait_ge(d_ready[BANK_OF[name]], USE_OF[name])

        def kept(eng, name):
            eng.wait_ge(d_free[BANK_OF[name]], USE_OF[name])

        def branch_weights(name):
            return name in ("WA", "WB")

        def quarter_released(eng, k, q):
            name = SPLIT[k]
            base = sum(2 if branch_weights(n) else 3 for n in SPLIT[:k])
            if q == 3:
                filled(eng, LAST_USE[name])
            elif branch_weights(name):
                if q == 1:
                    filled(eng, LAST_USE[name][:3] + "0")
                else:
                    eng.wait_ge(part_used, base + 1 + q // 2)
            else:
                eng.wait_ge(part_used, base + q + 1)

        def quarter(tensor, name, q):
            return tensor[:, 1024 * q:1024 * q + 1024].rearrange("p (c n) -> p c n", c=2)[:, :, 0:WIDTH.get(name, 512)]

        def released(eng, name):
            if name in SPLIT:
                eng.wait_ge(split_v, 4 * SPLIT.index(name) + 4)
            elif name in LAST_USE:
                filled(eng, LAST_USE[name])
            elif name[0] == "M":
                eng.wait_ge(mod_used, int(name[1:]) + 1)
            else:
                group, part = name[1:].split(".")
                eng.wait_ge(e_used, 12 * int(group) + 4 * "GUD".index(name[0]) + int(part) + 1)

        def experts_done(eng, stage, g):
            released(eng, f"{stage}{g}.3")

        def leave(ins, name):
            ins.then_inc(d_free[BANK_OF[name]], 1)

        def bc(t, n):
            return t.rearrange("p (k n) -> p k n", n=1).to_broadcast([P, t.shape[1], n])

        def over(t, n):
            return t.rearrange("p (n k) -> p n k", n=1).to_broadcast([P, n, t.shape[1]])

        def mla_turned(name):
            i = 2 * int(name[2])
            return {"qm": qmT, "kx": kmT[:, :, S:2 * S], "kc": kmT[:, :, 0:S]}[name[:2]][0:QK, i:i + 2, :]

        block = ctx.enter_context(nc.Block())

        @block.sync
        def _(eng):
            stream = A["stream"]
            for t in range(TOK):
                eng.dma_start(xn[:, t, :], A["x"][t * P:(t + 1) * P, :]).then_inc(x_in[t], 16)
            for n, name in enumerate(STREAM):
                b = BUFFER[n]
                before = [k for k in range(n) if BUFFER[k] == b]
                if n >= N_DENSE and b == 4 and before[-1] < N_DENSE:
                    filled(eng, "kx2")
                    filled(eng, "kx3")
                elif before:
                    released(eng, STREAM[before[-1]])
                elif b == 4:
                    eng.wait_ge(scores, len(UNITS))
                elif b in (2, 3):
                    filled(eng, "wo11")
                elif b == 5:
                    eng.wait_ge(u_scores, 32)
                elif b >= 6:
                    eng.wait_ge(u_pv, 32)
                eng.dma_start(slot(name), stream[n, :, :]).then_inc(slot_in[b], 16)
                if name == "W2":
                    eng.dma_start(tabs[:, 0:8 * CAUSAL], A["nsa_table"]).then_inc(nsa_table_in, 16)
                if name == "W9":
                    kept(eng, "cO1")
                    eng.dma_start(cn, A["ctx"].rearrange("(t p) d -> p t d", p=P)).then_inc(ctx_in, 16)
                    eng.dma_start(post, A["norm_post"].to_broadcast([P, D])).then_inc(post_in, 16)
                    eng.dma_start(gG, A["b_mod"][:, 2 * D:3 * D].to_broadcast([P, D])).then_inc(bg_in, 16)
                    eng.dma_start(gF, A["b_mod"][:, 5 * D:6 * D].to_broadcast([P, D])).then_inc(bf_in, 16)
            for t in range(TOK):
                eng.wait_ge(y_ready, t + 1)
                eng.dma_start(out[t * P:(t + 1) * P, :], xn[:, t, :]).then_inc(out_done, 16)
            eng.wait_ge(out_done, 16 * TOK)

        @block.scalar
        def _(eng):
            act = nc.scalar
            steps = [0]

            def own(ins):
                steps[0] += 1
                ins.then_inc(act_step, 1)
                eng.wait_ge(act_step, steps[0])

            eng.dma_start(ident[:, :], A["ident"]).then_inc(early_in, 16)
            eng.dma_start(gcol, A["norm_pre"]).then_inc(early_in, 16)
            def copy(dst, src, name=None, scale=1.0):
                ins = act.activation(dst, src, ACT.Copy, scale=scale)
                if name:
                    leave(ins, name)
                return ins

            n_sq = [0]

            def sum_squares(src, k, junk):
                if n_sq[0]:
                    eng.wait_ge(squares, n_sq[0])
                act.activation(junk, src, ACT.Square, accum_out=ss[:, k:k + 1]).then_inc(squares, 1)
                n_sq[0] += 1

            for t in range(TOK):
                eng.wait_ge(x_in[t], 16)
                sum_squares(xn[:, t, :], t, pt[:, 0:D])
            n_const = 0
            for dst, name in ((w2k, "w2k"), (w2v, "w2v"), (cB, "cmp_bias"), (cM, "cmp_mask"), (view(vc, 4832, 32), "pe"),
                              (rope[:, :], "rope"), (nat, "norm_attn"), (nff, "norm_ffn"), (bmod, "b_mod_cols"),
                              (qn, "q_norm"), (kvn, "kv_norm"), (iota, "iota"), (cc, "cond"),
                              (wr.rearrange("p c e -> p (c e)"), "w_router")):
                eng.dma_start(dst, A[name]).then_inc(const_in, 16)
                n_const += 1
            eng.dma_start(sink, A["sink"].to_broadcast([P, 8])).then_inc(const_in, 16)

            def turned_mod(name, dst, add, mult):
                filled(eng, name)
                t = int(name[-2])
                for c in range(4):
                    k = 4 + c
                    ins = act.activation(dst[:, k, t * P:(t + 1) * P], D_(name)[:, c * P:(c + 1) * P], ACT.Identity,
                                         bias=add[:, k:k + 1], scale=mult[:, k:k + 1])
                leave(ins, name)

            for kind, n in SCHEDULE:
                if kind == "split":
                    name = SPLIT[n]
                    i = STREAM.index(name)
                    eng.wait_ge(slot_in[BUFFER[i]], 16 * TURN[i])
                    for q in range(4):
                        if n:
                            quarter_released(eng, n - 1, q)
                        copy(quarter(weight_parts, name, q), quarter(slot(name), name, q)).then_inc(split_a, 1)
                elif kind == "score":
                    u = n
                    eng.wait_ge(maxed, u + 1)
                    for b in range(2):
                        for q in range(TOK):
                            k = spn[:, u % 2, b, P * q:P + S * q]
                            ins = act.activation(k, k, ACT.Exp, bias=nm[:, u % 2, 2 * b + q:2 * b + q + 1],
                                                 accum_out=sums[:, u, 2 * b + q:2 * b + q + 1])
                    ins.then_inc(exps, 1)
                elif kind == "turn":
                    u = n
                    eng.wait_ge(turns, u + 1)
                    if u >= 2:
                        eng.wait_ge(pvs, u - 1)
                    copy(ptn[:, u % 2, 0, :], TB[0][:, 0:CAUSAL]).then_inc(turned_a, 1)
                elif kind == "dense":
                    name = n
                    if name in ("qa0", "qa1", "qb0", "qb1"):
                        filled(eng, name)
                        i = int(name[2])
                        dst = qaT if name[1] == "a" else qbT
                        copy(dst[:, 2 * i:2 * i + 2, :], D_(name)[:, :].rearrange("p (j s) -> p j s", j=2), name, HD ** -0.5)
                    elif name in ("vb0", "vb1"):
                        filled(eng, name)
                        copy(vB[:, int(name[2]), :], D_(name)[:, :], name)
                    elif name in ("va0", "va1"):
                        filled(eng, name)
                        t = int(name[2])
                        copy(vv[:, S * t:S * t + S], D_(name)[:, 0:S])
                        leave(act.activation(gates[:, t, :], D_(name)[:, S:S + 24], ACT.Tanh, scale=0.5), name)
                        if t == 1:
                            eng.wait_ge(const_in, 16 * (n_const + 1))
                            act.activation(ccE, cc, ACT.Tanh, scale=0.5).then_inc(cond_tanh, 1)
                    elif name == "kvs":
                        kept(eng, "kvc")
                        for g in range(2):
                            src = kvT[64 * g:64 * g + 64, :, :]
                            eng.dma_start(kv2[0:64, :, g, :], src).then_inc(kv2_in, 16)
                            eng.dma_start(kv2[64:128, :, g, 0:S - 1], src[:, :, 1:S]).then_inc(kv2_in, 16)
                    elif name in ("za0", "za1", "zb0", "zb1"):
                        filled(eng, name)
                        dst = za if name[1] == "a" else zb
                        act.activation(dst[:, int(name[2]), :], D_(name)[:, :], ACT.Tanh, scale=0.5)\
                           .then_inc(tanhs, 1)
                    elif name[:2] in ("gA", "gB"):
                        filled(eng, name)
                        t, h = int(name[2]), int(name[3])
                        if name[:2] == "gB":
                            kept(eng, f"wa{t}{h}")
                        leave(act.activation(eg[:, t, 512 * h:512 * h + 512], D_(name)[:, :], ACT.Tanh, scale=0.5), name)
                    elif name == "cH":
                        filled(eng, name)
                        act.activation(cE[0:30, :], D_(name)[0:30, 0:256], ACT.Tanh, scale=0.5).then_inc(c_act, 1)
                    elif name == "cS":
                        eng.wait_ge(c_vec, 2)
                        act.activation(cS, cS, ACT.Exp).then_inc(c_act, 1)
                    elif name == "cP":
                        filled(eng, name)
                        copy(cPT, D_(name)[:, :].rearrange("p (i q) -> p i q", i=4), name)
                    elif name[:3] in ("yaT", "ybT"):
                        filled(eng, name)
                        t = int(name[3])
                        copy((yaT if name[1] == "a" else ybT)[:, :, t * P:(t + 1) * P], D_(name)[:, :].rearrange("p (c s) -> p c s", c=4), None, 0.5)\
                            .then_inc(high_ready, 1)
                    elif name[:2] == "mT":
                        filled(eng, name)
                        t, h = int(name[2]), int(name[3])
                        copy(uhigh[:, 4 * h:4 * h + 4, t * P:(t + 1) * P],
                             D_(name)[:, :].rearrange("p (c s) -> p c s", c=4), None, 0.5).then_inc(high_ready, 1)
                    elif name in ("cxT01", "cxT11"):
                        turned_mod(name, hcT, mc[:, 1, 0:8], scl[:, 1, :])
                    elif name in ("hT01", "hT11"):
                        turned_mod(name, uT, mc[:, 0, 0:8], scl[:, 0, :])
                    elif name in ("ck0", "ck1"):
                        filled(eng, name)
                        copy(pc[:, int(name[2]), 0:256], D_(name)[:, 0:256], name)
                    elif name in ("cc0", "cc1"):
                        filled(eng, name)
                        t = int(name[2])
                        copy(pc[:, t, 256:544], D_(name)[:, 0:288], name)
                        kept(eng, name)
                        sum_squares(pc[:, t, 256:512], 6 + t, pt[:, 0:256])
                    elif name[:2] == "wo":
                        filled(eng, name)
                        t, h = int(name[2]), int(name[3])
                        copy(rn[:, t, 512 * h:512 * h + 512], D_(name)[:, :], name)
                        if h == 1:
                            kept(eng, f"wo{t}0")
                            kept(eng, name)
                            sum_squares(rn[:, t, :], 4 + t, sp[:, 0:D])
                            if t == 0:
                                eng.wait_ge(x1_ready, 1)
                                sum_squares(xn[:, 0, :], 8, sp[:, 0:D])
                    elif name == "bF1":
                        kept(eng, "modT2")
                        kept(eng, "bG0")
                        kept(eng, "bG1")
                        eng.dma_start(modr[:, 0:1024], A["window_mask"]).then_inc(wmask_in, 16)
                    elif name[:2] == "xa":
                        filled(eng, name)
                        t, h = int(name[2]), int(name[3])
                        w = 512 if h < 2 else 416
                        copy(px[:, t, 512 * h:512 * h + w], D_(name)[:, 0:w], name)
                        if h == 2:
                            kept(eng, name)
                            kept(eng, f"xa{t}1")
                            sum_squares(px[:, t, CQ:CQ + QR], 10 + 2 * t, pt[:, 1024:1024 + QR])
                            sum_squares(px[:, t, CKV:CKV + KVR], 11 + 2 * t, pt[:, 1024:1024 + KVR])
                    elif name in ("qwT0", "qwT1"):
                        filled(eng, name)
                        t = int(name[3])
                        copy(qwT[:, :, t * P:(t + 1) * P], D_(name)[:, :].rearrange("p (j s) -> p j s", j=4), name,
                             HD ** -0.5)
                    elif name[:2] == "qu":
                        filled(eng, name)
                        t, h = int(name[2]), int(name[3])
                        w = 480 if h == 0 else 288
                        copy(qcat[:, t, :, :].rearrange("p h d -> p (h d)")[:, 480 * h:480 * h + w], D_(name)[:, 0:w], name)
                    elif name[:3] in ("ckv", "xkv"):
                        filled(eng, name)
                        t, h = int(name[3]), int(name[4])
                        tk = t if name[0] == "c" else TOK + t
                        src = D_(name)[:, :].rearrange("p (h d) -> p h d", h=4)
                        copy(kcat[:, tk, 4 * h:4 * h + 4, 0:NOPE], src[:, :, 0:64])
                        leave(copy(vm[:, tk, 4 * h:4 * h + 4, :], src[:, :, 64:128]), name)
                        if name == "ckv00":
                            eng.wait_ge(x1_ready, 2)
                            sum_squares(xn[:, 1, :], 9, sp[:, 0:D])
                    elif name[:2] in ("qm", "kx", "kc") and int(name[2]) % 2 == 0:
                        filled(eng, name)
                        copy(mla_turned(name), D_(name)[0:QK, :].rearrange("p (h s) -> p h s", h=2), name)

            def soften(u):
                eng.wait_ge(u_neg, u + 1)
                if u < 16:
                    act.activation(sp3[:, u % 3, :], sp3[:, u % 3, :], ACT.Exp, bias=nm2[:, u:u + 1],
                                   accum_out=sm2[:, u:u + 1]).then_inc(u_exp, 1)
                    h = (u // 2) % 2 * 4 + u // 4
                    act.activation(sk2[:, u:u + 1], sink[:, h:h + 1], ACT.Exp, bias=nm2[:, u:u + 1]).then_inc(u_sink, 1)
                else:
                    eng.wait_ge(u_turn, u - 2)
                    act.activation(sp3[:, u % 3, :], SB[u % 2][:, :], ACT.Exp, bias=nm2[:, u:u + 1], scale=MLA_SCALE,
                                   accum_out=sm2[:, u:u + 1]).then_inc(u_exp, 1)

            def turned_out(name):
                filled(eng, name)
                t, h = int(name[2]), int(name[3])
                copy(uT[:, 4 * h:4 * h + 4, t * P:(t + 1) * P] if h else oT0[:, :, t * P:(t + 1) * P],
                     D_(name)[:, :].rearrange("p (c s) -> p c s", c=4), name)

            for r in range(34):
                if r < 32:
                    soften(r)
                if 1 <= r <= 32 and (r - 1) % 2 == 0:
                    u = r - 1
                    eng.wait_ge(u_turn, u + 1)
                    if u >= 2:
                        eng.wait_ge(u_pv, u - 1)
                    copy(pt2[:, 0, :], TB[0][:, :]).then_inc(u_turned_a, 1)
                if r in (OT_ROUND, OT_ROUND + 1):
                    turned_out(f"oT{r - OT_ROUND}0")

            def chosen(src, g):
                for c in range(4):
                    ins = act.activation(xsT[:, c, g * P:(g + 1) * P], src[:, c * P:(c + 1) * P], ACT.Identity,
                                         bias=mc[:, 0, 24 + c:25 + c], scale=scl[:, 2, c:c + 1])
                return ins

            for name in TAIL:
                if name in ("oT01", "oT11"):
                    turned_out(name)
                elif name == "ou01" or name == "ou11":
                    t = int(name[2])
                    eng.wait_ge(x2_ready, t + 1)
                    sum_squares(xn[:, t, :], 14 + t, sp[:, 0:D])
                elif name in ("rT01", "rT11"):
                    turned_mod(name, uT, mc[:, 0, 24:32], scl[:, 2, :])
                    if name == "rT11":
                        eng.dma_start(nfin, A["norm_final"].to_broadcast([P, D])).then_inc(fin_in, 16)
                elif name == "lg1":
                    eng.wait_ge(logit_max, 1)
                    act.activation(aff, aff, ACT.Exp).then_inc(logit_exp, 1)
                elif name == "gx0":
                    filled(eng, name)
                    leave(chosen(D_(name), 0), name)

            for g in range(NG):
                experts_done(eng, "G", g)
                if g:
                    eng.wait_ge(e_h, g)
                act.activation(hE, bank[0][:, :], ACT.Tanh, scale=0.5).then_inc(e_tanh, 1)
                if g == 0:
                    eng.wait_ge(side_turn, 1)
                    copy(ohT[:, 0:2, :], bank[2][:, :].rearrange("p (g s) -> p g s", g=2)).then_inc(side_a, 1)
                if g < NG - 1:
                    eng.wait_ge(side_turn, g + 2)
                    chosen(bank[2], g + 1).then_inc(side_a, 1)
                eng.wait_ge(e_turn, g + 1)
                copy(hT, bank[0][:, :], scale=0.5).then_inc(e_hT, 1)
                experts_done(eng, "D", g)
                if g:
                    eng.wait_ge(e_out, g)
                copy(yE[:, 0:512], bank[2][:, :]).then_inc(e_y, 1)
            for t in range(TOK):
                eng.wait_ge(f_in, t + 1)
                sum_squares(xn[:, t, :], t, sp[:, 0:D])

        @block.gpsimd
        def _(eng):
            pool = nc.gpsimd
            pool.memset(half[:, 2:3], -0.5)
            pool.memset(qk[:, 1024:2048], 0.0)
            pool.memset(qk[:, 3072:5120], 0.0)
            pool.memset(csil, 0.0)
            pool.memset(view(vc, 3072, 256), 0.0)
            pool.memset(view(vc, 3520, 544), 0.0).then_inc(zeroed, 1)
            eng.wait_ge(zeroed, 1)
            for n, (k, w) in enumerate([(0, 1), (1, 1), (2, 2), (6, 2), (4, 1), (8, 1), (5, 1), (9, 1), (10, 2), (12, 2),
                                        (14, 1), (15, 1), (0, 1), (1, 1)]):
                eng.wait_ge(means, n + 1)
                pool.tensor_tensor(rs[:, k:k + w], ss[:, k:k + w], half[:, 2:3].to_broadcast([P, w]), ALU.pow)\
                    .then_inc(roots, 1)
                if n == 1:
                    eng.wait_ge(blocks_ready, 2)
                    pool.memset(view(vc, 512, 512), 0.0).then_inc(zeroed, 1)
                    both = [t_.rearrange("p (a b) -> p a b", a=4) for t_ in (tabs[:, 0:8 * CAUSAL], A["moba_table"])]
                    for i in range(2):
                        eng.wait_ge(masked, 6 + 2 * i)
                        eng.dma_start(both[0][:, i::2], both[1][:, i::2]).then_inc(moba_table_in[i], 16)
                if n == 3:
                    kept(eng, "wb11")
                    pool.memset(lat[:, 0:512], 0.0).then_inc(pool_step, 1)
                    eng.wait_ge(pool_step, 1)
                    for j in range(4):
                        pool.memset(pick[32 * j:32 * j + 1, j, :], 1.0).then_inc(picked, 1)
                        eng.wait_ge(picked, j + 1)
                    pool.memset(vv[:, 0:1024], 0.0).then_inc(kp_zeroed, 1)

        @block.tensor
        def _(eng):
            pe_ = nc.tensor

            def loaded(name):
                n = STREAM.index(name)
                eng.wait_ge(slot_in[BUFFER[n]], 16 * TURN[n])

            def begin(name):
                if USE_OF[name] >= 2:
                    eng.wait_ge(d_free[BANK_OF[name]], USE_OF[name] - 1)
                return D_(name)

            def turn(dst, src, n=P, m=P):
                return pe_.transpose(dst, src, ident[0:n, 0:n])

            def turn_tiles(name, src, cols=P):
                o = begin(name)
                for c in range(4):
                    ins = turn(o[:, c * P:(c + 1) * P], src[:, c * P:(c + 1) * P])
                ins.then_inc(d_ready[BANK_OF[name]], 1)

            def product(o, lhs, rhs, chunks):
                for c in range(chunks):
                    ins = pe_.matmul(o, lhs(c), rhs(c), start=(c == 0), stop=(c == chunks - 1))
                return ins

            def parts_product(name, outs_, lhs, rhs, chunks, quarter=0, last=False):
                k = SPLIT.index(name)
                for i, o in enumerate(outs_):
                    for c in range(chunks):
                        if not last and i == 0 and c % 2 == 0:
                            eng.wait_ge(split_v, 4 * k + quarter + c // 2 + 1)
                        for n, (a, b) in enumerate(((0, 0), (0, 1), (1, 0))):
                            ins = pe_.matmul(o, lhs(a, c, i), rhs(b, c, i), start=(c == 0 and n == 0),
                                             stop=(c == chunks - 1 and n == 2))
                        if last and i == len(outs_) - 1 and c % 2 == 1 and c < chunks - 1:
                            ins.then_inc(part_used, 1)
                return ins

            split_weights = [weight_parts[:, a * SLOT:a * SLOT + SLOT].rearrange("p (c n) -> p c n", c=KC) for a in range(2)]

            def turned_products(name, sl, col, last):
                w, u = split_weights, (uhigh, xlow)
                return parts_product(sl, [D_(name)[:, 0:S], D_(name)[:, S:2 * S]],
                                     lambda a, c, i: w[a][:, c, col + P * i:col + P * i + P], lambda b, c, i: u[b][:, c, :],
                                     KC, 0, last)

            def split_rows(name, sl, t, low, last, width=512):
                w, u = split_weights, (uhigh, low)
                return parts_product(sl, [D_(name)[:, 0:width]], lambda a, c, i: u[a][:, c, t * P:(t + 1) * P],
                                     lambda b, c, i: w[b][:, c, 0:width], KC, 0, last)

            def rows_product(name, w, col, width, t, src, dst=0, chunks=KC):
                return product(D_(name)[:, dst:dst + width], lambda c: src[:, c, t * P:(t + 1) * P],
                               lambda c: w[:, c, col:col + width], chunks)

            def weights(name, chunks, width):
                return slot(name)[:, 0:chunks * width].rearrange("p (c n) -> p c n", c=chunks)

            def done(ins, name):
                ins.then_inc(d_ready[BANK_OF[name]], 1)

            def dense(name):
                if name[:2] == "xT":
                    t, h = int(name[2]), int(name[3])
                    if name == "xT00":
                        eng.wait_ge(early_in, 32)
                    eng.wait_ge(normed, t + 1)
                    turn_tiles(name, xrow[:, t, 512 * h:512 * h + 512])
                elif name in ("qa0", "qa1", "qb0", "qb1", "kb0", "kb1"):
                    i = int(name[2])
                    if name == "qa0":
                        for x in ("xT00", "xT01", "xT10", "xT11"):
                            kept(eng, x)
                    begin(name)
                    done(turned_products(name, {"qa": "W0", "qb": "W3", "kb": "W4"}[name[:2]], 256 * i, i == 1), name)
                elif name in ("kvc", "kvs"):
                    begin(name)
                    i = int(name == "kvs")
                    done(turned_products(name, "W1", 256 * i, i == 1), name)
                elif name[:2] in ("va", "vb", "za", "zb", "gA", "gB"):
                    t = int(name[2])
                    sl = {"va": "W2", "vb": "W5", "za": "W6", "zb": "W7", "gA": "W8", "gB": "W10"}[name[:2]]
                    if name[:2] in ("gA", "gB") and name[3] == "1":
                        sl = {"gA": "W9", "gB": "W11"}[name[:2]]
                    begin(name)
                    done(split_rows(name, sl, t, xlow, t == 1, WIDTH.get(sl, 512)), name)
                elif name == "cH":
                    loaded("WC")
                    eng.wait_ge(blocks_ready, 2)
                    begin(name)
                    w = slot("WC").rearrange("p (i l e) -> p i l e", i=2, l=LP)
                    for i in range(2):
                        ins = product(D_(name)[0:30, i * P:(i + 1) * P], lambda c: blk[:, i, c, :],
                                      lambda c: w[:, i, c, :], LP)
                    done(ins, name)
                elif name == "cT":
                    eng.wait_ge(c_vec, 1)
                    begin(name)
                    for i in range(2):
                        ins = turn(D_(name)[:, 32 * i:32 * i + 30], cH[0:30, i * P:(i + 1) * P], 30)
                    done(ins, name)
                elif name == "cK":
                    kept(eng, "cT")
                    begin(name)
                    pe_.matmul(D_(name)[:, 0:30], w2k, hkT, start=True, stop=True)
                    for g in range(2):
                        ins = pe_.matmul(D_(name)[:, 64 + 64 * g:128 + 64 * g],
                                         hvR[:, g, :, :].rearrange("p h n -> p (h n)"), w2v, start=True, stop=True)
                    done(ins, name)
                elif name == "cS":
                    kept(eng, "cK")
                    begin(name)
                    for q in range(TOK):
                        for j in range(4):
                            a = (q * 4 + j) * 32
                            ins = pe_.matmul(D_(name)[:, a:a + 32], qaT[:, j, q * P:(q + 1) * P],
                                             kcD.rearrange("p g n -> p (g n)"), start=True, stop=True)
                    done(ins, name)
                elif name == "cP":
                    eng.wait_ge(c_vec, 3)
                    begin(name)
                    for i in range(4):
                        ins = turn(D_(name)[:, i * P:(i + 1) * P], cP[:, i, :, :].rearrange("p h n -> p (h n)"))
                    done(ins, name)
                elif name in ("cO0", "cO1"):
                    kept(eng, "cP")
                    q = int(name[2])
                    begin(name)
                    for g in range(2):
                        ins = pe_.matmul(D_(name)[:, 256 * g:256 * g + 256], cPT[:, 2 * q + g, :], vcD[:, g, :],
                                         start=True, stop=True)
                    done(ins, name)
                elif name[:3] in ("yaT", "ybT"):
                    eng.wait_ge(ya_ready if name[1] == "a" else yb_ready, 1)
                    turn_tiles(name, (oa if name[1] == "a" else ob)[:, int(name[3]), :])
                elif name[:2] in ("wa", "wb"):
                    t, h = int(name[2]), int(name[3])
                    if (t, h) == (0, 0):
                        for i in range(2):
                            kept(eng, f"y{name[1]}T{i}")
                    begin(name)
                    w = [w_[:, 4 * h:4 * h + 4, :] for w_ in split_weights]
                    y = (yaT, yalow) if name[1] == "a" else (ybT, yblow)
                    done(parts_product("WA" if name[1] == "a" else "WB", [D_(name)[:, :]],
                                       lambda a, c, i: y[a][:, c, t * P:(t + 1) * P], lambda b, c, i: w[b][:, c, :],
                                       4, 2 * h, t == 1), name)
                elif name[:2] == "mT":
                    t, h = int(name[2]), int(name[3])
                    eng.wait_ge(m_ready, 2 * h + t + 1)
                    turn_tiles(name, mrow[:, t, 512 * h:512 * h + 512])
                elif name[:4] == "modT":
                    r = int(name[4])
                    eng.wait_ge(mod_kept, r + 1)
                    turn_tiles(name, mod[:, r, :])
                elif name[:3] == "cxT":
                    t, h = int(name[3]), int(name[4])
                    eng.wait_ge(normed, 3 + t)
                    turn_tiles(name, cn[:, t, 512 * h:512 * h + 512])
                elif name in ("ck0", "ck1", "cc0", "cc1"):
                    t = int(name[2])
                    if t == 0:
                        loaded("C0" if name[1] == "k" else "C1")
                        for x in ("cxT00", "cxT01", "cxT10", "cxT11"):
                            kept(eng, x)
                    begin(name)
                    width = 256 if name[1] == "k" else 288
                    w = weights("C0" if name[1] == "k" else "C1", KC, width)
                    done(rows_product(name, w, 0, width, t, hcT), name)
                elif name == "clT":
                    eng.wait_ge(lat_ready, 1)
                    begin(name)
                    for c in range(2):
                        for t in range(TOK):
                            ins = turn(D_(name)[:, c * S + t * P:c * S + (t + 1) * P], pc[:, t, 256 + c * P:256 + (c + 1) * P])
                    done(ins, name)
                elif name[:3] in ("ckv", "xkv"):
                    t, h = int(name[3]), int(name[4])
                    sl = "KU0" if name[0] == "c" else "KU1"
                    if (t, h) == (0, 0):
                        loaded(sl)
                        if name[0] == "c":
                            kept(eng, "clT")
                    if h == 0 and name[0] == "x":
                        kept(eng, f"lk{t}")
                    begin(name)
                    done(rows_product(name, weights(sl, 2, D), 512 * h, 512, t, lcT if name[0] == "c" else lkT, 0, 2),
                         name)
                elif name[:2] == "wo":
                    t, h = int(name[2]), int(name[3])
                    if h == 0:
                        for i in range(2):
                            kept(eng, f"mT{t}{i}")
                    begin(name)
                    done(split_rows(name, f"WO{h}", t, mlow, t == 1), name)
                elif name[:2] in ("bG", "bF"):
                    h = int(name[2])
                    eng.wait_ge(picked, 4)
                    begin(name)
                    r, j = (1, h) if name[1] == "G" else (2, 2 + h)
                    done(pe_.matmul(D_(name)[:, :], pick[:, j, :], mod[:, r, :], start=True, stop=True), name)
                elif name[:2] == "hT":
                    t, h = int(name[2]), int(name[3])
                    eng.wait_ge(normed, 5 + t)
                    turn_tiles(name, rn[:, t, 512 * h:512 * h + 512])
                elif name[:2] == "xa":
                    t, h = int(name[2]), int(name[3])
                    if t == 0:
                        loaded(f"X{h}")
                    if h == 0:
                        for i in range(2):
                            kept(eng, f"hT{t}{i}")
                    begin(name)
                    width = 512 if h < 2 else 416
                    done(rows_product(name, weights(f"X{h}", KC, width), 0, width, t, uT), name)
                elif name in ("qwT0", "qwT1"):
                    t = int(name[3])
                    eng.wait_ge(roped, t + 1)
                    turn_tiles(name, px[:, t, 0:512])
                elif name == "kwT":
                    begin(name)
                    for i in range(4):
                        src = pc[:, i, 0:P] if i < 2 else px[:, i - 2, KA:KA + P]
                        ins = turn(D_(name)[:, i * P:(i + 1) * P], src)
                    done(ins, name)
                elif name[:2] in ("lq", "lk"):
                    t = int(name[2])
                    eng.wait_ge(lat_ready, t + 2)
                    begin(name)
                    base, n = (CQ, 3) if name[1] == "q" else (CKV, 2)
                    for c in range(n):
                        ins = turn(D_(name)[:, c * P:(c + 1) * P], px[:, t, base + c * P:base + (c + 1) * P])
                    done(ins, name)
                elif name[:2] == "qu":
                    t, h = int(name[2]), int(name[3])
                    if (t, h) == (0, 0):
                        loaded("QU")
                    if h == 0:
                        kept(eng, f"lq{t}")
                    begin(name)
                    width = 480 if h == 0 else 288
                    done(rows_product(name, weights("QU", 3, 768), 480 * h, width, t, lqT, 0, 3), name)
                elif name[:2] in ("qm", "kx", "kc"):
                    i = int(name[2])
                    if name == "qm0":
                        eng.wait_ge(cat_ready, 3)
                    if name == "kx0":
                        kept(eng, "xkv10")
                        kept(eng, "xkv11")
                    if name == "kc0":
                        kept(eng, "ckv10")
                        kept(eng, "ckv11")
                        eng.wait_ge(cat_ready, 1)
                    src, t0 = {"qm": (qcat, 0), "kx": (kcat, TOK), "kc": (kcat, 0)}[name[:2]]
                    begin(name)
                    for b in range(2):
                        for t in range(TOK):
                            ins = turn(D_(name)[0:QK, b * S + t * P:b * S + (t + 1) * P], src[:, t0 + t, 2 * i + b, :])
                    done(ins, name)

            def mod_slot(n):
                loaded(f"M{n}")
                if n == 0:
                    eng.wait_ge(cond_ready, 1)
                if n % 4 == 0 and n:
                    eng.wait_ge(mod_kept, n // 4)
                w = slot(f"M{n}").rearrange("p (k n) -> p k n", k=2)
                for k in range(2):
                    for j in range(4):
                        c = n % 4 * 2 + k
                        ins = pe_.matmul(MB[32 * j:32 * j + 32, :], csil[:, c, :], w[:, k, 512 * j:512 * j + 512],
                                         start=(c == 0), stop=(c == KC - 1), tile_position=(0, 32 * j))
                ins.then_inc(mod_used, 1)

            def operands(u):
                kind, j = UNITS[u]
                q = qbT if kind == MOBA else qaT
                k = {NSA: ksD, WIN: kwD, MOBA: kbD[:, j, :, :]}[kind]
                return q[:, j, :], k

            for kind, n in SCHEDULE:
                if kind == "dense":
                    dense(n)
                elif kind == "mod":
                    mod_slot(n)
                elif kind == "score":
                    q, k = operands(n)
                    if n == 0:
                        kept(eng, "kvs")
                        kept(eng, "qa0")
                        kept(eng, "qa1")
                    if n == 8:
                        for x in ("qb0", "qb1", "kb0", "kb1"):
                            kept(eng, x)
                    if n:
                        eng.wait_ge(masked, n)
                    pe_.matmul(SB[0][:, :], q[:, P:S], k.rearrange("p g s -> p (g s)"), start=True, stop=True)
                    pe_.matmul(SB[1][:, 0:S].rearrange("p (g s) -> p g s", g=2), q[:, 0:P], k[:, :, 0:P],
                               start=True, stop=True).then_inc(scores, 1)
                elif kind == "turn":
                    u = n
                    eng.wait_ge(exps, u + 1)
                    if u:
                        eng.wait_ge(turned_a, u)
                        eng.wait_ge(turned_b, u)
                    for b in range(2):
                        for i in range(3):
                            ins = turn(TB[b][:, i * P:(i + 1) * P], spn[:, u % 2, b, i * P:(i + 1) * P])
                    ins.then_inc(turns, 1)
                elif kind == "pv":
                    u = n
                    typ, j = UNITS[u]
                    v = {NSA: vS, WIN: vW, MOBA: vB}[typ]
                    eng.wait_ge(turned_a, u + 1)
                    eng.wait_ge(turned_b, u + 1)
                    if u == 0:
                        kept(eng, "va0")
                        kept(eng, "va1")
                    if u == 8:
                        kept(eng, "vb0")
                        kept(eng, "vb1")
                    if u:
                        eng.wait_ge(outs, u)
                    for b in range(2):
                        c = HD * b if typ != MOBA else HD * (2 * j + b)
                        o = VB[:, 128 * b:128 * b + 128]
                        pr = ptn[:, u % 2, b, :]
                        pe_.matmul(o[:, 0:64], pr[:, 0:P], v[:, 0, c:c + HD], start=True, stop=True)
                        pe_.matmul(o[:, 64:128], pr[:, P:2 * P], v[:, 0, c:c + HD], start=True, stop=False)
                        ins = pe_.matmul(o[:, 64:128], pr[:, 2 * P:3 * P], v[:, 1, c:c + HD], start=False, stop=True)
                    ins.then_inc(pvs, 1)

            def unit_scores(u):
                q = u % 2
                if u == 0:
                    for x in ("qwT0", "qwT1", "kwT"):
                        kept(eng, x)
                if u == 16:
                    for x in ("qm2", "qm3", "kx2", "kx3"):
                        kept(eng, x)
                if u == 0:
                    eng.wait_ge(masked, len(UNITS))
                if u >= 2:
                    eng.wait_ge(u_masked, min(u - 1, 16))
                    if u >= 18:
                        eng.wait_ge(u_exp, u - 1)
                o = SB[u % 2][:, :]
                if u < 16:
                    j, b = u // 4, u // 2 % 2
                    ins = pe_.matmul(o, qwT[:, j, q * P:(q + 1) * P], kP[:, b, :], start=True, stop=True)
                else:
                    h = (u - 16) // 2
                    ins = pe_.matmul(o, qmT[0:QK, h, q * P:(q + 1) * P], kmT[0:QK, h, :], start=True, stop=True)
                ins.then_inc(u_scores, 1)

            def unit_turn(u):
                eng.wait_ge(u_exp, u + 1)
                if u == 0:
                    eng.wait_ge(turned_a, len(UNITS))
                if u == 1:
                    eng.wait_ge(turned_b, len(UNITS))
                if u >= 2:
                    eng.wait_ge(u_turned_a if u % 2 == 0 else u_turned_v, u // 2)
                for i in range(4):
                    ins = turn(TB[u % 2][:, i * P:(i + 1) * P], sp3[:, u % 3, i * P:(i + 1) * P])
                ins.then_inc(u_turn, 1)

            def unit_pv(u):
                eng.wait_ge(u_turned_a if u % 2 == 0 else u_turned_v, u // 2 + 1)
                if u >= 2:
                    eng.wait_ge(u_out, u - 1)
                else:
                    eng.wait_ge(outs, len(UNITS))
                o = OB[u % 2][:, 0:HD]
                for i in range(4):
                    if u < 16:
                        b = u // 2 % 2
                        v = (pc[:, i, P + HD * b:P + HD * (b + 1)] if i < 2 else
                             xv[:, (i - 2) * P + HD * b:(i - 2) * P + HD * (b + 1)])
                    else:
                        v = vm[:, i, (u - 16) // 2, :]
                    ins = pe_.matmul(o, pt2[:, u % 2, i * P:(i + 1) * P], v, start=(i == 0), stop=(i == 3))
                ins.then_inc(u_pv, 1)

            def tail(name):
                if name[:2] == "oT":
                    t, h = int(name[2]), int(name[3])
                    eng.wait_ge(u_out, 16 * (h + 1))
                    turn_tiles(name, o2[:, t, 512 * h:512 * h + 512])
                elif name[:2] == "ou":
                    t, h = int(name[2]), int(name[3])
                    if t == 0:
                        loaded(f"OUT{h}")
                    if h == 0:
                        for i in range(2):
                            kept(eng, f"oT{t}{i}")
                    begin(name)
                    w = weights(f"OUT{h}", KC, 512)
                    done(product(D_(name)[:, :], lambda c: (oT0 if c < 4 else uT)[:, c, t * P:(t + 1) * P],
                                 lambda c: w[:, c, :], KC), name)
                elif name[:2] == "rT":
                    t, h = int(name[2]), int(name[3])
                    eng.wait_ge(normed, 7 + t)
                    turn_tiles(name, rn[:, t, 512 * h:512 * h + 512])
                elif name in ("lg0", "lg1"):
                    t = int(name[2])
                    for h in range(2):
                        kept(eng, f"rT{t}{h}")
                    begin(name)
                    done(product(D_(name)[:, 0:E], lambda c: uT[:, c, t * P:(t + 1) * P], lambda c: wr[:, c, :], KC),
                         name)
                elif name == "afT":
                    eng.wait_ge(aff_ready, 1)
                    begin(name)
                    for t in range(TOK):
                        ins = turn(D_(name)[0:E, t * P:(t + 1) * P], aff[:, t, :])
                    done(ins, name)
                elif name == "slT":
                    eng.wait_ge(slots_ready, 1)
                    begin(name)
                    for t in range(TOK):
                        ins = turn(D_(name)[:, t * E:(t + 1) * E], cum[0:E, t * P:(t + 1) * P], E)
                    done(ins, name)
                elif name in ("gx0", "gx1"):
                    eng.wait_ge(oh_ready, 1)
                    begin(name)
                    done(gather(D_(name), 0, int(name[2])), name)

            def gather(o, g, half):
                for i in range(4):
                    c = 4 * half + i
                    for t in range(TOK):
                        ins = pe_.matmul(o[:, i * P:(i + 1) * P], rn[:, t, c * P:(c + 1) * P], oh[:, t, g * P:(g + 1) * P],
                                         start=(t == 0), stop=(t == TOK - 1))
                return ins

            for r in range(34):
                if r < 32:
                    unit_scores(r)
                if 1 <= r <= 32:
                    unit_turn(r - 1)
                if r >= 2:
                    unit_pv(r - 2)
                if r in (OT_ROUND, OT_ROUND + 1):
                    tail(f"oT{r - OT_ROUND}0")

            for name in TAIL[2:]:
                tail(name)

            kept(eng, "gx0")
            kept(eng, "gx1")
            for g in range(NG):
                for m, b in (("G", 0), ("U", 1)):
                    if g:
                        eng.wait_ge(e_hT if b == 0 else e_h, g)
                    for i in range(4):
                        loaded(f"{m}{g}.{i}")
                        w = slot(f"{m}{g}.{i}").rearrange("p (e k n) -> p e k n", e=EG, k=2)
                        for k in range(2):
                            c = 2 * i + k
                            for e in range(EG):
                                a = (EG * g + e) * CAP
                                ins = pe_.matmul(bank[b][32 * e:32 * e + 32, :], xsT[:, c, a:a + CAP], w[:, e, k, :],
                                                 start=(c == 0), stop=(c == KC - 1), tile_position=(0, 32 * e))
                        ins.then_inc(e_used, 1)
                if g:
                    eng.wait_ge(e_y, g)
                    eng.wait_ge(e_y2, g)
                if g == 0:
                    eng.wait_ge(oh_ready, 3)
                    for i in range(2):
                        for k in range(2):
                            for t in range(TOK):
                                a = (2 * i + k) * P
                                ins = turn(bank[2 + i][:, k * S + t * P:k * S + (t + 1) * P], ohv[:, t, a:a + P])
                    ins.then_inc(side_turn, 1)
                    eng.wait_ge(side_a, 1)
                    eng.wait_ge(side_v, 1)
                if g < NG - 1:
                    eng.wait_ge(oh_ready, 2)
                    for i in range(2):
                        ins = gather(bank[2 + i], g + 1, i)
                    ins.then_inc(side_turn, 1)
                eng.wait_ge(e_h, g + 1)
                for i in range(4):
                    ins = turn(bank[0][:, i * P:(i + 1) * P], hA[:, i * P:(i + 1) * P])
                ins.then_inc(e_turn, 1)
                eng.wait_ge(e_hT, g + 1)
                if g < NG - 1:
                    eng.wait_ge(side_a, g + 2)
                    eng.wait_ge(side_v, g + 2)
                for i in range(4):
                    loaded(f"D{g}.{i}")
                    w = slot(f"D{g}.{i}").rearrange("p (e n) -> p e n", e=EG)
                    for h in range(2):
                        for e in range(EG):
                            ins = pe_.matmul(bank[2 + h][32 * e:32 * e + 32, :], hT[:, i * P + 32 * e:i * P + 32 * e + 32],
                                             w[:, e, 512 * h:512 * h + 512], start=(i == 0), stop=(i == 3),
                                             tile_position=(0, 32 * e))
                    ins.then_inc(e_used, 1)
                eng.wait_ge(e_y, g + 1)
                eng.wait_ge(e_y2, g + 1)
                for t in range(TOK):
                    for h in range(2):
                        ins = pe_.matmul(bank[4 + 2 * t + h][:, :], ohT[:, g, t * P:(t + 1) * P],
                                         yE[:, 512 * h:512 * h + 512], start=(g == 0), stop=(g == NG - 1))
                    if t == TOK - 1 or g == NG - 1:
                        ins.then_inc(e_out, 1)

        @block.vector
        def _(eng):
            dve = nc.vector
            steps = [0]
            n_mean = [0]
            n_norm = [0]

            def own(ins):
                steps[0] += 1
                ins.then_inc(dve_step, 1)
                eng.wait_ge(dve_step, steps[0])

            def mean_root(k, w, width, n_squares):
                eng.wait_ge(squares, n_squares)
                dve.tensor_scalar(ss[:, k:k + w], ss[:, k:k + w], 1.0 / width, EPS, ALU.mult, ALU.add).then_inc(means, 1)
                n_mean[0] += 1
                eng.wait_ge(roots, n_mean[0])

            def turned_mod(name, dst, add, mult):
                filled(eng, name)
                t, h = int(name[-2]), int(name[-1])
                for c in range(4):
                    k = 4 * h + c
                    o, i = dst[:, k, t * P:(t + 1) * P], D_(name)[:, c * P:(c + 1) * P]
                    if add is None:
                        ins = dve.tensor_scalar(o, i, mult[:, k:k + 1], None, ALU.mult)
                    else:
                        ins = dve.tensor_scalar(o, i, mult[:, k:k + 1], add[:, k:k + 1], ALU.mult, ALU.add)
                leave(ins, name)

            def normalise(t, k, n_squares, dst=rn):
                mean_root(k + t, 1, D, n_squares)
                dve.tensor_scalar(dst[:, t, :], xn[:, t, :], rs[:, k + t:k + t + 1], None, ALU.mult).then_inc(normed, 1)

            def block1_norm(t):
                mean_root(4 + t, 1, D, 5 + 2 * t)
                eng.wait_ge(post_in, 16)
                own(dve.scalar_tensor_tensor(rn[:, t, :], rn[:, t, :], rs[:, 4 + t:5 + t], post, ALU.mult, ALU.mult))
                dve.tensor_tensor(xn[:, t, :], xn[:, t, :], rn[:, t, :], ALU.add).then_inc(x1_ready, 1)
                eng.wait_ge(x1_ready, t + 1)

            def rotate(x, t, heads, n, at):
                w = 4 * n
                cos = rope[:, at + t * w:at + (t + 1) * w]
                sin = rope[:, at + (TOK + t) * w:at + (TOK + t + 1) * w]
                a, b = (rt[:, i, 0:heads * w].rearrange("p (h d) -> p h d", h=heads) for i in range(2))
                dve.tensor_tensor(a, x, over(cos, heads), ALU.mult)
                b5 = rt[:, 1, 0:heads * w].rearrange("p (h a f n) -> p h a f n", h=heads, a=2, f=2)
                s4 = sin.rearrange("p (h a f n) -> p h a f n", h=1, a=2, f=2)
                x5 = x.rearrange("p h (a f n) -> p h a f n", a=2, f=2)
                for f in range(2):
                    ins = dve.tensor_tensor(b5[:, :, :, f, :], x5[:, :, :, 1 - f, :],
                                            s4[:, :, :, f, :].to_broadcast([P, heads, 2, n]), ALU.mult)
                own(ins)
                return dve.tensor_tensor(x, a, b, ALU.add)

            def late_x(t):
                kept(eng, f"xa{t}1")
                kept(eng, f"xa{t}2")
                rotate(px[:, t, 0:640].rearrange("p (h d) -> p h d", d=HD), t, 10, 16, 0).then_inc(roped, 1)
                eng.wait_ge(roped, t + 1)
                own(rotate(px[:, t, KR:KR + ROPE].rearrange("p (h d) -> p h d", h=1), t, 1, 8, 256))
                own(dve.tensor_copy(kcat[:, TOK + t, :, NOPE:QK], over(px[:, t, KR:KR + ROPE], HB)))
                i = 10 + 2 * t
                eng.wait_ge(squares, i)
                dve.tensor_scalar(ss[:, i:i + 1], ss[:, i:i + 1], 1.0 / QR, EPS, ALU.mult, ALU.add)
                dve.tensor_scalar(ss[:, i + 1:i + 2], ss[:, i + 1:i + 2], 1.0 / KVR, EPS, ALU.mult, ALU.add)\
                   .then_inc(means, 1)
                n_mean[0] += 1
                eng.wait_ge(roots, n_mean[0])
                dve.tensor_scalar(px[:, t, CQ:CQ + QR], px[:, t, CQ:CQ + QR], rs[:, i:i + 1], None, ALU.mult)
                dve.tensor_scalar(px[:, t, CKV:CKV + KVR], px[:, t, CKV:CKV + KVR], rs[:, i + 1:i + 2], None, ALU.mult)\
                   .then_inc(lat_ready, 1)

            def rope_q(t):
                kept(eng, f"qu{t}0")
                kept(eng, f"qu{t}1")
                rotate(qcat[:, t, :, NOPE:QK], t, HB, 8, 256).then_inc(cat_ready, 1)
                eng.wait_ge(cat_ready, t + 2)

            def spread_keys(name, src, dst):
                dve.tensor_copy(dst[0:64, 0], src[0:64])
                return dve.tensor_copy(dst[64:128, 1], src[64:128])

            for t in range(TOK):
                normalise(t, 0, t + 1, xrow)

            def unit_mask(u):
                kind, j = UNITS[u]
                eng.wait_ge(scores, u + 1)
                if u == 0:
                    eng.wait_ge(nsa_table_in, 16)
                if u in (8, 9):
                    eng.wait_ge(moba_table_in[u - 8], 16)
                if u >= 2:
                    eng.wait_ge(turns, u - 1)
                for b in range(2):
                    h = j + 4 * b if kind != MOBA else 2 * j + b
                    for q in range(TOK):
                        w = P if q == 0 else S
                        src = SB[1 - q][:, b * w:(b + 1) * w]
                        ins = dve.tensor_tensor_reduce(spn[:, u % 2, b, P * q:P * q + w], src,
                                                       table[:, h, P * q:P * q + w], 1.0, -3e38, ALU.add, ALU.max,
                                                       mx[:, u % 2, 2 * b + q:2 * b + q + 1])
                ins.then_inc(masked, 1)
                eng.wait_ge(masked, u + 1)
                dve.tensor_scalar(nm[:, u % 2, :], mx[:, u % 2, :], -1.0, None, ALU.mult).then_inc(maxed, 1)

            def unit_out(u):
                kind, j = UNITS[u]
                eng.wait_ge(pvs, u + 1)
                own(dve.reciprocal(rc[:, u, :], sums[:, u, :]))
                if kind != MOBA:
                    i = 8 * (kind + 1) + j
                    own(dve.tensor_tensor(rc[:, u, :].rearrange("p (b q) -> p b q", b=2),
                                          rc[:, u, :].rearrange("p (b q) -> p b q", b=2),
                                          gates[:, :, i:i + 5:4].rearrange("p q b -> p b q"), ALU.mult))
                for b in range(2):
                    h = j + 4 * b if kind != MOBA else 2 * j + b
                    for q in range(TOK):
                        o = VB[:, 128 * b + 64 * q:128 * b + 64 * q + 64]
                        r = rc[:, u, 2 * b + q:2 * b + q + 1]
                        dst = (ob if kind == MOBA else oa)[:, q, HD * h:HD * h + HD]
                        if kind == WIN:
                            ins = dve.scalar_tensor_tensor(dst, o, r, dst, ALU.mult, ALU.add)
                        else:
                            ins = dve.tensor_scalar(dst, o, r, None, ALU.mult)
                ins.then_inc(outs, 1)

            n_high = [0]

            def low_part(name, dst, high):
                n_high[0] += 1
                eng.wait_ge(high_ready, n_high[0])
                leave(dve.scalar_tensor_tensor(dst, D_(name)[:, :].rearrange("p (c s) -> p c s", c=4), 0.5, high.bitcast(F32),
                                               ALU.mult, ALU.subtract), name)

            for kind, n in SCHEDULE:
                if kind == "split":
                    name = SPLIT[n]
                    for q in range(4):
                        eng.wait_ge(split_a, 4 * n + q + 1)
                        dve.tensor_tensor(quarter(weight_parts[:, SLOT:], name, q), quarter(slot(name), name, q),
                                          quarter(weight_parts, name, q).bitcast(F32), ALU.subtract)\
                           .then_inc(split_v, 1)
                elif kind == "score":
                    unit_mask(n)
                elif kind == "turn":
                    u = n
                    eng.wait_ge(turns, u + 1)
                    if u >= 2:
                        eng.wait_ge(pvs, u - 1)
                    dve.tensor_copy(ptn[:, u % 2, 1, :], TB[1][:, 0:CAUSAL]).then_inc(turned_b, 1)
                elif kind == "pv":
                    unit_out(n)
                elif kind == "mod":
                    if n % 4 == 3:
                        eng.wait_ge(mod_used, n + 1)
                        dve.tensor_copy(mod[:, n // 4, :], MB[:, :]).then_inc(mod_kept, 1)
                elif kind == "ya":
                    eng.wait_ge(outs, 8)
                    kept(eng, "cO1")
                    dve.tensor_tensor(mo[:, 2048:3072], mo[:, 2048:3072], zz[:, 0:1024], ALU.mult).then_inc(ya_ready, 1)
                elif kind == "yb":
                    eng.wait_ge(outs, 12)
                    dve.tensor_tensor(mo[:, 3072:4096], mo[:, 3072:4096], zz[:, 1024:2048], ALU.mult).then_inc(yb_ready, 1)
                elif kind == "context":
                    eng.wait_ge(ctx_in, 16)
                    for t in range(TOK):
                        own(dve.tensor_tensor_reduce(pt[:, 0:D], cn[:, t, :], cn[:, t, :], 1.0, 0.0, ALU.mult,
                                                     ALU.add, ss[:, 2 + t:3 + t]))
                    mean_root(2, 2, D, 2)
                    for t in range(TOK):
                        dve.tensor_scalar(cn[:, t, :], cn[:, t, :], rs[:, 2 + t:3 + t], None, ALU.mult)\
                           .then_inc(normed, 1)
                elif kind == "dense":
                    name = n
                    if name[:2] == "xT":
                        if name == "xT00":
                            eng.wait_ge(early_in, 32)
                        filled(eng, name)
                        t, h = int(name[2]), int(name[3])
                        own(dve.tensor_tensor(uhigh[:, 4 * h:4 * h + 4, t * P:(t + 1) * P],
                                              D_(name)[:, :].rearrange("p (c s) -> p c s", c=4),
                                              bc(gcol[:, 4 * h:4 * h + 4], P), ALU.mult))
                        for c in range(4):
                            k = 4 * h + c
                            ins = dve.scalar_tensor_tensor(xlow[:, k, t * P:(t + 1) * P], D_(name)[:, c * P:(c + 1) * P],
                                                           gcol[:, k:k + 1],
                                                           uhigh[:, k, t * P:(t + 1) * P].bitcast(F32), ALU.mult,
                                                           ALU.subtract)
                        leave(ins, name)
                    elif name == "kvc":
                        filled(eng, name)
                        leave(dve.tensor_copy(kvT, D_(name)[:, :].rearrange("p (i s) -> p i s", i=2)), name)
                    elif name == "kvs":
                        filled(eng, name)
                        spread_keys(name, D_(name)[:, 0:S], ksD)
                        leave(spread_keys(name, D_(name)[:, S:2 * S], kwD), name)
                    elif name in ("yaT0", "yaT1", "ybT0", "ybT1"):
                        t = int(name[3])
                        high, low = (yaT, yalow) if name[1] == "a" else (ybT, yblow)
                        low_part(name, low[:, :, t * P:(t + 1) * P], high[:, :, t * P:(t + 1) * P])
                    elif name[:2] == "mT":
                        t, h = int(name[2]), int(name[3])
                        low_part(name, mlow[:, 4 * h:4 * h + 4, t * P:(t + 1) * P], uhigh[:, 4 * h:4 * h + 4, t * P:(t + 1) * P])
                    elif name == "va1":
                        kept(eng, name)
                        own(dve.tensor_scalar(gates, gates, 0.5, 0.5, ALU.mult, ALU.add))
                        eng.wait_ge(kv2_in, 16 * 4)
                        eng.wait_ge(const_in, 16 * 15)
                        for i in range(2):
                            for a in range(2):
                                src = kv2[:, i, :, :].rearrange("p g (n l r) -> p g n l r", l=8, r=2)
                                src = src[:, :, a:a + N_CMP, :, 0].rearrange("p g n l -> p l g n")
                                dst = blk[:, i, 8 * a:8 * a + 8, :].rearrange("p l (g n) -> p l g n", g=2)
                                pos = pe[:, i, 8 * a:8 * a + 8].rearrange("p (l g n) -> p l g n", g=1, n=1)
                                ins = dve.tensor_tensor(dst, src, pos.to_broadcast([P, 8, 2, N_CMP]), ALU.add)
                            ins.then_inc(blocks_ready, 1)
                        eng.wait_ge(cond_tanh, 1)
                        eng.wait_ge(zeroed, 1)
                        own(dve.scalar_tensor_tensor(ccE, ccE, 1.0, cc, ALU.add, ALU.mult))
                        dve.tensor_scalar(csil[:, :, 0:2], ccE.rearrange("p (c v) -> p c v", c=KC), 0.5, None, ALU.mult)\
                           .then_inc(cond_ready, 1)
                    elif name in ("kb0", "kb1"):
                        filled(eng, name)
                        i = int(name[2])
                        src = D_(name)[:, :].rearrange("p (j s) -> p j s", j=2)
                        dve.tensor_copy(kbD[0:64, 2 * i:2 * i + 2, 0, :], src[0:64])
                        leave(dve.tensor_copy(kbD[64:128, 2 * i:2 * i + 2, 1, :], src[64:128]), name)
                    elif name in ("za0", "za1", "zb0", "zb1"):
                        k = {"za0": 1, "za1": 2, "zb0": 3, "zb1": 4}[name]
                        eng.wait_ge(tanhs, k)
                        z = (za if name[1] == "a" else zb)[:, int(name[2]), :]
                        leave(dve.scalar_tensor_tensor(z, z, 1.0, D_(name)[:, :], ALU.add, ALU.mult), name)
                    elif name == "cH":
                        eng.wait_ge(c_act, 1)
                        leave(dve.scalar_tensor_tensor(cH[0:30, :], cE[0:30, :], 1.0, D_(name)[0:30, 0:256], ALU.add,
                                                       ALU.mult), name)
                        kept(eng, name)
                        dve.tensor_scalar(cH[0:30, :], cH[0:30, :], 0.5, None, ALU.mult).then_inc(c_vec, 1)
                    elif name == "cT":
                        filled(eng, name)
                        dve.tensor_copy(hkT, D_(name)[:, 0:30])
                        for g in range(2):
                            ins = dve.tensor_copy(hvR[:, g, :, 0:15],
                                                  D_(name)[:, 32 + 15 * g:47 + 15 * g].rearrange("p (a n) -> p a n", a=1)
                                                  .to_broadcast([P, 4, 15]))
                        leave(ins, name)
                    elif name == "cK":
                        filled(eng, name)
                        for g in range(2):
                            dve.tensor_copy(kcD[64 * g:64 * g + 64, g, 0:15], D_(name)[64 * g:64 * g + 64, 15 * g:15 * g + 15])
                        for g in range(2):
                            for h in range(4):
                                ins = dve.tensor_copy(vcD[32 * h:32 * h + 32, g, 64 * h:64 * h + 64],
                                                      D_(name)[32 * h:32 * h + 32, 64 + 64 * g:128 + 64 * g])
                        leave(ins, name)
                    elif name == "cS":
                        filled(eng, name)
                        leave(dve.tensor_tensor(cS, D_(name)[:, 0:256], cB, ALU.add), name)
                        kept(eng, name)
                        s3 = cS.rearrange("p (i n) -> p i n", n=CMPW)
                        own(dve.tensor_reduce(cst[:, 0, :], s3, AX_X, ALU.max))
                        dve.tensor_tensor(s3, s3, bc(cst[:, 0, :], CMPW), ALU.subtract).then_inc(c_vec, 1)
                        eng.wait_ge(c_act, 2)
                        own(dve.tensor_tensor(cS, cS, cM, ALU.mult))
                        own(dve.tensor_reduce(cst[:, 0, :], s3, AX_X, ALU.add))
                        own(dve.tensor_scalar(cst[:, 0, :], cst[:, 0, :], 1e-30, None, ALU.max))
                        own(dve.reciprocal(cst[:, 1, :], cst[:, 0, :]))
                        for q in range(TOK):
                            ins = dve.tensor_tensor(cst[:, 0, 8 * q:8 * q + 8].rearrange("p (j g) -> p j g", g=2),
                                                    cst[:, 1, 8 * q:8 * q + 8].rearrange("p (j g) -> p j g", g=2),
                                                    gates[:, q, 0:8].rearrange("p (g j) -> p j g", g=2), ALU.mult)
                        own(ins)
                        own(dve.tensor_tensor(s3, s3, bc(cst[:, 0, :], CMPW), ALU.mult))
                        eng.wait_ge(zeroed, 2)
                        s5 = cS.rearrange("p (q j g n) -> p q j g n", q=2, j=4, g=2)
                        for q in range(TOK):
                            for g in range(2):
                                ins = dve.tensor_copy(cP[:, 2 * q + g, :, 0:CMPW], s5[:, q, :, g, :])
                        ins.then_inc(c_vec, 1)
                    elif name in ("cO0", "cO1"):
                        q = int(name[2])
                        filled(eng, name)
                        eng.wait_ge(outs, 8)
                        leave(dve.tensor_tensor(oa[:, q, :], oa[:, q, :], D_(name)[:, :], ALU.add), name)
                    elif name[:2] == "wa":
                        t, h = int(name[2]), int(name[3])
                        filled(eng, name)
                        kept(eng, f"gA{t}{h}")
                        leave(dve.scalar_tensor_tensor(mrow[:, t, 512 * h:512 * h + 512], eg[:, t, 512 * h:512 * h + 512], 1.0,
                                                       D_(name)[:, :], ALU.add, ALU.mult), name)
                    elif name[:2] == "wb":
                        t, h = int(name[2]), int(name[3])
                        filled(eng, name)
                        kept(eng, f"gB{t}{h}")
                        e = eg[:, t, 512 * h:512 * h + 512]
                        leave(dve.scalar_tensor_tensor(e, e, 1.0, D_(name)[:, :], ALU.add, ALU.mult), name)
                        kept(eng, name)
                        m = mrow[:, t, 512 * h:512 * h + 512]
                        dve.tensor_tensor(m, m, e, ALU.add).then_inc(m_ready, 1)
                    elif name[:4] == "modT":
                        r = int(name[4])
                        filled(eng, name)
                        src = D_(name)[:, :].rearrange("p (b j v) -> p v j b", b=4, j=4)
                        for v in range(2):
                            ins = dve.tensor_copy(mc[:, v, 16 * r:16 * r + 16].rearrange("p (j b) -> p j b", j=4), src[:, v, :, :])
                        leave(ins, name)
                        kept(eng, name)
                        for v in range(2):
                            m = mc[:, v, 16 * r:16 * r + 16]
                            ins = dve.tensor_tensor(m, m, bmod[:, 16 * r:16 * r + 16], ALU.add)
                        own(ins)
                        if r == 0:
                            for v in range(2):
                                ins = dve.scalar_tensor_tensor(scl[:, v, :], mc[:, v, 8:16], 1.0, nat, ALU.add, ALU.mult)
                            own(ins)
                        if r == 2:
                            own(dve.scalar_tensor_tensor(scl[:, 2, :], mc[:, 0, 32:40], 1.0, nff, ALU.add, ALU.mult))
                    elif name in ("cxT00", "cxT10"):
                        turned_mod(name, hcT, mc[:, 1, 0:8], scl[:, 1, :])
                    elif name == "cc1":
                        mean_root(6, 2, KVR, 4)
                        for t in range(TOK):
                            ins = dve.tensor_scalar(pc[:, t, 256:512], pc[:, t, 256:512], rs[:, 6 + t:7 + t], None, ALU.mult)
                        ins.then_inc(lat_ready, 1)
                    elif name == "clT":
                        filled(eng, name)
                        for c in range(2):
                            ins = dve.tensor_scalar(lcT[:, c, :], D_(name)[:, c * S:(c + 1) * S], kvn[:, c:c + 1], None, ALU.mult)
                        leave(ins, name)
                        for t in range(TOK):
                            ins = dve.tensor_copy(kcat[:, t, :, NOPE:QK], over(pc[:, t, 512:544], HB))
                        ins.then_inc(cat_ready, 1)
                    elif name[:2] == "wo" and name[3] == "1":
                        t = int(name[2])
                        block1_norm(t)
                        normalise(t, 8, 6 + 2 * t)
                    elif name[:2] in ("bG", "bF"):
                        h = int(name[2])
                        filled(eng, name)
                        dst = (gG if name[1] == "G" else gF)[:, 512 * h:512 * h + 512]
                        eng.wait_ge(bg_in if name[1] == "G" else bf_in, 16)
                        leave(dve.tensor_tensor(dst, D_(name)[:, :], dst, ALU.add), name)
                    elif name in ("hT00", "hT10"):
                        turned_mod(name, uT, mc[:, 0, 0:8], scl[:, 0, :])
                    elif name in ("xa02", "xa12"):
                        late_x(int(name[2]))
                    elif name == "kwT":
                        filled(eng, name)
                        eng.wait_ge(kp_zeroed, 1)
                        leave(spread_keys(name, D_(name)[:, :], kP), name)
                        dve.tensor_copy(xv.rearrange("p (t d) -> p t d", t=TOK), px[:, :, VA:VA + P])
                    elif name[:2] in ("lq", "lk"):
                        filled(eng, name)
                        t = int(name[2])
                        dst, w, n_ = (lqT, qn, 3) if name[1] == "q" else (lkT, kvn, 2)
                        leave(dve.tensor_tensor(dst[:, :, t * P:(t + 1) * P],
                                                D_(name)[:, 0:n_ * P].rearrange("p (c s) -> p c s", c=n_), bc(w, P),
                                                ALU.mult), name)
                    elif name in ("qu01", "qu11"):
                        rope_q(int(name[2]))
                    elif name[:2] in ("qm", "kx", "kc") and int(name[2]) % 2 == 1:
                        filled(eng, name)
                        leave(dve.tensor_copy(mla_turned(name), D_(name)[0:QK, :].rearrange("p (h s) -> p h s", h=2)),
                              name)

            def unit_mask2(u):
                q = u % 2
                eng.wait_ge(u_scores, u + 1)
                if u == 0:
                    eng.wait_ge(wmask_in, 16)
                if u < 16:
                    if u >= 3:
                        eng.wait_ge(u_turn, u - 2)
                    h = u // 2 % 2 * 4 + u // 4
                    dve.tensor_tensor_reduce(sp3[:, u % 3, :], SB[u % 2][:, :], wB[:, q, :], 1.0, -3e38, ALU.add, ALU.max,
                                             mx2[:, u:u + 1]).then_inc(u_masked, 1)
                    eng.wait_ge(u_masked, u + 1)
                    dve.tensor_scalar(nm2[:, u:u + 1], mx2[:, u:u + 1], sink[:, h:h + 1], -1.0, ALU.max, ALU.mult)\
                       .then_inc(u_neg, 1)
                else:
                    own(dve.tensor_reduce(mx2[:, u:u + 1], SB[u % 2][:, :], AX_X, ALU.max))
                    dve.tensor_scalar(nm2[:, u:u + 1], mx2[:, u:u + 1], -MLA_SCALE, None, ALU.mult).then_inc(u_neg, 1)

            def unit_out2(u):
                q = u % 2
                eng.wait_ge(u_pv, u + 1)
                if u < 16:
                    eng.wait_ge(u_sink, u + 1)
                    own(dve.tensor_tensor(sm2[:, u:u + 1], sm2[:, u:u + 1], sk2[:, u:u + 1], ALU.add))
                    col = HD * (u // 2 % 2 * 4 + u // 4)
                else:
                    col = 512 + HD * ((u - 16) // 2)
                own(dve.reciprocal(rc2[:, u:u + 1], sm2[:, u:u + 1]))
                dve.tensor_scalar(o2[:, q, col:col + HD], OB[u % 2][:, 0:HD], rc2[:, u:u + 1], None, ALU.mult)\
                   .then_inc(u_out, 1)

            for r in range(34):
                if r < 32:
                    unit_mask2(r)
                if 1 <= r <= 32 and (r - 1) % 2 == 1:
                    u = r - 1
                    eng.wait_ge(u_turn, u + 1)
                    if u >= 2:
                        eng.wait_ge(u_pv, u - 1)
                    dve.tensor_copy(pt2[:, 1, :], TB[1][:, :]).then_inc(u_turned_v, 1)
                if r >= 2:
                    unit_out2(r - 2)

            def chosen(src, g):
                for i in range(4):
                    c = 4 + i
                    ins = dve.tensor_scalar(xsT[:, c, g * P:(g + 1) * P], src[:, i * P:(i + 1) * P], scl[:, 2, c:c + 1],
                                            mc[:, 0, 24 + c:25 + c], ALU.mult, ALU.add)
                return ins

            for name in TAIL:
                if name[:2] == "ou":
                    t, h = int(name[2]), int(name[3])
                    filled(eng, name)
                    r = rn[:, t, 512 * h:512 * h + 512]
                    x = xn[:, t, 512 * h:512 * h + 512]
                    leave(dve.tensor_tensor(r, D_(name)[:, :], gG[:, 512 * h:512 * h + 512], ALU.mult), name)
                    kept(eng, name)
                    ins = dve.tensor_tensor(x, x, r, ALU.add)
                    if h == 1:
                        ins.then_inc(x2_ready, 1)
                        normalise(t, 14, 13 + t)
                elif name in ("rT00", "rT10"):
                    turned_mod(name, uT, mc[:, 0, 24:32], scl[:, 2, :])
                elif name == "lg0":
                    filled(eng, name)
                    leave(dve.tensor_copy(aff[:, 0, :], D_(name)[:, 0:E]), name)
                elif name == "lg1":
                    filled(eng, name)
                    leave(dve.tensor_copy(aff[:, 1, :], D_(name)[:, 0:E]), name)
                    kept(eng, name)
                    own(dve.tensor_reduce(rst[:, 0:2], aff, AX_X, ALU.max))
                    dve.tensor_tensor(aff, aff, bc(rst[:, 0:2], E), ALU.subtract).then_inc(logit_max, 1)
                    eng.wait_ge(logit_exp, 1)
                    own(dve.tensor_reduce(rst[:, 2:4], aff, AX_X, ALU.add))
                    own(dve.reciprocal(rst[:, 4:6], rst[:, 2:4]))
                    dve.tensor_tensor(aff, aff, bc(rst[:, 4:6], E), ALU.mult).then_inc(aff_ready, 1)
                elif name == "afT":
                    filled(eng, name)
                    leave(dve.tensor_copy(affT[0:E], D_(name)[0:E, 0:S]), name)
                    own(dve.memset(zer[0:E], 0.0))
                    kept(eng, name)
                    cur = affT
                    for i in range(CAP // 8):
                        own(dve.max(top8[0:E], cur[0:E]))
                        nxt = work if cur is affT else affT
                        own(dve.match_replace(nxt[0:E], top8[0:E], cur[0:E], -1.0))
                        cur = nxt
                    own(dve.tensor_scalar(msk[0:E], cur[0:E], 0.0, None, ALU.is_lt))
                    own(dve.tensor_tensor_scan(cum[0:E], msk[0:E], zer[0:E], 0.0, ALU.add, ALU.add))
                    dve.tensor_tensor(cum[0:E], cum[0:E], msk[0:E], ALU.mult).then_inc(slots_ready, 1)
                elif name == "slT":
                    filled(eng, name)
                    leave(dve.tensor_copy(slt, D_(name)[:, 0:2 * E].rearrange("p (t e) -> p t e", t=TOK)), name)
                    kept(eng, name)
                    for lo, n_ in ((0, EG), (EG, E - EG)):
                        for t in range(TOK):
                            ins = dve.tensor_tensor(oh[:, t, lo * CAP:(lo + n_) * CAP].rearrange("p (e s) -> p e s", e=n_),
                                                    bc(slt[:, t, lo:lo + n_], CAP), over(iota, n_), ALU.is_equal)
                        ins.then_inc(oh_ready, 1)
                elif name == "gx1":
                    filled(eng, name)
                    leave(chosen(D_(name), 0), name)
                    eng.wait_ge(oh_ready, 2)
                    for t in range(TOK):
                        ins = dve.tensor_tensor(ohv[:, t, :].rearrange("p (e s) -> p e s", e=E),
                                                oh[:, t, :].rearrange("p (e s) -> p e s", e=E), bc(aff[:, t, :], CAP), ALU.mult)
                    ins.then_inc(oh_ready, 1)

            for g in range(NG):
                eng.wait_ge(e_tanh, g + 1)
                own(dve.scalar_tensor_tensor(hA, hE, 1.0, bank[0][:, :], ALU.add, ALU.mult))
                experts_done(eng, "U", g)
                dve.tensor_tensor(hA, hA, bank[1][:, :], ALU.mult).then_inc(e_h, 1)
                if g == 0:
                    eng.wait_ge(side_turn, 1)
                    dve.tensor_copy(ohT[:, 2:4, :], bank[3][:, :].rearrange("p (g s) -> p g s", g=2)).then_inc(side_v, 1)
                if g < NG - 1:
                    eng.wait_ge(side_turn, g + 2)
                    chosen(bank[3], g + 1).then_inc(side_v, 1)
                experts_done(eng, "D", g)
                if g:
                    eng.wait_ge(e_out, g)
                dve.tensor_copy(yE[:, 512:1024], bank[3][:, :]).then_inc(e_y2, 1)

            for t in range(TOK):
                eng.wait_ge(e_out, NG + t)
                for h in range(2):
                    r = rn[:, t, 512 * h:512 * h + 512]
                    own(dve.tensor_tensor(r, bank[4 + 2 * t + h][:, :], gF[:, 512 * h:512 * h + 512], ALU.mult))
                dve.tensor_tensor(xn[:, t, :], xn[:, t, :], rn[:, t, :], ALU.add).then_inc(f_in, 1)
            eng.wait_ge(fin_in, 16)
            for t in range(TOK):
                mean_root(t, 1, D, 15 + t)
                dve.scalar_tensor_tensor(xn[:, t, :], xn[:, t, :], rs[:, t:t + 1], nfin, ALU.mult, ALU.mult)\
                   .then_inc(y_ready, 1)


def shape_tables():
    q = np.arange(S)
    dist = (q[:, None] - q[None, :]).astype(np.float32)
    slopes = alibi(16)
    far = np.where(dist < 0, np.float32(FAR), dist)

    def table(sl):
        out = np.zeros((P, 8, CAUSAL), np.float32)
        for h in range(8):
            b = -np.float32(sl[h]) * far
            out[:, h, 0:P] = b[0:P, 0:P]
            out[:, h, P:CAUSAL] = b[P:S, :]
        return out.reshape(P, -1)

    end = np.arange(N_CMP) * 16 + 31
    cd = (q[:, None] - end[None, :]).astype(np.float32)
    bias = np.full((P, 2, 4, 2, CMPW), -FAR, np.float32)
    mask = np.zeros((P, 2, 4, 2, CMPW), np.float32)
    for t in range(2):
        for j in range(4):
            for g in range(2):
                d = cd[t * P:(t + 1) * P]
                bias[:, t, j, g, :N_CMP] = np.where(d >= 0, -np.float32(slopes[0::2][4 * g + j]) * d, -FAR)
                mask[:, t, j, g, :N_CMP] = d >= 0
    win = np.zeros((P, 2, 512), np.float32)
    for t in range(2):
        win[:, t, S:] = np.where(np.abs(dist[t * P:(t + 1) * P]) <= 128, 0.0, -FAR)

    def rotary(n):
        inv = 10000.0 ** (-np.arange(n, dtype=np.float32) / n)
        pos = np.stack([q // 64, q % 64], 1).astype(np.float32)
        ang = (pos[:, :, None] * inv[None, None, :]).astype(np.float32)
        c, s = np.cos(ang), np.sin(ang)
        cos = np.concatenate([c, c], 2).reshape(S, 4 * n)
        sin = np.concatenate([-s, s], 2).reshape(S, 4 * n)
        return [np.concatenate([m[0:P], m[P:S]], 1) for m in (cos, sin)]

    rope = np.concatenate(rotary(16) + rotary(8), 1).astype(np.float32)
    return {
        "ident": np.eye(P, dtype=np.float32), "nsa_table": table(slopes[0::2]), "moba_table": table(slopes[1::2]),
        "cmp_bias": bias.reshape(P, -1), "cmp_mask": mask.reshape(P, -1), "window_mask": win.reshape(P, -1),
        "rope": rope, "iota": np.tile(np.arange(1, CAP + 1, dtype=np.float32), (P, 1)),
    }


def chunks(w):
    return w.reshape(-1, P, w.shape[1]).transpose(1, 0, 2)


def stream_of(a):
    w = a["w_in"][0]
    pair = np.concatenate([np.arange(64) + 64 * h for j in range(4) for h in (j, 4 + j)])
    kv = lambda i: w[:, 512 + 128 * i:640 + 128 * i]
    parts = {"W0": w[:, pair], "W1": np.concatenate([kv(0), kv(1), kv(2), kv(4)], 1),
             "W2": np.concatenate([kv(3), kv(5), w[:, 1280:1304]], 1),
             "W6": w[:, 1304:1816], "W3": w[:, 1816:2328], "W4": w[:, 2328:2840], "W5": w[:, 2840:3352],
             "W7": w[:, 3352:3864]}
    for i in range(4):
        parts[f"W{8 + i}"] = w[:, 3864 + 512 * i:4376 + 512 * i]
    w2 = a["w_in_2"][0]
    ckv, kr = w2[:, 1152:1408], w2[:, 1408:1440]
    parts |= {"C0": w2[:, 512:768], "C1": np.concatenate([ckv, kr], 1), "X0": w2[:, pair],
              "X1": np.concatenate([w2[:, 512:768], ckv], 1), "X2": np.concatenate([w2[:, 768:1152], kr], 1),
              "WA": a["w_branch_a"][0], "WB": a["w_branch_b"][0], "QU": a["w_q_up_2"][0],
              "KU0": a["w_kv_up_2"][0], "KU1": a["w_kv_up_2"][0]}
    for i in range(2):
        parts[f"WO{i}"] = a["w_o"][0][:, 512 * i:512 * i + 512]
        parts[f"OUT{i}"] = a["w_out_2"][0][:, 512 * i:512 * i + 512]
    flat = {n: chunks(p).reshape(P, -1) for n, p in parts.items()}
    flat["W2"] = np.pad(chunks(parts["W2"]), ((0, 0), (0, 0), (0, 512 - WIDTH["W2"]))).reshape(P, -1)
    for n in ("WA", "WB"):
        flat[n] = chunks(parts[n]).reshape(P, 4, 2, 512).transpose(0, 2, 1, 3).reshape(P, -1)
    flat["WC"] = np.concatenate([chunks(a[f"cmp_w1_{k}"][0].reshape(-1, P)).reshape(P, -1) for k in "kv"], 1)
    wm = chunks(a["w_mod_2"][0])
    for n in range(12):
        flat[f"M{n}"] = wm[:, 2 * (n % 4):2 * (n % 4) + 2, 2048 * (n // 4):2048 * (n // 4) + 2048].reshape(P, -1)
    out = np.zeros((len(STREAM), P, SLOT), np.float32)
    for g in range(NG):
        for m, src in (("G", "w_gate_2"), ("U", "w_up_2"), ("D", "w_down_2")):
            e = a[src][0][EG * g:EG * g + EG]
            e = e.reshape(EG, -1, P, e.shape[2]).transpose(2, 0, 1, 3)
            for i in range(4):
                flat[f"{m}{g}.{i}"] = (e[:, :, 2 * i:2 * i + 2] if m != "D" else e[:, :, i]).reshape(P, -1)
    for n, name in enumerate(STREAM):
        out[n, :, :flat[name].shape[1]] = flat[name]
    return out


def host_arrays(a):
    col = lambda v: np.ascontiguousarray(v.reshape(-1, P).T)
    pe = np.concatenate([a[f"cmp_pe_{k}_"].reshape(LP, P).T for k in "kv"], 1)
    cond = np.stack([col(a["c_2"]), col(a["c_ctx_2"])], 2).reshape(P, -1)
    return {
        "stream": stream_of(a), "x": a["x"][0], "ctx": a["ctx_2"][0],
        "norm_pre": col(a["norm_pre"][0]), "norm_post": a["norm_post"], "norm_attn": col(a["norm_attn_2"][0]),
        "norm_ffn": col(a["norm_ffn_2"][0]), "norm_final": a["norm_final_2"].reshape(1, D),
        "b_mod": a["b_mod_2"], "b_mod_cols": col(a["b_mod_2"][0]), "q_norm": col(a["q_norm_2"][0]),
        "kv_norm": col(a["kv_norm_2"][0]), "sink": a["sink_2"], "cond": cond, "pe": pe,
        "w2k": np.concatenate([a["cmp_w2_k"][0]] * 2, 1), "w2v": a["cmp_w2_v"][0],
        "w_router": chunks(a["w_router_2"][0]).reshape(P, -1), **shape_tables(),
    }


def kernel(**inputs):
    import concourse.bacc as bacc
    from concourse.bass_utils import run_bass_kernel_spmd

    a = {k: np.asarray(v) for k, v in inputs.items()}
    a |= {f"cmp_pe_{k}_": a[f"cmp_pe_{k}"][0] for k in "kv"}
    nc = bacc.Bacc("TRN2", target_bir_lowering=False, num_devices=1)
    arrays, args = {}, {}
    for name, v in host_arrays(a).items():
        v = np.ascontiguousarray(v)
        arrays[f"in_{name}"] = v
        args[name] = nc.dram_tensor(f"in_{name}", v.shape, mybir.dt.from_np(v.dtype), kind="ExternalInput").ap()
    y = nc.dram_tensor("out_y", (S, D), F32, kind="ExternalOutput").ap()
    build(nc, args, y)
    got = run_bass_kernel_spmd(nc, [arrays], core_ids=[0])
    return got.results[0]["out_y"].reshape(1, S, D)
```

```python
from contextlib import ExitStack

import numpy as np

import concourse.bass as bass
from concourse import mybir

F32 = mybir.dt.float32
F32R = mybir.dt.float32r
ALU = mybir.AluOpType
ACT = mybir.ActivationFunctionType
AX_X = mybir.AxisListType.X

P = 128
S = 256
TOK = S // P
D = 1024
KC = D // P
HD = 64
EPS = 1e-6
FAR = 1e30
SLOT = 4096
SBUF_START = 16512
SBUF_END = 229344

N_CMP = 15
CMPW = 16
LP = 16
CAUSAL = P + S

XP = 1440
KA, VA, CKV, CQ, KR = 512, 640, 768, 1024, 1408
CP = 544
QR, KVR = 384, 256
HB, NOPE, ROPE, QK = 8, 64, 32, 96
MLA_SCALE = float(QK) ** -0.5
E = 16
CAP = 32
EG = 4
NG = E // EG

STREAM = (["W0", "W1", "W2", "W3", "W4", "M0", "WC", "W5", "M1", "W6", "M2", "W7", "M3", "W8", "M4", "W9", "M5",
           "WA", "M6", "W10", "M7", "W11", "M8", "WB", "M9", "C0", "M10", "WO0", "M11", "WO1", "C1", "KU0",
           "X2", "X1", "X0", "QU", "KU1", "OUT0", "OUT1"]
          + [f"{m}{g}.{i}" for g in range(NG) for m in ("G", "U", "D") for i in range(4)])
N_DENSE = STREAM.index("G0.0")
BUFFERS = 9
SECOND = STREAM.index("WA")
LATE = {"KU0": 0, "X2": 1, "X1": 0, "X0": 1, "QU": 0, "KU1": 1, "OUT0": 2, "OUT1": 3}
EXPERT_CYCLE = [0, 1, 4, 5, 6, 7, 2, 3, 8]


def buffer_of(n):
    if n >= N_DENSE:
        return EXPERT_CYCLE[(n - N_DENSE) % len(EXPERT_CYCLE)]
    return n % 2 if n < SECOND else LATE.get(STREAM[n], (1, 4, 0)[(n - SECOND) % 3])


BUFFER = [buffer_of(n) for n in range(len(STREAM))]
TURN = [BUFFER[:n + 1].count(BUFFER[n]) for n in range(len(STREAM))]

SPLIT = [n for n in STREAM if n in ("WA", "WB", "WO0", "WO1") or n[0] in "WX" and n[1:].isdigit()]
WIDTH = {"W2": 280, "X2": 416}

SPLIT_AFTER = {"hT01": "X2", "modT2": "X2", "bF1": "X2", "hT10": "X2"}

DENSE = ["xT00", "xT01", "xT10", "xT11", "qa0", "qa1", "kvc", "kvs", "va0", "va1", "qb0", "qb1",
         "kb0", "cH", "kb1", "cT", "vb0", "cK", "vb1", "cS", "za0", "za1", "cP", "zb0", "zb1",
         "cO0", "cO1", "gA00", "gA10", "yaT0", "gA01", "yaT1", "gA11", "modT0", "wa00", "ybT0",
         "wa10", "ybT1", "wa01", "wa11", "gB00", "gB10", "cxT00", "cxT01", "cxT10", "cxT11",
         "gB01", "gB11", "wb00", "ck0", "wb10", "ck1", "wb01", "wb11", "mT00", "mT10", "mT01",
         "mT11", "modT1", "wo00", "cc0", "cc1", "wo10", "clT", "wo01", "wo11", "ckv00", "ckv01",
         "ckv10", "hT00", "hT01", "ckv11", "bG0", "bG1", "modT2", "bF1", "bF0", "hT10", "hT11",
         "kc0", "kc1", "kc3", "xa02", "kc2", "xa12", "xa01", "xa11", "xa00", "lq0", "lq1",
         "xa10", "lk0", "lk1", "qu00", "qu01", "xkv00", "xkv01", "qwT0", "qu10", "qwT1", "kwT",
         "qu11", "xkv10", "xkv11", "qm0", "qm1", "qm2", "qm3", "kx0", "kx1", "kx2", "kx3"]
TAIL = ["ou00", "ou01", "ou10", "rT00", "ou11", "rT01", "rT10", "lg0", "rT11", "lg1", "afT", "slT", "gx0", "gx1"]
GROUPS = DENSE + TAIL
BANK_OF = {name: n % 2 for n, name in enumerate(GROUPS)}
assert BANK_OF["gx0"] == 0 and BANK_OF["gx1"] == 1
USE_OF = {name: n // 2 + 1 for n, name in enumerate(GROUPS)}

MOD_AFTER = {"qb1": 0, "cT": 1, "za0": 2, "za1": 3, "cO1": 4, "gA11": 5, "wa10": 6, "wa11": 7,
             "gB10": 8, "gB11": 9, "ck1": 10, "wb11": 11}

LAST_USE = {"W0": "qa1", "W1": "kvs", "W2": "va1", "W3": "qb1", "W4": "kb1", "W5": "vb1", "W6": "za1", "W7": "zb1",
            "W8": "gA10", "W9": "gA11", "W10": "gB10", "W11": "gB11", "WA": "wa11", "WB": "wb11", "WC": "cH",
            "C0": "ck1", "C1": "cc1", "KU0": "ckv11", "WO0": "wo10", "WO1": "wo11", "X2": "xa12", "X1": "xa11",
            "X0": "xa10", "QU": "qu11", "KU1": "xkv11", "OUT0": "ou10", "OUT1": "ou11"}

NSA, WIN, MOBA = range(3)
UNITS = [(NSA, j) for j in range(4)] + [(WIN, j) for j in range(4)] + [(MOBA, j) for j in range(4)]
ROUND_AFTER = {name: r for r, name in enumerate(
    ["qb0", "qb1", "kb0", "kb1", "vb0", "vb1", "za0", "za1", "zb0", "zb1", "gA00", "gA10", "gA01", "gA11"])}


def schedule():
    out = []
    for name in DENSE:
        for k in range(1, len(SPLIT)):
            if LAST_USE[SPLIT[k - 1]] == name and SPLIT[k] not in SPLIT_AFTER.values():
                out += [("split", (k, q)) for q in range(4)]
        out.append(("dense", name))
        if name in ("xT10", "xT11"):
            out += [("split", (0, q)) for q in range(4) if (q == 0) == (name == "xT10")]
        if name in SPLIT_AFTER:
            k = SPLIT.index(SPLIT_AFTER[name])
            out.append(("split", (k, sum(i == ("split", (k, q)) for i in out for q in range(4)))))
        if name in MOD_AFTER:
            out.append(("mod", MOD_AFTER[name]))
        if name in ROUND_AFTER:
            r = ROUND_AFTER[name]
            if r < len(UNITS):
                out.append(("score", r))
            if 0 <= r - 1 < len(UNITS):
                out.append(("turn", r - 1))
            if 0 <= r - 2:
                out.append(("pv", r - 2))
        if name == "cO1":
            out.append(("ya", 0))
        if name == "gA11":
            out.append(("yb", 0))
        if name == "wa11":
            out.append(("context", 0))
    return out


SCHEDULE = schedule()


def alibi(n):
    return [float(np.float32(2.0 ** (-8.0 * k / n))) for k in range(1, n + 1)]


def build(nc, A, out):
    ctx = ExitStack()
    with ctx:
        def sem(name):
            return ctx.enter_context(nc.semaphore(name))

        placed = {}

        def sb(name, cols):
            start = max((a + 4 * n for a, n in placed.values()), default=SBUF_START)
            assert start + 4 * cols <= SBUF_END
            placed[name] = (start, cols)
            return nc.alloc_sbuf_tensor_at(name, [P, cols], F32, offset=start)

        def parts_at(name, where, start, cols):
            return nc.alloc_sbuf_tensor_at(name, [P, cols], F32R, offset=placed[where][0] + 4 * start)

        ring = sb("ring", 2 * SLOT)
        parts = sb("parts", 2 * SLOT)
        x_sb = sb("x_sb", TOK * D)
        tz = sb("tz", 4096)
        turned = tz[:, 0:2048]
        zz = tz[:, 2048:4096]
        rows = sb("rows", TOK * D)
        tabs = sb("tabs", 4096)
        mo = sb("mo", 4096)
        qk = sb("qk", 5120)
        vvc = sb("vvc", 6656)
        vv = vvc[:, 0:1536]
        vc = vvc[:, 1536:6656]
        sp = sb("sp", 1536)
        pt = sb("pt", 1536)
        lat = sb("lat", 2176)
        ident = sb("ident", P)
        modr = sb("modr", 1536)
        rope = lat[:, 1792:2176]
        small = sb("small", 1400)

        used = {}

        def view(tensor, start, cols, pattern=None, **sizes):
            v = tensor[:, start:start + cols]
            return v.rearrange(pattern, **sizes) if pattern else v

        def tiny(cols):
            a = used.get("small", 0)
            used["small"] = a + cols
            assert a + cols <= 1400
            return small[:, a:a + cols]

        def slot(name):
            b = BUFFER[STREAM.index(name)]
            if b < 2:
                return ring[:, b * SLOT:(b + 1) * SLOT]
            if b < 4:
                return parts[:, (b - 2) * SLOT:(b - 1) * SLOT]
            return {4: qk, 5: tabs, 6: mo, 7: vvc}[b][:, 0:SLOT]

        def slot_pieces(name):
            if BUFFER[STREAM.index(name)] < 8:
                return [slot(name)]
            return [zz, lat[:, 0:SLOT // 2]]

        def expert_weights(name, e):
            pieces = slot_pieces(name)
            n = EG // len(pieces)
            return pieces[e // n][:, e % n * 1024:e % n * 1024 + 1024]

        def arrived(eng, name):
            n = STREAM.index(name)
            eng.wait_ge(slot_in[BUFFER[n]], 16 * len(slot_pieces(name)) * TURN[n])

        weight_parts = parts_at("weight_parts", "parts", 0, 2 * SLOT)
        u_parts = parts_at("u_parts", "tz", 0, 2048)
        x_parts = parts_at("x_parts", "rows", 0, 2048)
        ml_parts = parts_at("ml_parts", "tabs", 2048, 2048)
        hl_parts = parts_at("hl_parts", "tz", 2048, 2048)
        ya_parts = parts_at("ya_parts", "lat", 0, 1024)
        yb_parts = parts_at("yb_parts", "tabs", 3072, 1024)
        yal_parts = parts_at("yal_parts", "tabs", 2048, 1024)
        ybl_parts = parts_at("ybl_parts", "qk", 4096, 1024)

        xn = x_sb[:, :].rearrange("p (t d) -> p t d", t=TOK)
        rn = rows[:, :].rearrange("p (t d) -> p t d", t=TOK)
        uT = turned[:, :].rearrange("p (c s) -> p c s", c=KC)
        uhigh, xlow, mlow, hlow = (t_[:, :].rearrange("p (c s) -> p c s", c=KC)
                                   for t_ in (u_parts, x_parts, ml_parts, hl_parts))
        yaT, ybT, yalow, yblow = (t_[:, :].rearrange("p (c s) -> p c s", c=4)
                                  for t_ in (ya_parts, yb_parts, yal_parts, ybl_parts))
        xrow = view(mo, 0, 2048, "p (t d) -> p t d", t=TOK)
        mrow = view(tabs, 0, 2048, "p (t d) -> p t d", t=TOK)
        table = view(tabs, 0, 8 * CAUSAL, "p (h k) -> p h k", h=8)
        eg = view(mo, 0, 2048, "p (t d) -> p t d", t=TOK)
        oa = view(mo, 2048, 1024, "p (t d) -> p t d", t=TOK)
        ob = view(mo, 3072, 1024, "p (t d) -> p t d", t=TOK)
        qaT = view(qk, 0, 1024, "p (j s) -> p j s", j=4)
        ksD = view(qk, 1024, 512, "p (g s) -> p g s", g=2)
        kwD = view(qk, 1536, 512, "p (g s) -> p g s", g=2)
        qbT = view(qk, 2048, 1024, "p (j s) -> p j s", j=4)
        kbD = view(qk, 3072, 2048, "p (j g s) -> p j g s", j=4, g=2)
        za = view(zz, 0, 1024, "p (t d) -> p t d", t=TOK)
        zb = view(zz, 1024, 1024, "p (t d) -> p t d", t=TOK)
        vSW = view(vv, 0, 512, "p (t i d) -> p t i d", t=TOK, i=2)
        vS, vW = vSW[:, :, 0, :], vSW[:, :, 1, :]
        vB = view(vv, 512, 1024, "p (t d) -> p t d", t=TOK)
        kvT = view(vc, 0, 512, "p (i s) -> p i s", i=2)
        kv2 = view(vc, 512, 1024, "p (i g s) -> p i g s", i=2, g=2)
        blk = view(vc, 1536, 1024, "p (i l n) -> p i l n", i=2, l=LP)
        cW = view(vc, 2560, P)
        cE = view(vc, 2752, 60, "p (i n) -> p i n", i=2)
        cH = view(vc, 2880, 60, "p (i n) -> p i n", i=2)
        hkT = view(vc, 3008, 30)
        hvR = view(vc, 3072, 256, "p (g h n) -> p g h n", g=2, h=4)
        w2k = view(vc, 3328, 128)
        w2v = view(vc, 3456, 64)
        kcD = view(vc, 3520, 32, "p (g n) -> p g n", g=2)
        vcD = view(vc, 3552, 512, "p (g d) -> p g d", g=2)
        cB = view(vc, 4064, 256)
        cM = view(vc, 4320, 256)
        cS = view(vc, 4576, 256)
        cP = view(vc, 512, 512, "p (i h n) -> p i h n", i=4, h=4)
        cPT = view(vc, 1024, 512, "p (i q) -> p i q", i=4)
        pe = view(vc, 4832, 32, "p (i l) -> p i l", i=2)
        spn = sp[:, :].rearrange("p (u b k) -> p u b k", u=2, b=2)
        ptn = pt[:, :].rearrange("p (u b k) -> p u b k", u=2, b=2)
        post = view(vc, 2048, 1024)

        hcT = zz[:, :].rearrange("p (c s) -> p c s", c=KC)
        hfull = hcT
        cn = view(vc, 0, 2048, "p (t d) -> p t d", t=TOK)
        px = view(mo, 0, TOK * XP, "p (t d) -> p t d", t=TOK)
        pc = view(mo, TOK * XP, TOK * CP, "p (t d) -> p t d", t=TOK)
        kcat = view(qk, 0, 3072, "p (t h d) -> p t h d", t=2 * TOK, h=HB)
        qcat = view(qk, 3072, 1536, "p (t h d) -> p t h d", t=TOK, h=HB)
        kP = view(vv, 0, 1024, "p (g s) -> p g s", g=2)
        rt = view(sp, 0, 1280, "p (i d) -> p i d", i=2)
        gG = view(vc, 3072, 1024)
        gF = view(vc, 4096, 1024)
        vm = view(vc, 0, 2048, "p (t h d) -> p t h d", t=2 * TOK, h=HB)
        qwT = view(pt, 0, 1024, "p (j s) -> p j s", j=4)
        xv = view(vv, 1024, 256)
        lqT = view(lat, 0, 768, "p (c s) -> p c s", c=3)
        lkT = view(lat, 768, 512, "p (c s) -> p c s", c=2)
        lcT = view(lat, 1280, 512, "p (c s) -> p c s", c=2)
        qmT = turned[:, :].rearrange("p (h s) -> p h s", h=HB)
        kmT = tabs[:, :].rearrange("p (h s) -> p h s", h=HB)
        wB = view(modr, 0, 1024, "p (t k) -> p t k", t=TOK)
        oT = zz[:, :].rearrange("p (c s) -> p c s", c=KC)
        sp3 = sp[:, :].rearrange("p (u k) -> p u k", u=3)
        pT = [view(where, 0, 2048, "p (b i q) -> p b i q", b=2, i=4) for where in (mo, rows)]
        mod = modr[:, :].rearrange("p (r n) -> p r n", r=3)
        bias = [view(tabs, 3072, 512), view(vc, 3072, 512), view(vc, 3584, 512)]
        pick = view(lat, 0, 512, "p (j q) -> p j q", j=4)

        nfin = gG
        xs = view(tz, 0, 2048, "p (g c s) -> p g c s", g=2, c=KC)
        oh = view(modr, 0, 1024, "p (t s) -> p t s", t=TOK)
        ohv = view(pt, 0, 1024, "p (t s) -> p t s", t=TOK)
        ohT = view(qk, 4096, 1024, "p (g s) -> p g s", g=NG)
        hE = view(sp, 0, 512)
        hA = view(sp, 512, 512)
        hT = view(sp, 1024, 512)
        yE = view(pt, 0, 1024)

        gcol = tiny(KC)
        nat = tiny(KC)
        nff = tiny(KC)
        modc = tiny(96)
        mc = modc.rearrange("p (v q) -> p v q", v=2)
        qn = tiny(3)
        kvn = tiny(2)
        sink = tiny(8)
        iota = tiny(CAP)
        wr = tiny(KC * E).rearrange("p (c e) -> p c e", c=KC)
        cc = tiny(2 * KC)
        ccE = tiny(2 * KC)
        csil = tiny(KC * 32).rearrange("p (c v) -> p c v", c=KC)
        gates = tiny(48).rearrange("p (t i) -> p t i", t=TOK)
        ss = tiny(16)
        rs = tiny(16)
        half = tiny(4)
        mx = tiny(8).rearrange("p (u i) -> p u i", u=2)
        nm = tiny(8).rearrange("p (u i) -> p u i", u=2)
        sums = tiny(48).rearrange("p (u i) -> p u i", u=12)
        rc = tiny(48).rearrange("p (u i) -> p u i", u=12)
        cst = tiny(48).rearrange("p (i n) -> p i n", i=3)
        mx2 = tiny(32)
        nm2 = tiny(32)
        sm2 = tiny(32)
        sk2 = tiny(32)
        rc2 = tiny(32)
        scl = tiny(4 * KC).rearrange("p (i c) -> p i c", i=4)
        aff = tiny(32).rearrange("p (t e) -> p t e", t=TOK)
        slt = tiny(32).rearrange("p (t e) -> p t e", t=TOK)
        rst = tiny(8)
        affT = view(pt, 1024, 256)
        work = view(pt, 1280, 256)
        top8 = tiny(8)
        msk = view(sp, 0, 256)
        cum = view(sp, 256, 256)
        zer = view(sp, 512, 256)

        bank = [ctx.enter_context(nc.psum_tensor(f"bank{i}", [P, 512], F32)) for i in range(8)]
        DB = bank[0:2]
        MB = bank[2]
        SB = bank[3:5]
        TB = bank[5:7]
        VB = bank[7]
        OB = (VB, MB)

        slot_in = [sem(f"slot_in{i}") for i in range(BUFFERS)]
        last_in = sem("last_in")
        mod_used = sem("mod_used")
        e_used = sem("e_used")
        d_ready = [sem(f"d_ready{i}") for i in range(2)]
        d_free = [sem(f"d_free{i}") for i in range(2)]
        x_in = [sem(f"x_in{t}") for t in range(TOK)]
        early_in = sem("early_in")
        const_in = sem("const_in")
        nsa_table_in = sem("nsa_table_in")
        moba_table_in = [sem(f"moba_table_in{i}") for i in range(2)]
        ctx_in = sem("ctx_in")
        post_in = sem("post_in")
        wmask_in = sem("wmask_in")
        bias_in = [sem(f"bias_in{i}") for i in range(2)]
        fin_in = sem("fin_in")
        out_done = sem("out_done")
        kv2_in = sem("kv2_in")
        zeroed = sem("zeroed")
        picked = sem("picked")
        kp_zeroed = sem("kp_zeroed")
        split_a = sem("split_a")
        split_v = sem("split_v")
        part_used = sem("part_used")
        high_ready = sem("high_ready")
        h_ready = sem("h_ready")
        squares = sem("squares")
        means = sem("means")
        roots = sem("roots")
        normed = sem("normed")
        tanhs = sem("tanhs")
        cond_tanh = sem("cond_tanh")
        cond_ready = sem("cond_ready")
        mod_kept = sem("mod_kept")
        scores = sem("scores")
        masked = sem("masked")
        maxed = sem("maxed")
        exps = sem("exps")
        turns = sem("turns")
        turned_a = sem("turned_a")
        turned_b = sem("turned_b")
        pvs = sem("pvs")
        outs = sem("outs")
        blocks_ready = sem("blocks_ready")
        c_act = sem("c_act")
        c_vec = sem("c_vec")
        ya_ready = sem("ya_ready")
        yb_ready = sem("yb_ready")
        m_ready = sem("m_ready")
        x1_ready = sem("x1_ready")
        roped = sem("roped")
        lat_ready = sem("lat_ready")
        cat_ready = sem("cat_ready")
        u_scores = sem("u_scores")
        u_masked = sem("u_masked")
        u_neg = sem("u_neg")
        u_exp = sem("u_exp")
        u_turn = sem("u_turn")
        u_turned_a = sem("u_turned_a")
        u_turned_v = sem("u_turned_v")
        u_pv = sem("u_pv")
        u_out = sem("u_out")
        u_sink = sem("u_sink")
        u_summed = sem("u_summed")
        u_norm = sem("u_norm")
        x2_ready = sem("x2_ready")
        logit_max = sem("logit_max")
        aff_ready = sem("aff_ready")
        slots_ready = sem("slots_ready")
        oh_ready = sem("oh_ready")
        side_turn = sem("side_turn")
        side_a = sem("side_a")
        side_v = sem("side_v")
        e_tanh = sem("e_tanh")
        e_h = sem("e_h")
        e_turn = sem("e_turn")
        e_hT = sem("e_hT")
        e_first = sem("e_first")
        e_y = sem("e_y")
        e_y2 = sem("e_y2")
        e_out = sem("e_out")
        f_in = sem("f_in")
        y_ready = sem("y_ready")
        dve_step = sem("dve_step")
        act_step = sem("act_step")
        pool_step = sem("pool_step")

        def D_(name):
            return DB[BANK_OF[name]]

        def filled(eng, name):
            eng.wait_ge(d_ready[BANK_OF[name]], USE_OF[name])

        def kept(eng, name):
            eng.wait_ge(d_free[BANK_OF[name]], USE_OF[name])

        def branch_weights(name):
            return name in ("WA", "WB")

        def quarter_released(eng, k, q):
            name = SPLIT[k]
            base = sum(2 if branch_weights(n) else 3 for n in SPLIT[:k])
            if q == 3:
                filled(eng, LAST_USE[name])
            elif branch_weights(name):
                if q == 1:
                    filled(eng, LAST_USE[name][:3] + "0")
                else:
                    eng.wait_ge(part_used, base + 1 + q // 2)
            else:
                eng.wait_ge(part_used, base + q + 1)

        def quarter(tensor, name, q):
            return tensor[:, 1024 * q:1024 * q + 1024].rearrange("p (c n) -> p c n", c=2)[:, :, 0:WIDTH.get(name, 512)]

        def released(eng, name):
            if name in SPLIT:
                eng.wait_ge(split_v, 4 * SPLIT.index(name) + 4)
            elif name in LAST_USE:
                filled(eng, LAST_USE[name])
            elif name[0] == "M":
                eng.wait_ge(mod_used, int(name[1:]) + 1)
            else:
                group, part = name[1:].split(".")
                eng.wait_ge(e_used, 12 * int(group) + 4 * "GUD".index(name[0]) + int(part) + 1)

        def experts_done(eng, stage, g):
            released(eng, f"{stage}{g}.3")

        def leave(ins, name):
            ins.then_inc(d_free[BANK_OF[name]], 1)

        def bc(t, n):
            return t.rearrange("p (k n) -> p k n", n=1).to_broadcast([P, t.shape[1], n])

        def over(t, n):
            return t.rearrange("p (n k) -> p n k", n=1).to_broadcast([P, n, t.shape[1]])

        def mla_turned(name):
            i = 2 * int(name[2])
            return {"qm": qmT, "kx": kmT[:, :, S:2 * S], "kc": kmT[:, :, 0:S]}[name[:2]][0:QK, i:i + 2, :]

        def vector_turns(u):
            return u < 16 and u % 2 == 1

        def turned_out(eng, u):
            by_vector = sum(vector_turns(i) for i in range(u + 1))
            if vector_turns(u):
                eng.wait_ge(u_turned_v, by_vector)
            else:
                eng.wait_ge(u_turned_a, u + 1 - by_vector)

        def unit_turned(eng, u, copy):
            eng.wait_ge(u_turn, u + 1)
            if u >= 8:
                eng.wait_ge(u_pv, u // 4 - 1)
            q = u % 2
            return copy(pT[u // 4 % 2][:, u // 2 % 2, :, q * P:(q + 1) * P],
                        TB[u % 2][:, :].rearrange("p (i q) -> p i q", i=4))

        constants = ((w2k, "w2k"), (w2v, "w2v"), (cB, "cmp_bias"), (cM, "cmp_mask"), (view(vc, 4832, 32), "pe"),
                     (rope, "rope"), (nat, "norm_attn"), (nff, "norm_ffn"),
                     (qn, "q_norm"), (kvn, "kv_norm"), (iota, "iota"), (cc, "cond"),
                     (wr.rearrange("p c e -> p (c e)"), "w_router"))

        block = ctx.enter_context(nc.Block())

        @block.sync
        def _(eng):
            stream = A["stream"]
            for t in range(TOK):
                eng.dma_start(xn[:, t, :], A["x"][t * P:(t + 1) * P, :]).then_inc(x_in[t], 16)
            for n, name in enumerate(STREAM):
                b = BUFFER[n]
                before = [k for k in range(n) if BUFFER[k] == b]
                if n >= N_DENSE and b == 4 and before[-1] < N_DENSE:
                    filled(eng, "kx2")
                    filled(eng, "kx3")
                elif before:
                    released(eng, STREAM[before[-1]])
                elif b == 4:
                    eng.wait_ge(scores, len(UNITS))
                elif b in (2, 3):
                    filled(eng, LAST_USE[SPLIT[-1]])
                elif b == 5:
                    eng.wait_ge(u_scores, 32)
                elif b == 8:
                    filled(eng, "ou11")
                elif b >= 6:
                    eng.wait_ge(u_pv, 8)
                pieces = slot_pieces(name)
                for i, piece in enumerate(pieces):
                    w = SLOT // len(pieces)
                    if name != STREAM[-1]:
                        eng.dma_start(piece, stream[n, :, i * w:(i + 1) * w]).then_inc(slot_in[b], 16)
                if name == STREAM[-1]:
                    both = [t_.rearrange("p (e h n) -> p e h n", e=EG, h=2) for t_ in (slot(name), stream[n, :, :])]
                    for h in range(2):
                        eng.dma_start(both[0][:, :, h], both[1][:, :, h]).then_inc((slot_in[b], last_in)[h], 16)
                if name == "W2":
                    eng.dma_start(tabs[:, 0:8 * CAUSAL], A["nsa_table"]).then_inc(nsa_table_in, 16)
                    eng.dma_start(tabs[:, 3072:3584], A["mod_bias"][:, 0:512]).then_inc(bias_in[0], 16)
                if name == "W9":
                    kept(eng, "cO1")
                    eng.dma_start(cn, A["ctx"].rearrange("(t p) d -> p t d", p=P)).then_inc(ctx_in, 16)
                    eng.dma_start(post, A["norm_post"].to_broadcast([P, D])).then_inc(post_in, 16)
                    eng.dma_start(gG, A["mod_bias"][:, 512:1536]).then_inc(bias_in[1], 16)
            for t in range(TOK):
                eng.wait_ge(y_ready, t + 1)
                eng.dma_start(out[t * P:(t + 1) * P, :], xn[:, t, :]).then_inc(out_done, 16)
            eng.wait_ge(out_done, 16 * TOK)

        @block.scalar
        def _(eng):
            act = nc.scalar
            steps = [0]

            def own(ins):
                steps[0] += 1
                ins.then_inc(act_step, 1)
                eng.wait_ge(act_step, steps[0])

            eng.dma_start(ident[:, :], A["ident"]).then_inc(early_in, 16)
            eng.dma_start(gcol, A["norm_pre"]).then_inc(early_in, 16)

            def copy(dst, src, name=None, scale=1.0):
                ins = act.activation(dst, src, ACT.Copy, scale=scale)
                if name:
                    leave(ins, name)
                return ins

            n_sq = [0]

            def sum_squares(src, k, junk):
                if n_sq[0]:
                    eng.wait_ge(squares, n_sq[0])
                act.activation(junk, src, ACT.Square, accum_out=ss[:, k:k + 1]).then_inc(squares, 1)
                n_sq[0] += 1

            for t in range(TOK):
                eng.wait_ge(x_in[t], 16)
                sum_squares(xn[:, t, :], t, pt[:, 0:D])

            def load_constants():
                for dst, name in constants:
                    eng.dma_start(dst, A[name]).then_inc(const_in, 16)
                eng.dma_start(sink, A["sink"].to_broadcast([P, 8])).then_inc(const_in, 16)

            def turned_mod(name, dst, add, mult):
                filled(eng, name)
                t = int(name[-2])
                for c in range(4):
                    k = 4 + c
                    ins = act.activation(dst[:, k, t * P:(t + 1) * P], D_(name)[:, c * P:(c + 1) * P], ACT.Identity,
                                         bias=add[:, k:k + 1], scale=mult[:, k:k + 1])
                leave(ins, name)

            for kind, n in SCHEDULE:
                if kind == "split":
                    n, q = n
                    name = SPLIT[n]
                    if q == 0:
                        arrived(eng, name)
                    if n:
                        quarter_released(eng, n - 1, q)
                    copy(quarter(weight_parts, name, q), quarter(slot(name), name, q)).then_inc(split_a, 1)
                elif kind == "score":
                    u = n
                    eng.wait_ge(maxed, u + 1)
                    for b in range(2):
                        for q in range(TOK):
                            k = spn[:, u % 2, b, P * q:P + S * q]
                            ins = act.activation(k, k, ACT.Exp, bias=nm[:, u % 2, 2 * b + q:2 * b + q + 1],
                                                 accum_out=sums[:, u, 2 * b + q:2 * b + q + 1])
                    ins.then_inc(exps, 1)
                elif kind == "turn":
                    u = n
                    eng.wait_ge(turns, u + 1)
                    if u >= 2:
                        eng.wait_ge(pvs, u - 1)
                    copy(ptn[:, u % 2, 0, :], TB[0][:, 0:CAUSAL]).then_inc(turned_a, 1)
                elif kind == "dense":
                    name = n
                    if name in ("xT01", "xT11"):
                        if name == "xT01":
                            eng.wait_ge(early_in, 32)
                        filled(eng, name)
                        t = int(name[2])
                        for c in range(4):
                            ins = act.activation(uhigh[:, 4 + c, t * P:(t + 1) * P], D_(name)[:, c * P:(c + 1) * P], ACT.Copy,
                                                 scale=gcol[:, 4 + c:5 + c])
                        ins.then_inc(high_ready, 1)
                    elif name in ("qa0", "qa1", "qb0", "qb1"):
                        if name == "qa0":
                            load_constants()
                        filled(eng, name)
                        i = int(name[2])
                        dst = qaT if name[1] == "a" else qbT
                        copy(dst[:, 2 * i:2 * i + 2, :], D_(name)[:, :].rearrange("p (j s) -> p j s", j=2), name, HD ** -0.5)
                    elif name in ("vb0", "vb1"):
                        filled(eng, name)
                        copy(vB[:, int(name[2]), :], D_(name)[:, :], name)
                    elif name in ("va0", "va1"):
                        filled(eng, name)
                        t = int(name[2])
                        copy(vv[:, S * t:S * t + S], D_(name)[:, 0:S])
                        leave(act.activation(gates[:, t, :], D_(name)[:, S:S + 24], ACT.Tanh, scale=0.5), name)
                        if t == 1:
                            eng.wait_ge(const_in, 16 * (len(constants) + 1))
                            act.activation(ccE, cc, ACT.Tanh, scale=0.5).then_inc(cond_tanh, 1)
                    elif name == "kvs":
                        kept(eng, "kvc")
                        for g in range(2):
                            src = kvT[64 * g:64 * g + 64, :, :]
                            eng.dma_start(kv2[0:64, :, g, :], src).then_inc(kv2_in, 16)
                            eng.dma_start(kv2[64:128, :, g, 0:S - 1], src[:, :, 1:S]).then_inc(kv2_in, 16)
                    elif name in ("za0", "za1", "zb0", "zb1"):
                        filled(eng, name)
                        dst = za if name[1] == "a" else zb
                        act.activation(dst[:, int(name[2]), :], D_(name)[:, :], ACT.Tanh, scale=0.5)\
                           .then_inc(tanhs, 1)
                    elif name[:2] in ("gA", "gB"):
                        filled(eng, name)
                        t, h = int(name[2]), int(name[3])
                        if name[:2] == "gB":
                            kept(eng, f"wa{t}{h}")
                        leave(act.activation(eg[:, t, 512 * h:512 * h + 512], D_(name)[:, :], ACT.Tanh, scale=0.5), name)
                    elif name == "cH":
                        filled(eng, name)
                        copy(cW, D_(name)[:, 0:P], name)
                    elif name == "cT":
                        kept(eng, name)
                        act.activation(cE, cH, ACT.Tanh, scale=0.5).then_inc(c_act, 1)
                    elif name == "cS":
                        eng.wait_ge(c_vec, 2)
                        act.activation(cS, cS, ACT.Exp).then_inc(c_act, 1)
                    elif name == "cP":
                        filled(eng, name)
                        copy(cPT, D_(name)[:, :].rearrange("p (i q) -> p i q", i=4), name)
                    elif name[:3] in ("yaT", "ybT"):
                        filled(eng, name)
                        t = int(name[3])
                        copy((yaT if name[1] == "a" else ybT)[:, :, t * P:(t + 1) * P], D_(name)[:, :].rearrange("p (c s) -> p c s", c=4), None, 0.5)\
                            .then_inc(high_ready, 1)
                    elif name[:2] == "mT":
                        filled(eng, name)
                        t, h = int(name[2]), int(name[3])
                        copy(uhigh[:, 4 * h:4 * h + 4, t * P:(t + 1) * P],
                             D_(name)[:, :].rearrange("p (c s) -> p c s", c=4), None, 0.5).then_inc(high_ready, 1)
                    elif name in ("cxT01", "cxT11"):
                        turned_mod(name, hcT, mc[:, 1, 0:8], scl[:, 1, :])
                    elif name in ("hT01", "hT11"):
                        turned_mod(name, hfull, mc[:, 0, 0:8], scl[:, 0, :])
                        kept(eng, name)
                        t = int(name[2])
                        copy(uhigh[:, 4:8, t * P:(t + 1) * P], hfull[:, 4:8, t * P:(t + 1) * P]).then_inc(high_ready, 1)
                    elif name in ("ck0", "ck1"):
                        filled(eng, name)
                        copy(pc[:, int(name[2]), 0:256], D_(name)[:, 0:256], name)
                    elif name in ("cc0", "cc1"):
                        filled(eng, name)
                        t = int(name[2])
                        copy(pc[:, t, 256:544], D_(name)[:, 0:288], name)
                        kept(eng, name)
                        sum_squares(pc[:, t, 256:512], 6 + t, pt[:, 0:256])
                    elif name[:2] == "wo":
                        filled(eng, name)
                        t, h = int(name[2]), int(name[3])
                        copy(rn[:, t, 512 * h:512 * h + 512], D_(name)[:, :], name)
                        if h == 1:
                            kept(eng, f"wo{t}0")
                            kept(eng, name)
                            sum_squares(rn[:, t, :], 4 + t, sp[:, 0:D])
                            if t == 0:
                                eng.wait_ge(x1_ready, 1)
                                sum_squares(xn[:, 0, :], 8, sp[:, 0:D])
                    elif name[:2] in ("bG", "bF"):
                        filled(eng, name)
                        h = int(name[2])
                        copy((gG if name[1] == "G" else gF)[:, 512 * h:512 * h + 512], D_(name)[:, :], name)
                        if name == "bF1":
                            kept(eng, "modT2")
                            eng.dma_start(modr[:, 0:1024], A["window_mask"]).then_inc(wmask_in, 16)
                    elif name[:2] == "xa":
                        filled(eng, name)
                        t, h = int(name[2]), int(name[3])
                        w = 512 if h < 2 else 416
                        copy(px[:, t, 512 * h:512 * h + w], D_(name)[:, 0:w], name)
                        if h == 1:
                            kept(eng, name)
                            kept(eng, f"xa{t}2")
                            sum_squares(px[:, t, CQ:CQ + QR], 10 + 2 * t, pt[:, 1024:1024 + QR])
                            sum_squares(px[:, t, CKV:CKV + KVR], 11 + 2 * t, pt[:, 1024:1024 + KVR])
                    elif name in ("qwT0", "qwT1"):
                        filled(eng, name)
                        t = int(name[3])
                        copy(qwT[:, :, t * P:(t + 1) * P], D_(name)[:, :].rearrange("p (j s) -> p j s", j=4), name,
                             HD ** -0.5)
                    elif name[:2] == "qu":
                        filled(eng, name)
                        t, h = int(name[2]), int(name[3])
                        w = 480 if h == 0 else 288
                        copy(qcat[:, t, :, :].rearrange("p h d -> p (h d)")[:, 480 * h:480 * h + w], D_(name)[:, 0:w], name)
                    elif name[:3] in ("ckv", "xkv"):
                        filled(eng, name)
                        t, h = int(name[3]), int(name[4])
                        tk = t if name[0] == "c" else TOK + t
                        src = D_(name)[:, :].rearrange("p (h d) -> p h d", h=4)
                        copy(kcat[:, tk, 4 * h:4 * h + 4, 0:NOPE], src[:, :, 0:64])
                        leave(copy(vm[:, tk, 4 * h:4 * h + 4, :], src[:, :, 64:128]), name)
                        if name == "ckv11":
                            eng.wait_ge(x1_ready, 2)
                            sum_squares(xn[:, 1, :], 9, sp[:, 0:D])
                    elif name[:2] in ("qm", "kx", "kc") and int(name[2]) % 2 == 0:
                        filled(eng, name)
                        copy(mla_turned(name), D_(name)[0:QK, :].rearrange("p (h s) -> p h s", h=2), name)

            def soften(u):
                eng.wait_ge(u_neg, u + 1)
                if u < 16:
                    act.activation(sp3[:, u % 3, :], sp3[:, u % 3, :], ACT.Exp, bias=nm2[:, u:u + 1],
                                   accum_out=sm2[:, u:u + 1]).then_inc(u_exp, 1)
                    h = (u // 2) % 2 * 4 + u // 4
                    act.activation(sk2[:, u:u + 1], sink[:, h:h + 1], ACT.Exp, bias=nm2[:, u:u + 1]).then_inc(u_sink, 1)
                else:
                    eng.wait_ge(u_turn, u - 2)
                    act.activation(sp3[:, u % 3, :], SB[u % 2][:, :], ACT.Exp, bias=nm2[:, u:u + 1], scale=MLA_SCALE,
                                   accum_out=sm2[:, u:u + 1]).then_inc(u_exp, 1)

            for r in range(36):
                if r < 32:
                    soften(r)
                if 2 <= r < 34 and not vector_turns(r - 2):
                    unit_turned(eng, r - 2, copy).then_inc(u_turned_a, 1)
                if r % 4 == 2 and r >= 10 or r == 35:
                    p = 7 if r == 35 else (r - 10) // 4
                    eng.wait_ge(u_pv, p + 1)
                    copy(oT[:, p, :], OB[p % 2][:, 0:S]).then_inc(u_out, 1)

            def chosen(src, g):
                for c in range(4):
                    ins = act.activation(xs[:, g % 2, c, :], src[:, c * P:(c + 1) * P], ACT.Identity,
                                         bias=mc[:, 0, 24 + c:25 + c], scale=scl[:, 2, c:c + 1])
                return ins

            for name in TAIL:
                if name[:2] == "ou":
                    t, h = int(name[2]), int(name[3])
                    eng.wait_ge(x2_ready, 2 * t + h + 1)
                    sum_squares(xn[:, t, 512 * h:512 * h + 512], 14 + t if h else t, sp[:, 0:512])
                elif name in ("rT01", "rT11"):
                    turned_mod(name, uT, mc[:, 0, 24:32], scl[:, 2, :])
                    if name == "rT11":
                        eng.dma_start(nfin, A["norm_final"].to_broadcast([P, D])).then_inc(fin_in, 16)
                elif name in ("lg0", "lg1"):
                    t = int(name[2])
                    eng.wait_ge(logit_max, t + 1)
                    leave(act.activation(aff[:, t, :], D_(name)[:, 0:E], ACT.Exp, bias=rst[:, t:t + 1],
                                         accum_out=rst[:, 2 + t:3 + t]), name)
                elif name == "gx0":
                    filled(eng, name)
                    leave(chosen(D_(name), 0), name)

            for g in range(NG):
                experts_done(eng, "G", g)
                if g:
                    eng.wait_ge(e_h, g)
                act.activation(hE, bank[0][:, :], ACT.Tanh, scale=0.5).then_inc(e_tanh, 1)
                if g == 0:
                    eng.wait_ge(side_turn, 1)
                    copy(ohT[:, 0:2, :], bank[2][:, :].rearrange("p (g s) -> p g s", g=2)).then_inc(side_a, 1)
                if g < NG - 1:
                    eng.wait_ge(side_turn, g + 2)
                    chosen(bank[2], g + 1).then_inc(side_a, 1)
                eng.wait_ge(e_turn, g + 1)
                copy(hT, bank[0][:, :], scale=0.5).then_inc(e_hT, 1)
                eng.wait_ge(e_first, g + 1)
                if g:
                    eng.wait_ge(e_out, g)
                copy(yE[:, 0:512], bank[2][:, :]).then_inc(e_y, 1)
            for n, (h, t) in enumerate((h, t) for h in range(2) for t in range(TOK)):
                eng.wait_ge(f_in, n + 1)
                sum_squares(xn[:, t, 512 * h:512 * h + 512], 4 * h + t, sp[:, 0:512])

        @block.gpsimd
        def _(eng):
            pool = nc.gpsimd
            pool.memset(half[:, 2:3], -0.5)
            pool.memset(qk[:, 1024:2048], 0.0)
            pool.memset(qk[:, 3072:5120], 0.0)
            pool.memset(csil, 0.0)
            pool.memset(view(vc, 1536, 1024), 0.0)
            pool.memset(view(vc, 3072, 256), 0.0)
            pool.memset(view(vc, 3520, 544), 0.0).then_inc(zeroed, 1)
            eng.wait_ge(zeroed, 1)
            for n, (k, w) in enumerate([(0, 1), (1, 1), (2, 2), (6, 2), (4, 1), (8, 1), (5, 1), (9, 1), (10, 2), (12, 2),
                                        (14, 1), (15, 1), (4, 1), (5, 1)]):
                eng.wait_ge(means, n + 1)
                pool.tensor_tensor(rs[:, k:k + w], ss[:, k:k + w], half[:, 2:3].to_broadcast([P, w]), ALU.pow)\
                    .then_inc(roots, 1)
                if n == 1:
                    eng.wait_ge(blocks_ready, 2)
                    pool.memset(view(vc, 512, 512), 0.0).then_inc(zeroed, 1)
                    both = [t_.rearrange("p (a b) -> p a b", a=4) for t_ in (tabs[:, 0:8 * CAUSAL], A["moba_table"])]
                    for i in range(2):
                        eng.wait_ge(masked, 6 + 2 * i)
                        eng.dma_start(both[0][:, i::2], both[1][:, i::2]).then_inc(moba_table_in[i], 16)
                if n == 3:
                    kept(eng, "wb11")
                    pool.memset(lat[:, 0:512], 0.0).then_inc(pool_step, 1)
                    eng.wait_ge(pool_step, 1)
                    for j in range(4):
                        pool.memset(pick[32 * j:32 * j + 1, j, :], 1.0).then_inc(picked, 1)
                        eng.wait_ge(picked, j + 1)
                    pool.memset(vv[:, 0:1024], 0.0).then_inc(kp_zeroed, 1)

        @block.tensor
        def _(eng):
            pe_ = nc.tensor

            def begin(name):
                if USE_OF[name] >= 2:
                    eng.wait_ge(d_free[BANK_OF[name]], USE_OF[name] - 1)
                return D_(name)

            def turn(dst, src, n=P, m=P):
                return pe_.transpose(dst, src, ident[0:n, 0:n])

            def turn_tiles(name, src, cols=P):
                o = begin(name)
                for c in range(4):
                    ins = turn(o[:, c * P:(c + 1) * P], src[:, c * P:(c + 1) * P])
                ins.then_inc(d_ready[BANK_OF[name]], 1)

            def product(o, lhs, rhs, chunks):
                for c in range(chunks):
                    ins = pe_.matmul(o, lhs(c), rhs(c), start=(c == 0), stop=(c == chunks - 1))
                return ins

            def parts_product(name, outs_, lhs, rhs, chunks, quarter=0, last=False):
                k = SPLIT.index(name)
                for i, o in enumerate(outs_):
                    for c in range(chunks):
                        if not last and i == 0 and c % 2 == 0:
                            eng.wait_ge(split_v, 4 * k + quarter + c // 2 + 1)
                        for n, (a, b) in enumerate(((0, 0), (0, 1), (1, 0))):
                            ins = pe_.matmul(o, lhs(a, c, i), rhs(b, c, i), start=(c == 0 and n == 0),
                                             stop=(c == chunks - 1 and n == 2))
                        if last and i == len(outs_) - 1 and c % 2 == 1 and c < chunks - 1:
                            ins.then_inc(part_used, 1)
                return ins

            split_weights = [weight_parts[:, a * SLOT:a * SLOT + SLOT].rearrange("p (c n) -> p c n", c=KC) for a in range(2)]

            def turned_products(name, sl, col, last):
                w, u = split_weights, (uhigh, xlow)
                return parts_product(sl, [D_(name)[:, 0:S], D_(name)[:, S:2 * S]],
                                     lambda a, c, i: w[a][:, c, col + P * i:col + P * i + P], lambda b, c, i: u[b][:, c, :],
                                     KC, 0, last)

            def split_rows(name, sl, t, low, last, width=512):
                w, u = split_weights, (uhigh, low)
                return parts_product(sl, [D_(name)[:, 0:width]], lambda a, c, i: u[a][:, c, t * P:(t + 1) * P],
                                     lambda b, c, i: w[b][:, c, 0:width], KC, 0, last)

            def rows_product(name, w, col, width, t, src, dst=0, chunks=KC):
                return product(D_(name)[:, dst:dst + width], lambda c: src[:, c, t * P:(t + 1) * P],
                               lambda c: w[:, c, col:col + width], chunks)

            def weights(name, chunks, width):
                return slot(name)[:, 0:chunks * width].rearrange("p (c n) -> p c n", c=chunks)

            def done(ins, name):
                ins.then_inc(d_ready[BANK_OF[name]], 1)

            def dense(name):
                if name[:2] == "xT":
                    t, h = int(name[2]), int(name[3])
                    if name == "xT00":
                        eng.wait_ge(early_in, 32)
                    eng.wait_ge(normed, t + 1)
                    turn_tiles(name, xrow[:, t, 512 * h:512 * h + 512])
                elif name in ("qa0", "qa1", "qb0", "qb1", "kb0", "kb1"):
                    i = int(name[2])
                    if name == "qa0":
                        for x in ("xT00", "xT01", "xT10", "xT11"):
                            kept(eng, x)
                    begin(name)
                    done(turned_products(name, {"qa": "W0", "qb": "W3", "kb": "W4"}[name[:2]], 256 * i, i == 1), name)
                elif name in ("kvc", "kvs"):
                    begin(name)
                    i = int(name == "kvs")
                    done(turned_products(name, "W1", 256 * i, i == 1), name)
                elif name[:2] in ("va", "vb", "za", "zb", "gA", "gB"):
                    t = int(name[2])
                    sl = {"va": "W2", "vb": "W5", "za": "W6", "zb": "W7", "gA": "W8", "gB": "W10"}[name[:2]]
                    if name[:2] in ("gA", "gB") and name[3] == "1":
                        sl = {"gA": "W9", "gB": "W11"}[name[:2]]
                    begin(name)
                    done(split_rows(name, sl, t, xlow, t == 1, WIDTH.get(sl, 512)), name)
                elif name == "cH":
                    arrived(eng, "WC")
                    eng.wait_ge(blocks_ready, 2)
                    begin(name)
                    w = slot("WC").rearrange("p (i l e) -> p i l e", i=2, l=LP)
                    for c in range(LP // 2):
                        for i in range(2):
                            for half_ in range(2):
                                a, l = 32 * (2 * i + half_), LP // 2 * half_ + c
                                ins = pe_.matmul(D_(name)[a:a + 32, 0:P], blk[:, i, l, :], w[:, i, l, :], start=(c == 0),
                                                 stop=(c == LP // 2 - 1), tile_position=(0, a))
                    done(ins, name)
                elif name == "cT":
                    kept(eng, "cH")
                    begin(name)
                    done(turn(D_(name)[:, 0:P], cW), name)
                elif name == "cK":
                    eng.wait_ge(c_vec, 1)
                    begin(name)
                    pe_.matmul(D_(name)[:, 0:30], w2k, hkT, start=True, stop=True)
                    for g in range(2):
                        ins = pe_.matmul(D_(name)[:, 64 + 64 * g:128 + 64 * g],
                                         hvR[:, g, :, :].rearrange("p h n -> p (h n)"), w2v, start=True, stop=True)
                    done(ins, name)
                elif name == "cS":
                    kept(eng, "cK")
                    begin(name)
                    for q in range(TOK):
                        for j in range(4):
                            a = (q * 4 + j) * 32
                            ins = pe_.matmul(D_(name)[:, a:a + 32], qaT[:, j, q * P:(q + 1) * P],
                                             kcD.rearrange("p g n -> p (g n)"), start=True, stop=True)
                    done(ins, name)
                elif name == "cP":
                    eng.wait_ge(c_vec, 3)
                    begin(name)
                    for i in range(4):
                        ins = turn(D_(name)[:, i * P:(i + 1) * P], cP[:, i, :, :].rearrange("p h n -> p (h n)"))
                    done(ins, name)
                elif name in ("cO0", "cO1"):
                    kept(eng, "cP")
                    q = int(name[2])
                    begin(name)
                    for g in range(2):
                        ins = pe_.matmul(D_(name)[:, 256 * g:256 * g + 256], cPT[:, 2 * q + g, :], vcD[:, g, :],
                                         start=True, stop=True)
                    done(ins, name)
                elif name[:3] in ("yaT", "ybT"):
                    eng.wait_ge(ya_ready if name[1] == "a" else yb_ready, 1)
                    turn_tiles(name, (oa if name[1] == "a" else ob)[:, int(name[3]), :])
                elif name[:2] in ("wa", "wb"):
                    t, h = int(name[2]), int(name[3])
                    if (t, h) == (0, 0):
                        for i in range(2):
                            kept(eng, f"y{name[1]}T{i}")
                    begin(name)
                    w = [w_[:, 4 * h:4 * h + 4, :] for w_ in split_weights]
                    y = (yaT, yalow) if name[1] == "a" else (ybT, yblow)
                    done(parts_product("WA" if name[1] == "a" else "WB", [D_(name)[:, :]],
                                       lambda a, c, i: y[a][:, c, t * P:(t + 1) * P], lambda b, c, i: w[b][:, c, :],
                                       4, 2 * h, t == 1), name)
                elif name[:2] == "mT":
                    t, h = int(name[2]), int(name[3])
                    eng.wait_ge(m_ready, 2 * h + t + 1)
                    turn_tiles(name, mrow[:, t, 512 * h:512 * h + 512])
                elif name[:4] == "modT":
                    r = int(name[4])
                    eng.wait_ge(mod_kept, r + 1)
                    turn_tiles(name, mod[:, r, :])
                elif name[:3] == "cxT":
                    t, h = int(name[3]), int(name[4])
                    eng.wait_ge(normed, 3 + t)
                    turn_tiles(name, cn[:, t, 512 * h:512 * h + 512])
                elif name in ("ck0", "ck1", "cc0", "cc1"):
                    t = int(name[2])
                    if t == 0:
                        arrived(eng, "C0" if name[1] == "k" else "C1")
                        for x in ("cxT00", "cxT01", "cxT10", "cxT11"):
                            kept(eng, x)
                    begin(name)
                    width = 256 if name[1] == "k" else 288
                    w = weights("C0" if name[1] == "k" else "C1", KC, width)
                    done(rows_product(name, w, 0, width, t, hcT), name)
                elif name == "clT":
                    eng.wait_ge(lat_ready, 1)
                    begin(name)
                    for c in range(2):
                        for t in range(TOK):
                            ins = turn(D_(name)[:, c * S + t * P:c * S + (t + 1) * P], pc[:, t, 256 + c * P:256 + (c + 1) * P])
                    done(ins, name)
                elif name[:3] in ("ckv", "xkv"):
                    t, h = int(name[3]), int(name[4])
                    sl = "KU0" if name[0] == "c" else "KU1"
                    if (t, h) == (0, 0):
                        arrived(eng, sl)
                        if name[0] == "c":
                            kept(eng, "clT")
                    if h == 0 and name[0] == "x":
                        kept(eng, f"lk{t}")
                    begin(name)
                    done(rows_product(name, weights(sl, 2, D), 512 * h, 512, t, lcT if name[0] == "c" else lkT, 0, 2),
                         name)
                elif name[:2] == "wo":
                    t, h = int(name[2]), int(name[3])
                    if h == 0:
                        for i in range(2):
                            kept(eng, f"mT{t}{i}")
                    begin(name)
                    done(split_rows(name, f"WO{h}", t, mlow, t == 1), name)
                elif name[:2] in ("bG", "bF"):
                    h = int(name[2])
                    eng.wait_ge(picked, 4)
                    begin(name)
                    r, j = (1, h) if name[1] == "G" else (2, 2 + h)
                    done(pe_.matmul(D_(name)[:, :], pick[:, j, :], mod[:, r, :], start=True, stop=True), name)
                elif name[:2] == "hT":
                    t, h = int(name[2]), int(name[3])
                    eng.wait_ge(normed, 5 + t)
                    turn_tiles(name, rn[:, t, 512 * h:512 * h + 512])
                elif name[:2] == "xa":
                    t, h = int(name[2]), int(name[3])
                    if h == 2:
                        eng.wait_ge(h_ready, 2 * t + 2)
                    begin(name)
                    sl = f"X{h}"
                    done(split_rows(name, sl, t, hlow, t == 1, WIDTH.get(sl, 512)), name)
                elif name in ("qwT0", "qwT1"):
                    t = int(name[3])
                    eng.wait_ge(roped, t + 1)
                    turn_tiles(name, px[:, t, 0:512])
                elif name == "kwT":
                    begin(name)
                    for i in range(4):
                        src = pc[:, i, 0:P] if i < 2 else px[:, i - 2, KA:KA + P]
                        ins = turn(D_(name)[:, i * P:(i + 1) * P], src)
                    done(ins, name)
                elif name[:2] in ("lq", "lk"):
                    t = int(name[2])
                    eng.wait_ge(lat_ready, t + 2)
                    begin(name)
                    base, n = (CQ, 3) if name[1] == "q" else (CKV, 2)
                    for c in range(n):
                        ins = turn(D_(name)[:, c * P:(c + 1) * P], px[:, t, base + c * P:base + (c + 1) * P])
                    done(ins, name)
                elif name[:2] == "qu":
                    t, h = int(name[2]), int(name[3])
                    if (t, h) == (0, 0):
                        arrived(eng, "QU")
                    if h == 0:
                        kept(eng, f"lq{t}")
                    begin(name)
                    width = 480 if h == 0 else 288
                    done(rows_product(name, weights("QU", 3, 768), 480 * h, width, t, lqT, 0, 3), name)
                elif name[:2] in ("qm", "kx", "kc"):
                    i = int(name[2])
                    if name == "qm0":
                        eng.wait_ge(cat_ready, 3)
                    if name == "kx0":
                        kept(eng, "xkv10")
                        kept(eng, "xkv11")
                    if name == "kc0":
                        kept(eng, "ckv10")
                        kept(eng, "ckv11")
                        eng.wait_ge(cat_ready, 1)
                    src, t0 = {"qm": (qcat, 0), "kx": (kcat, TOK), "kc": (kcat, 0)}[name[:2]]
                    begin(name)
                    for b in range(2):
                        for t in range(TOK):
                            ins = turn(D_(name)[0:QK, b * S + t * P:b * S + (t + 1) * P], src[:, t0 + t, 2 * i + b, :])
                    done(ins, name)

            def mod_slot(n):
                arrived(eng, f"M{n}")
                if n == 0:
                    eng.wait_ge(cond_ready, 1)
                if n % 4 == 0 and n:
                    eng.wait_ge(mod_kept, n // 4)
                w = slot(f"M{n}").rearrange("p (k n) -> p k n", k=2)
                for k in range(2):
                    for j in range(4):
                        c = n % 4 * 2 + k
                        ins = pe_.matmul(MB[32 * j:32 * j + 32, :], csil[:, c, :], w[:, k, 512 * j:512 * j + 512],
                                         start=(c == 0), stop=(c == KC - 1), tile_position=(0, 32 * j))
                ins.then_inc(mod_used, 1)

            def operands(u):
                kind, j = UNITS[u]
                q = qbT if kind == MOBA else qaT
                k = {NSA: ksD, WIN: kwD, MOBA: kbD[:, j, :, :]}[kind]
                return q[:, j, :], k

            for kind, n in SCHEDULE:
                if kind == "dense":
                    dense(n)
                elif kind == "mod":
                    mod_slot(n)
                elif kind == "score":
                    q, k = operands(n)
                    if n == 0:
                        kept(eng, "kvs")
                        kept(eng, "qa0")
                        kept(eng, "qa1")
                    if n == 8:
                        for x in ("qb0", "qb1", "kb0", "kb1"):
                            kept(eng, x)
                    if n:
                        eng.wait_ge(masked, n)
                    pe_.matmul(SB[0][:, :], q[:, P:S], k.rearrange("p g s -> p (g s)"), start=True, stop=True)
                    pe_.matmul(SB[1][:, 0:S].rearrange("p (g s) -> p g s", g=2), q[:, 0:P], k[:, :, 0:P],
                               start=True, stop=True).then_inc(scores, 1)
                elif kind == "turn":
                    u = n
                    eng.wait_ge(exps, u + 1)
                    if u:
                        eng.wait_ge(turned_a, u)
                        eng.wait_ge(turned_b, u)
                    for b in range(2):
                        for i in range(3):
                            ins = turn(TB[b][:, i * P:(i + 1) * P], spn[:, u % 2, b, i * P:(i + 1) * P])
                    ins.then_inc(turns, 1)
                elif kind == "pv":
                    u = n
                    typ, j = UNITS[u]
                    v = {NSA: vS, WIN: vW, MOBA: vB}[typ]
                    eng.wait_ge(turned_a, u + 1)
                    eng.wait_ge(turned_b, u + 1)
                    if u == 0:
                        kept(eng, "va0")
                        kept(eng, "va1")
                    if u == 8:
                        kept(eng, "vb0")
                        kept(eng, "vb1")
                    if u:
                        eng.wait_ge(outs, u)
                    for b in range(2):
                        c = HD * b if typ != MOBA else HD * (2 * j + b)
                        o = VB[:, 128 * b:128 * b + 128]
                        pr = ptn[:, u % 2, b, :]
                        pe_.matmul(o[:, 0:64], pr[:, 0:P], v[:, 0, c:c + HD], start=True, stop=True)
                        pe_.matmul(o[:, 64:128], pr[:, P:2 * P], v[:, 0, c:c + HD], start=True, stop=False)
                        ins = pe_.matmul(o[:, 64:128], pr[:, 2 * P:3 * P], v[:, 1, c:c + HD], start=False, stop=True)
                    ins.then_inc(pvs, 1)

            def unit_scores(u):
                q = u % 2
                if u == 0:
                    for x in ("qwT0", "qwT1", "kwT"):
                        kept(eng, x)
                if u == 16:
                    for x in ("qm2", "qm3", "kx2", "kx3"):
                        kept(eng, x)
                if u == 0:
                    eng.wait_ge(masked, len(UNITS))
                if u >= 2:
                    eng.wait_ge(u_masked, u - 1)
                    if u >= 18:
                        eng.wait_ge(u_exp, u - 1)
                o = SB[u % 2][:, :]
                if u < 16:
                    j, b = u // 4, u // 2 % 2
                    ins = pe_.matmul(o, qwT[:, j, q * P:(q + 1) * P], kP[:, b, :], start=True, stop=True)
                else:
                    h = (u - 16) // 2
                    ins = pe_.matmul(o, qmT[0:QK, h, q * P:(q + 1) * P], kmT[0:QK, h, :], start=True, stop=True)
                ins.then_inc(u_scores, 1)

            def unit_turn(u):
                eng.wait_ge(u_norm, u + 1)
                if u == 0:
                    eng.wait_ge(turned_a, len(UNITS))
                if u == 1:
                    eng.wait_ge(turned_b, len(UNITS))
                if u >= 2:
                    turned_out(eng, u - 2)
                for i in range(4):
                    ins = turn(TB[u % 2][:, i * P:(i + 1) * P], sp3[:, u % 3, i * P:(i + 1) * P])
                ins.then_inc(u_turn, 1)

            def pair_pv(p, tiles):
                if 0 in tiles:
                    turned_out(eng, 4 * p + 2)
                    turned_out(eng, 4 * p + 3)
                    if p >= 2:
                        eng.wait_ge(u_out, p - 1)
                    else:
                        eng.wait_ge(outs, len(UNITS))
                for i in tiles:
                    for b in range(2):
                        if p < 4:
                            v = (pc[:, i, P + HD * b:P + HD * (b + 1)] if i < 2 else
                                 xv[:, (i - 2) * P + HD * b:(i - 2) * P + HD * (b + 1)])
                        else:
                            v = vm[:, i, 2 * (p - 4) + b, :]
                        ins = pe_.matmul(OB[p % 2][HD * b:HD * b + HD, 0:S], v, pT[p % 2][:, b, i, :], start=(i == 0),
                                         stop=(i == 3), tile_position=(0, HD * b))
                if 3 in tiles:
                    ins.then_inc(u_pv, 1)

            def tail(name):
                if name == "ou00":
                    first_output(6, KC)
                elif name[:2] == "ou":
                    t, h = int(name[2]), int(name[3])
                    if t == 0:
                        arrived(eng, f"OUT{h}")
                    begin(name)
                    w = weights(f"OUT{h}", KC, 512)
                    done(product(D_(name)[:, :], lambda c: oT[:, c, t * P:(t + 1) * P],
                                 lambda c: w[:, c, :], KC), name)
                elif name[:2] == "rT":
                    t, h = int(name[2]), int(name[3])
                    eng.wait_ge(normed, 7 + 2 * t + h)
                    turn_tiles(name, rn[:, t, 512 * h:512 * h + 512])
                elif name in ("lg0", "lg1"):
                    t = int(name[2])
                    for h in range(2):
                        kept(eng, f"rT{t}{h}")
                    begin(name)
                    done(product(D_(name)[:, 0:E], lambda c: uT[:, c, t * P:(t + 1) * P], lambda c: wr[:, c, :], KC),
                         name)
                elif name == "afT":
                    eng.wait_ge(aff_ready, 2)
                    begin(name)
                    for t in range(TOK):
                        ins = turn(D_(name)[0:E, t * P:(t + 1) * P], aff[:, t, :])
                    done(ins, name)
                elif name == "slT":
                    eng.wait_ge(slots_ready, 1)
                    begin(name)
                    for t in range(TOK):
                        ins = turn(D_(name)[:, t * E:(t + 1) * E], cum[0:E, t * P:(t + 1) * P], E)
                    done(ins, name)
                elif name in ("gx0", "gx1"):
                    eng.wait_ge(oh_ready, 1)
                    begin(name)
                    done(gather(D_(name), 0, int(name[2])), name)

            def gather(o, g, half):
                for i in range(4):
                    c = 4 * half + i
                    for t in range(TOK):
                        ins = pe_.matmul(o[:, i * P:(i + 1) * P], rn[:, t, c * P:(c + 1) * P], oh[:, t, g * P:(g + 1) * P],
                                         start=(t == 0), stop=(t == TOK - 1))
                return ins

            def first_output(first, last):
                if first == 0:
                    arrived(eng, "OUT0")
                    begin("ou00")
                w = weights("OUT0", KC, 512)
                for c in range(first, last):
                    eng.wait_ge(u_out, c + 1)
                    ins = pe_.matmul(D_("ou00")[:, :], oT[:, c, 0:P], w[:, c, :], start=(c == 0), stop=(c == KC - 1))
                if last == KC:
                    done(ins, "ou00")

            for r in range(35):
                if r < 32:
                    unit_scores(r)
                if r == 32:
                    first_output(0, 2)
                if 2 <= r < 34:
                    unit_turn(r - 2)
                if r == 32:
                    first_output(2, 4)
                if r == 33:
                    first_output(4, 6)
                if 6 <= r < 34:
                    pair_pv((r - 6) // 4, [(r - 6) % 4])
                if r == 34:
                    pair_pv(7, range(4))

            for name in TAIL:
                tail(name)

            for g in range(NG):
                for m, b in (("G", 0), ("U", 1)):
                    if g == 0 and m == "G":
                        kept(eng, "gx0")
                    if g:
                        eng.wait_ge(e_hT if b == 0 else e_h, g)
                    for i in range(4):
                        if (g, m, i) == (0, "G", 2):
                            kept(eng, "gx1")
                        arrived(eng, f"{m}{g}.{i}")
                        w = [expert_weights(f"{m}{g}.{i}", e).rearrange("p (k n) -> p k n", k=2) for e in range(EG)]
                        for k in range(2):
                            c = 2 * i + k
                            for e in range(EG):
                                ins = pe_.matmul(bank[b][32 * e:32 * e + 32, :], xs[:, g % 2, c, e * CAP:(e + 1) * CAP], w[e][:, k, :],
                                                 start=(c == 0), stop=(c == KC - 1), tile_position=(0, 32 * e))
                        ins.then_inc(e_used, 1)
                if g:
                    eng.wait_ge(e_y, g)
                    eng.wait_ge(e_y2, g)
                if g == 0:
                    eng.wait_ge(oh_ready, 3)
                    for i in range(2):
                        for k in range(2):
                            for t in range(TOK):
                                a = (2 * i + k) * P
                                ins = turn(bank[2 + i][:, k * S + t * P:k * S + (t + 1) * P], ohv[:, t, a:a + P])
                    ins.then_inc(side_turn, 1)
                    eng.wait_ge(side_a, 1)
                    eng.wait_ge(side_v, 1)
                if g < NG - 1:
                    eng.wait_ge(oh_ready, 2)
                    for i in range(2):
                        ins = gather(bank[2 + i], g + 1, i)
                    ins.then_inc(side_turn, 1)
                eng.wait_ge(e_h, g + 1)
                for i in range(4):
                    ins = turn(bank[0][:, i * P:(i + 1) * P], hA[:, i * P:(i + 1) * P])
                ins.then_inc(e_turn, 1)
                eng.wait_ge(e_hT, g + 1)
                if g < NG - 1:
                    eng.wait_ge(side_a, g + 2)
                    eng.wait_ge(side_v, g + 2)
                for i in range(4):
                    arrived(eng, f"D{g}.{i}")
                    w = [expert_weights(f"D{g}.{i}", e) for e in range(EG)]
                    for h in range(2):
                        if h == 1 and f"D{g}.{i}" == STREAM[-1]:
                            eng.wait_ge(last_in, 16)
                        for e in range(EG):
                            ins = pe_.matmul(bank[2 + h][32 * e:32 * e + 32, :], hT[:, i * P + 32 * e:i * P + 32 * e + 32],
                                             w[e][:, 512 * h:512 * h + 512], start=(i == 0), stop=(i == 3),
                                             tile_position=(0, 32 * e))
                        if h == 0 and i == 3:
                            ins.then_inc(e_first, 1)
                    ins.then_inc(e_used, 1)
                for h in range(2):
                    eng.wait_ge((e_y, e_y2)[h], g + 1)
                    for t in range(TOK):
                        ins = pe_.matmul(bank[4 + 2 * t + h][:, :], ohT[:, g, t * P:(t + 1) * P],
                                         yE[:, 512 * h:512 * h + 512], start=(g == 0), stop=(g == NG - 1))
                        if g == NG - 1 or (h, t) == (1, TOK - 1):
                            ins.then_inc(e_out, 1)

        @block.vector
        def _(eng):
            dve = nc.vector
            steps = [0]
            n_mean = [0]

            def own(ins):
                steps[0] += 1
                ins.then_inc(dve_step, 1)
                eng.wait_ge(dve_step, steps[0])

            def mean_root(k, w, width, n_squares):
                eng.wait_ge(squares, n_squares)
                dve.tensor_scalar(ss[:, k:k + w], ss[:, k:k + w], 1.0 / width, EPS, ALU.mult, ALU.add).then_inc(means, 1)
                n_mean[0] += 1
                eng.wait_ge(roots, n_mean[0])

            def first_half(k, n_squares):
                eng.wait_ge(squares, n_squares)
                own(dve.tensor_scalar(ss[:, k:k + 1], ss[:, k:k + 1], 1.0 / D, EPS, ALU.mult, ALU.add))

            def half_root(k, k_first, n_squares):
                eng.wait_ge(squares, n_squares)
                dve.scalar_tensor_tensor(ss[:, k:k + 1], ss[:, k:k + 1], 1.0 / D, ss[:, k_first:k_first + 1],
                                         ALU.mult, ALU.add).then_inc(means, 1)
                n_mean[0] += 1
                eng.wait_ge(roots, n_mean[0])

            def turned_mod(name, dst, add, mult):
                filled(eng, name)
                t, h = int(name[-2]), int(name[-1])
                for c in range(4):
                    k = 4 * h + c
                    o, i = dst[:, k, t * P:(t + 1) * P], D_(name)[:, c * P:(c + 1) * P]
                    if add is None:
                        ins = dve.tensor_scalar(o, i, mult[:, k:k + 1], None, ALU.mult)
                    else:
                        ins = dve.tensor_scalar(o, i, mult[:, k:k + 1], add[:, k:k + 1], ALU.mult, ALU.add)
                leave(ins, name)

            def normalise(t, k, n_squares, dst=rn):
                mean_root(k + t, 1, D, n_squares)
                dve.tensor_scalar(dst[:, t, :], xn[:, t, :], rs[:, k + t:k + t + 1], None, ALU.mult).then_inc(normed, 1)

            def block1_norm(t):
                mean_root(4 + t, 1, D, 5 + 2 * t)
                eng.wait_ge(post_in, 16)
                own(dve.scalar_tensor_tensor(rn[:, t, :], rn[:, t, :], rs[:, 4 + t:5 + t], post, ALU.mult, ALU.mult))
                dve.tensor_tensor(xn[:, t, :], xn[:, t, :], rn[:, t, :], ALU.add).then_inc(x1_ready, 1)
                eng.wait_ge(x1_ready, t + 1)

            def rotate(x, t, heads, n, at):
                w = 4 * n
                cos = rope[:, at + t * w:at + (t + 1) * w]
                sin = rope[:, at + (TOK + t) * w:at + (TOK + t + 1) * w]
                a, b = (rt[:, i, 0:heads * w].rearrange("p (h d) -> p h d", h=heads) for i in range(2))
                dve.tensor_tensor(a, x, over(cos, heads), ALU.mult)
                b5 = rt[:, 1, 0:heads * w].rearrange("p (h a f n) -> p h a f n", h=heads, a=2, f=2)
                s4 = sin.rearrange("p (h a f n) -> p h a f n", h=1, a=2, f=2)
                x5 = x.rearrange("p h (a f n) -> p h a f n", a=2, f=2)
                for f in range(2):
                    ins = dve.tensor_tensor(b5[:, :, :, f, :], x5[:, :, :, 1 - f, :],
                                            s4[:, :, :, f, :].to_broadcast([P, heads, 2, n]), ALU.mult)
                own(ins)
                return dve.tensor_tensor(x, a, b, ALU.add)

            def rope_queries(t):
                kept(eng, f"xa{t}0")
                rotate(px[:, t, 0:512].rearrange("p (h d) -> p h d", d=HD), t, 8, 16, 0).then_inc(roped, 1)
                eng.wait_ge(roped, t + 1)

            def late_x(t):
                kept(eng, f"xa{t}1")
                kept(eng, f"xa{t}2")
                own(rotate(px[:, t, KA:KA + P].rearrange("p (h d) -> p h d", d=HD), t, 2, 16, 0))
                own(rotate(px[:, t, KR:KR + ROPE].rearrange("p (h d) -> p h d", h=1), t, 1, 8, 256))
                own(dve.tensor_copy(kcat[:, TOK + t, :, NOPE:QK], over(px[:, t, KR:KR + ROPE], HB)))
                i = 10 + 2 * t
                eng.wait_ge(squares, i)
                dve.tensor_scalar(ss[:, i:i + 1], ss[:, i:i + 1], 1.0 / QR, EPS, ALU.mult, ALU.add)
                dve.tensor_scalar(ss[:, i + 1:i + 2], ss[:, i + 1:i + 2], 1.0 / KVR, EPS, ALU.mult, ALU.add)\
                   .then_inc(means, 1)
                n_mean[0] += 1
                eng.wait_ge(roots, n_mean[0])
                dve.tensor_scalar(px[:, t, CQ:CQ + QR], px[:, t, CQ:CQ + QR], rs[:, i:i + 1], None, ALU.mult)
                dve.tensor_scalar(px[:, t, CKV:CKV + KVR], px[:, t, CKV:CKV + KVR], rs[:, i + 1:i + 2], None, ALU.mult)\
                   .then_inc(lat_ready, 1)

            def rope_q(t):
                kept(eng, f"qu{t}0")
                kept(eng, f"qu{t}1")
                rotate(qcat[:, t, :, NOPE:QK], t, HB, 8, 256).then_inc(cat_ready, 1)
                eng.wait_ge(cat_ready, t + 2)

            def spread_keys(name, src, dst):
                dve.tensor_copy(dst[0:64, 0], src[0:64])
                return dve.tensor_copy(dst[64:128, 1], src[64:128])

            for t in range(TOK):
                normalise(t, 0, t + 1, xrow)

            def unit_mask(u):
                kind, j = UNITS[u]
                eng.wait_ge(scores, u + 1)
                if u == 0:
                    eng.wait_ge(nsa_table_in, 16)
                if u in (8, 9):
                    eng.wait_ge(moba_table_in[u - 8], 16)
                if u >= 2:
                    eng.wait_ge(turns, u - 1)
                for b in range(2):
                    h = j + 4 * b if kind != MOBA else 2 * j + b
                    for q in range(TOK):
                        w = P if q == 0 else S
                        src = SB[1 - q][:, b * w:(b + 1) * w]
                        ins = dve.tensor_tensor_reduce(spn[:, u % 2, b, P * q:P * q + w], src,
                                                       table[:, h, P * q:P * q + w], 1.0, -3e38, ALU.add, ALU.max,
                                                       mx[:, u % 2, 2 * b + q:2 * b + q + 1])
                ins.then_inc(masked, 1)
                eng.wait_ge(masked, u + 1)
                dve.tensor_scalar(nm[:, u % 2, :], mx[:, u % 2, :], -1.0, None, ALU.mult).then_inc(maxed, 1)

            def unit_out(u):
                kind, j = UNITS[u]
                eng.wait_ge(pvs, u + 1)
                own(dve.reciprocal(rc[:, u, :], sums[:, u, :]))
                if kind != MOBA:
                    i = 8 * (kind + 1) + j
                    own(dve.tensor_tensor(rc[:, u, :].rearrange("p (b q) -> p b q", b=2),
                                          rc[:, u, :].rearrange("p (b q) -> p b q", b=2),
                                          gates[:, :, i:i + 5:4].rearrange("p q b -> p b q"), ALU.mult))
                for b in range(2):
                    h = j + 4 * b if kind != MOBA else 2 * j + b
                    for q in range(TOK):
                        o = VB[:, 128 * b + 64 * q:128 * b + 64 * q + 64]
                        r = rc[:, u, 2 * b + q:2 * b + q + 1]
                        dst = (ob if kind == MOBA else oa)[:, q, HD * h:HD * h + HD]
                        if kind == WIN:
                            ins = dve.scalar_tensor_tensor(dst, o, r, dst, ALU.mult, ALU.add)
                        else:
                            ins = dve.tensor_scalar(dst, o, r, None, ALU.mult)
                ins.then_inc(outs, 1)

            n_high = [0]

            def low_part(name, dst, high):
                n_high[0] += 1
                eng.wait_ge(high_ready, n_high[0])
                leave(dve.scalar_tensor_tensor(dst, D_(name)[:, :].rearrange("p (c s) -> p c s", c=4), 0.5, high.bitcast(F32),
                                               ALU.mult, ALU.subtract), name)

            for kind, n in SCHEDULE:
                if kind == "split":
                    n, q = n
                    name = SPLIT[n]
                    eng.wait_ge(split_a, 4 * n + q + 1)
                    dve.tensor_tensor(quarter(weight_parts[:, SLOT:], name, q), quarter(slot(name), name, q),
                                      quarter(weight_parts, name, q).bitcast(F32), ALU.subtract).then_inc(split_v, 1)
                elif kind == "score":
                    unit_mask(n)
                elif kind == "turn":
                    u = n
                    eng.wait_ge(turns, u + 1)
                    if u >= 2:
                        eng.wait_ge(pvs, u - 1)
                    dve.tensor_copy(ptn[:, u % 2, 1, :], TB[1][:, 0:CAUSAL]).then_inc(turned_b, 1)
                elif kind == "pv":
                    unit_out(n)
                elif kind == "mod":
                    if n % 4 == 3:
                        eng.wait_ge(mod_used, n + 1)
                        eng.wait_ge(bias_in[min(n // 4, 1)], 16)
                        dve.tensor_tensor(mod[:, n // 4, :], MB[:, :], bias[n // 4], ALU.add).then_inc(mod_kept, 1)
                elif kind == "ya":
                    eng.wait_ge(outs, 8)
                    kept(eng, "cO1")
                    dve.tensor_tensor(mo[:, 2048:3072], mo[:, 2048:3072], zz[:, 0:1024], ALU.mult).then_inc(ya_ready, 1)
                elif kind == "yb":
                    eng.wait_ge(outs, 12)
                    dve.tensor_tensor(mo[:, 3072:4096], mo[:, 3072:4096], zz[:, 1024:2048], ALU.mult).then_inc(yb_ready, 1)
                elif kind == "context":
                    eng.wait_ge(ctx_in, 16)
                    for t in range(TOK):
                        own(dve.tensor_tensor_reduce(pt[:, 0:D], cn[:, t, :], cn[:, t, :], 1.0, 0.0, ALU.mult,
                                                     ALU.add, ss[:, 2 + t:3 + t]))
                    mean_root(2, 2, D, 2)
                    for t in range(TOK):
                        dve.tensor_scalar(cn[:, t, :], cn[:, t, :], rs[:, 2 + t:3 + t], None, ALU.mult)\
                           .then_inc(normed, 1)
                elif kind == "dense":
                    name = n
                    if name[:2] == "xT":
                        if name == "xT00":
                            eng.wait_ge(early_in, 32)
                        filled(eng, name)
                        t, h = int(name[2]), int(name[3])
                        if h == 0:
                            own(dve.tensor_tensor(uhigh[:, 0:4, t * P:(t + 1) * P],
                                                  D_(name)[:, :].rearrange("p (c s) -> p c s", c=4),
                                                  bc(gcol[:, 0:4], P), ALU.mult))
                        else:
                            n_high[0] += 1
                            eng.wait_ge(high_ready, n_high[0])
                        for c in range(4):
                            k = 4 * h + c
                            ins = dve.scalar_tensor_tensor(xlow[:, k, t * P:(t + 1) * P], D_(name)[:, c * P:(c + 1) * P],
                                                           gcol[:, k:k + 1],
                                                           uhigh[:, k, t * P:(t + 1) * P].bitcast(F32), ALU.mult,
                                                           ALU.subtract)
                        leave(ins, name)
                    elif name == "kvc":
                        filled(eng, name)
                        leave(dve.tensor_copy(kvT, D_(name)[:, :].rearrange("p (i s) -> p i s", i=2)), name)
                    elif name == "kvs":
                        filled(eng, name)
                        spread_keys(name, D_(name)[:, 0:S], ksD)
                        leave(spread_keys(name, D_(name)[:, S:2 * S], kwD), name)
                    elif name in ("yaT0", "yaT1", "ybT0", "ybT1"):
                        t = int(name[3])
                        high, low = (yaT, yalow) if name[1] == "a" else (ybT, yblow)
                        low_part(name, low[:, :, t * P:(t + 1) * P], high[:, :, t * P:(t + 1) * P])
                    elif name[:2] == "mT":
                        t, h = int(name[2]), int(name[3])
                        low_part(name, mlow[:, 4 * h:4 * h + 4, t * P:(t + 1) * P], uhigh[:, 4 * h:4 * h + 4, t * P:(t + 1) * P])
                    elif name == "va1":
                        kept(eng, name)
                        own(dve.tensor_scalar(gates, gates, 0.5, 0.5, ALU.mult, ALU.add))
                        eng.wait_ge(kv2_in, 16 * 4)
                        eng.wait_ge(const_in, 16 * (len(constants) + 1))
                        eng.wait_ge(zeroed, 1)
                        for i in range(2):
                            for a in range(2):
                                src = kv2[:, i, :, :].rearrange("p g (n l r) -> p g n l r", l=8, r=2)
                                src = src[:, :, a:a + N_CMP, :, 0].rearrange("p g n l -> p l g n")
                                dst = blk[:, i, 8 * a:8 * a + 8, 0:2 * N_CMP].rearrange("p l (g n) -> p l g n", g=2)
                                pos = pe[:, i, 8 * a:8 * a + 8].rearrange("p (l g n) -> p l g n", g=1, n=1)
                                ins = dve.tensor_tensor(dst, src, pos.to_broadcast([P, 8, 2, N_CMP]), ALU.add)
                            ins.then_inc(blocks_ready, 1)
                        eng.wait_ge(cond_tanh, 1)
                        own(dve.scalar_tensor_tensor(ccE, ccE, 1.0, cc, ALU.add, ALU.mult))
                        dve.tensor_scalar(csil[:, :, 0:2], ccE.rearrange("p (c v) -> p c v", c=KC), 0.5, None, ALU.mult)\
                           .then_inc(cond_ready, 1)
                    elif name in ("kb0", "kb1"):
                        filled(eng, name)
                        i = int(name[2])
                        src = D_(name)[:, :].rearrange("p (j s) -> p j s", j=2)
                        dve.tensor_copy(kbD[0:64, 2 * i:2 * i + 2, 0, :], src[0:64])
                        leave(dve.tensor_copy(kbD[64:128, 2 * i:2 * i + 2, 1, :], src[64:128]), name)
                    elif name in ("za0", "za1", "zb0", "zb1"):
                        k = {"za0": 1, "za1": 2, "zb0": 3, "zb1": 4}[name]
                        eng.wait_ge(tanhs, k)
                        z = (za if name[1] == "a" else zb)[:, int(name[2]), :]
                        leave(dve.scalar_tensor_tensor(z, z, 1.0, D_(name)[:, :], ALU.add, ALU.mult), name)
                    elif name == "cT":
                        filled(eng, name)
                        halves = D_(name)[:, 0:P].rearrange("p (i a n) -> p a i n", i=2, a=2)
                        own(dve.tensor_copy(cH, halves[:, 0, :, 0:30]))
                        leave(dve.tensor_tensor(cH, cH, halves[:, 1, :, 0:30], ALU.add), name)
                        kept(eng, name)
                        eng.wait_ge(c_act, 1)
                        own(dve.scalar_tensor_tensor(cH, cE, 1.0, cH, ALU.add, ALU.mult))
                        dve.tensor_scalar(hkT, cH[:, 0, :], 0.5, None, ALU.mult)
                        for g in range(2):
                            ins = dve.tensor_scalar(hvR[:, g, :, 0:15], over(cH[:, 1, 15 * g:15 * g + 15], 4), 0.5, None, ALU.mult)
                        ins.then_inc(c_vec, 1)
                    elif name == "cK":
                        filled(eng, name)
                        for g in range(2):
                            dve.tensor_copy(kcD[64 * g:64 * g + 64, g, 0:15], D_(name)[64 * g:64 * g + 64, 15 * g:15 * g + 15])
                        for g in range(2):
                            for h in range(4):
                                ins = dve.tensor_copy(vcD[32 * h:32 * h + 32, g, 64 * h:64 * h + 64],
                                                      D_(name)[32 * h:32 * h + 32, 64 + 64 * g:128 + 64 * g])
                        leave(ins, name)
                    elif name == "cS":
                        filled(eng, name)
                        leave(dve.tensor_tensor(cS, D_(name)[:, 0:256], cB, ALU.add), name)
                        kept(eng, name)
                        s3 = cS.rearrange("p (i n) -> p i n", n=CMPW)
                        own(dve.tensor_reduce(cst[:, 0, :], s3, AX_X, ALU.max))
                        dve.tensor_tensor(s3, s3, bc(cst[:, 0, :], CMPW), ALU.subtract).then_inc(c_vec, 1)
                        eng.wait_ge(c_act, 2)
                        own(dve.tensor_tensor(cS, cS, cM, ALU.mult))
                        own(dve.tensor_reduce(cst[:, 0, :], s3, AX_X, ALU.add))
                        own(dve.tensor_scalar(cst[:, 0, :], cst[:, 0, :], 1e-30, None, ALU.max))
                        own(dve.reciprocal(cst[:, 1, :], cst[:, 0, :]))
                        for q in range(TOK):
                            ins = dve.tensor_tensor(cst[:, 0, 8 * q:8 * q + 8].rearrange("p (j g) -> p j g", g=2),
                                                    cst[:, 1, 8 * q:8 * q + 8].rearrange("p (j g) -> p j g", g=2),
                                                    gates[:, q, 0:8].rearrange("p (g j) -> p j g", g=2), ALU.mult)
                        own(ins)
                        own(dve.tensor_tensor(s3, s3, bc(cst[:, 0, :], CMPW), ALU.mult))
                        eng.wait_ge(zeroed, 2)
                        s5 = cS.rearrange("p (q j g n) -> p q j g n", q=2, j=4, g=2)
                        for q in range(TOK):
                            for g in range(2):
                                ins = dve.tensor_copy(cP[:, 2 * q + g, :, 0:CMPW], s5[:, q, :, g, :])
                        ins.then_inc(c_vec, 1)
                    elif name in ("cO0", "cO1"):
                        q = int(name[2])
                        filled(eng, name)
                        eng.wait_ge(outs, 8)
                        leave(dve.tensor_tensor(oa[:, q, :], oa[:, q, :], D_(name)[:, :], ALU.add), name)
                    elif name[:2] == "wa":
                        t, h = int(name[2]), int(name[3])
                        filled(eng, name)
                        kept(eng, f"gA{t}{h}")
                        leave(dve.scalar_tensor_tensor(mrow[:, t, 512 * h:512 * h + 512], eg[:, t, 512 * h:512 * h + 512], 1.0,
                                                       D_(name)[:, :], ALU.add, ALU.mult), name)
                    elif name[:2] == "wb":
                        t, h = int(name[2]), int(name[3])
                        filled(eng, name)
                        kept(eng, f"gB{t}{h}")
                        e = eg[:, t, 512 * h:512 * h + 512]
                        leave(dve.scalar_tensor_tensor(e, e, 1.0, D_(name)[:, :], ALU.add, ALU.mult), name)
                        kept(eng, name)
                        m = mrow[:, t, 512 * h:512 * h + 512]
                        dve.tensor_tensor(m, m, e, ALU.add).then_inc(m_ready, 1)
                    elif name[:4] == "modT":
                        r = int(name[4])
                        filled(eng, name)
                        src = D_(name)[:, :].rearrange("p (b j v) -> p v j b", b=4, j=4)
                        for v in range(2):
                            ins = dve.tensor_copy(mc[:, v, 16 * r:16 * r + 16].rearrange("p (j b) -> p j b", j=4), src[:, v, :, :])
                        leave(ins, name)
                        kept(eng, name)
                        if r == 0:
                            for v in range(2):
                                ins = dve.scalar_tensor_tensor(scl[:, v, :], mc[:, v, 8:16], 1.0, nat, ALU.add, ALU.mult)
                            own(ins)
                        if r == 2:
                            own(dve.scalar_tensor_tensor(scl[:, 2, :], mc[:, 0, 32:40], 1.0, nff, ALU.add, ALU.mult))
                    elif name in ("cxT00", "cxT10"):
                        turned_mod(name, hcT, mc[:, 1, 0:8], scl[:, 1, :])
                    elif name == "cc1":
                        mean_root(6, 2, KVR, 4)
                        for t in range(TOK):
                            ins = dve.tensor_scalar(pc[:, t, 256:512], pc[:, t, 256:512], rs[:, 6 + t:7 + t], None, ALU.mult)
                        ins.then_inc(lat_ready, 1)
                    elif name == "clT":
                        filled(eng, name)
                        for c in range(2):
                            ins = dve.tensor_scalar(lcT[:, c, :], D_(name)[:, c * S:(c + 1) * S], kvn[:, c:c + 1], None, ALU.mult)
                        leave(ins, name)
                        for t in range(TOK):
                            ins = dve.tensor_copy(kcat[:, t, :, NOPE:QK], over(pc[:, t, 512:544], HB))
                        ins.then_inc(cat_ready, 1)
                    elif name[:2] == "wo" and name[3] == "1":
                        t = int(name[2])
                        block1_norm(t)
                        if t == 0:
                            normalise(0, 8, 6)
                    elif name[:2] == "hT":
                        t, h = int(name[2]), int(name[3])
                        c, q = slice(4 * h, 4 * h + 4), slice(t * P, (t + 1) * P)
                        if h == 0:
                            turned_mod(name, hfull, mc[:, 0, 0:8], scl[:, 0, :])
                            kept(eng, name)
                            own(dve.tensor_copy(uhigh[:, c, q], hfull[:, c, q]))
                        else:
                            n_high[0] += 1
                            eng.wait_ge(high_ready, n_high[0])
                        dve.tensor_tensor(hlow[:, c, q], hfull[:, c, q], uhigh[:, c, q].bitcast(F32), ALU.subtract)\
                           .then_inc(h_ready, 1)
                        if name == "hT01":
                            normalise(1, 8, 8)
                    elif name in ("xa01", "xa11"):
                        late_x(int(name[2]))
                    elif name == "xa10":
                        rope_queries(0)
                    elif name == "kwT":
                        filled(eng, name)
                        eng.wait_ge(kp_zeroed, 1)
                        leave(spread_keys(name, D_(name)[:, :], kP), name)
                        dve.tensor_copy(xv.rearrange("p (t d) -> p t d", t=TOK), px[:, :, VA:VA + P])
                    elif name[:2] in ("lq", "lk"):
                        filled(eng, name)
                        t = int(name[2])
                        dst, w, n_ = (lqT, qn, 3) if name[1] == "q" else (lkT, kvn, 2)
                        leave(dve.tensor_tensor(dst[:, :, t * P:(t + 1) * P],
                                                D_(name)[:, 0:n_ * P].rearrange("p (c s) -> p c s", c=n_), bc(w, P),
                                                ALU.mult), name)
                        if name == "lk1":
                            rope_queries(1)
                    elif name in ("qu01", "qu11"):
                        rope_q(int(name[2]))
                    elif name[:2] in ("qm", "kx", "kc") and int(name[2]) % 2 == 1:
                        filled(eng, name)
                        leave(dve.tensor_copy(mla_turned(name), D_(name)[0:QK, :].rearrange("p (h s) -> p h s", h=2)),
                              name)

            def unit_max(u):
                q = u % 2
                eng.wait_ge(u_scores, u + 1)
                if u == 0:
                    eng.wait_ge(wmask_in, 16)
                if u < 16:
                    if u >= 3:
                        eng.wait_ge(u_turn, u - 2)
                    ins = dve.tensor_tensor_reduce(sp3[:, u % 3, :], SB[u % 2][:, :], wB[:, q, :], 1.0, -3e38, ALU.add,
                                                   ALU.max, mx2[:, u:u + 1])
                else:
                    ins = dve.tensor_reduce(mx2[:, u:u + 1], SB[u % 2][:, :], AX_X, ALU.max)
                ins.then_inc(u_masked, 1)

            def unit_neg(u):
                eng.wait_ge(u_masked, u + 1)
                if u < 16:
                    h = u // 2 % 2 * 4 + u // 4
                    ins = dve.tensor_scalar(nm2[:, u:u + 1], mx2[:, u:u + 1], sink[:, h:h + 1], -1.0, ALU.max, ALU.mult)
                else:
                    ins = dve.tensor_scalar(nm2[:, u:u + 1], mx2[:, u:u + 1], -MLA_SCALE, None, ALU.mult)
                ins.then_inc(u_neg, 1)

            def unit_sum(u):
                eng.wait_ge(u_exp, u + 1)
                if u < 16:
                    eng.wait_ge(u_sink, u + 1)
                    dve.tensor_tensor(sm2[:, u:u + 1], sm2[:, u:u + 1], sk2[:, u:u + 1], ALU.add).then_inc(u_summed, 1)

            def unit_norm(u):
                if u < 16:
                    eng.wait_ge(u_summed, u + 1)
                own(dve.reciprocal(rc2[:, u:u + 1], sm2[:, u:u + 1]))
                dve.tensor_scalar(sp3[:, u % 3, :], sp3[:, u % 3, :], rc2[:, u:u + 1], None, ALU.mult).then_inc(u_norm, 1)

            for r in range(34):
                if r < 32:
                    unit_max(r)
                if 1 <= r <= 32:
                    unit_sum(r - 1)
                if r < 32:
                    unit_neg(r)
                if 1 <= r <= 32:
                    unit_norm(r - 1)
                if r >= 2 and vector_turns(r - 2):
                    unit_turned(eng, r - 2, dve.tensor_copy).then_inc(u_turned_v, 1)

            def chosen(src, g):
                for i in range(4):
                    c = 4 + i
                    ins = dve.tensor_scalar(xs[:, g % 2, c, :], src[:, i * P:(i + 1) * P], scl[:, 2, c:c + 1],
                                            mc[:, 0, 24 + c:25 + c], ALU.mult, ALU.add)
                return ins

            for name in TAIL:
                if name[:2] == "ou":
                    t, h = int(name[2]), int(name[3])
                    if h == 1:
                        first_half(t, 13 + 2 * t)
                    filled(eng, name)
                    r = rn[:, t, 512 * h:512 * h + 512]
                    x = xn[:, t, 512 * h:512 * h + 512]
                    leave(dve.tensor_tensor(r, D_(name)[:, :], gG[:, 512 * h:512 * h + 512], ALU.mult), name)
                    kept(eng, name)
                    dve.tensor_tensor(x, x, r, ALU.add).then_inc(x2_ready, 1)
                    if h == 1:
                        half_root(14 + t, t, 14 + 2 * t)
                        for w in range(2):
                            cols = slice(512 * w, 512 * w + 512)
                            dve.tensor_scalar(rn[:, t, cols], xn[:, t, cols], rs[:, 14 + t:15 + t], None, ALU.mult)\
                               .then_inc(normed, 1)
                elif name in ("rT00", "rT10"):
                    turned_mod(name, uT, mc[:, 0, 24:32], scl[:, 2, :])
                elif name in ("lg0", "lg1"):
                    filled(eng, name)
                    t = int(name[2])
                    dve.tensor_reduce(rst[:, t:t + 1], D_(name)[:, 0:E], AX_X, ALU.max, negate=True).then_inc(logit_max, 1)
                    kept(eng, name)
                    own(dve.reciprocal(rst[:, 4 + t:5 + t], rst[:, 2 + t:3 + t]))
                    dve.tensor_scalar(aff[:, t, :], aff[:, t, :], rst[:, 4 + t:5 + t], None, ALU.mult).then_inc(aff_ready, 1)
                elif name == "afT":
                    dve.memset(zer[0:E], 0.0)
                    filled(eng, name)
                    leave(dve.tensor_copy(affT[0:E], D_(name)[0:E, 0:S]), name)
                    kept(eng, name)
                    cur = affT
                    for i in range(CAP // 8):
                        own(dve.max(top8[0:E], cur[0:E]))
                        nxt = work if cur is affT else affT
                        own(dve.match_replace(nxt[0:E], top8[0:E], cur[0:E], -1.0))
                        cur = nxt
                    own(dve.tensor_scalar(msk[0:E], cur[0:E], 0.0, None, ALU.is_lt))
                    own(dve.tensor_tensor_scan(cum[0:E], msk[0:E], zer[0:E], 0.0, ALU.add, ALU.add))
                    dve.tensor_tensor(cum[0:E], cum[0:E], msk[0:E], ALU.mult).then_inc(slots_ready, 1)
                elif name == "slT":
                    filled(eng, name)
                    leave(dve.tensor_copy(slt, D_(name)[:, 0:2 * E].rearrange("p (t e) -> p t e", t=TOK)), name)
                    kept(eng, name)
                    for lo, n_ in ((0, EG), (EG, E - EG)):
                        for t in range(TOK):
                            ins = dve.tensor_tensor(oh[:, t, lo * CAP:(lo + n_) * CAP].rearrange("p (e s) -> p e s", e=n_),
                                                    bc(slt[:, t, lo:lo + n_], CAP), over(iota, n_), ALU.is_equal)
                        ins.then_inc(oh_ready, 1)
                elif name == "gx1":
                    filled(eng, name)
                    leave(chosen(D_(name), 0), name)
                    eng.wait_ge(oh_ready, 2)
                    for t in range(TOK):
                        ins = dve.tensor_tensor(ohv[:, t, :].rearrange("p (e s) -> p e s", e=E),
                                                oh[:, t, :].rearrange("p (e s) -> p e s", e=E), bc(aff[:, t, :], CAP), ALU.mult)
                    ins.then_inc(oh_ready, 1)

            for g in range(NG):
                eng.wait_ge(e_tanh, g + 1)
                own(dve.scalar_tensor_tensor(hA, hE, 1.0, bank[0][:, :], ALU.add, ALU.mult))
                experts_done(eng, "U", g)
                dve.tensor_tensor(hA, hA, bank[1][:, :], ALU.mult).then_inc(e_h, 1)
                if g == 0:
                    eng.wait_ge(side_turn, 1)
                    dve.tensor_copy(ohT[:, 2:4, :], bank[3][:, :].rearrange("p (g s) -> p g s", g=2)).then_inc(side_v, 1)
                if g < NG - 1:
                    eng.wait_ge(side_turn, g + 2)
                    chosen(bank[3], g + 1).then_inc(side_v, 1)
                experts_done(eng, "D", g)
                if g:
                    eng.wait_ge(e_out, g)
                dve.tensor_copy(yE[:, 512:1024], bank[3][:, :]).then_inc(e_y2, 1)

            for h in range(2):
                cols = slice(512 * h, 512 * h + 512)
                for t in range(TOK):
                    eng.wait_ge(e_out, NG + TOK * h + t)
                    ins = dve.tensor_tensor(rn[:, t, cols], bank[4 + 2 * t + h][:, :], gF[:, cols], ALU.mult)
                own(ins)
                for t in range(TOK):
                    dve.tensor_tensor(xn[:, t, cols], xn[:, t, cols], rn[:, t, cols], ALU.add).then_inc(f_in, 1)
            for t in range(TOK):
                first_half(t, 17 + t)
            eng.wait_ge(fin_in, 16)
            for t in range(TOK):
                half_root(4 + t, t, 19 + t)
                dve.scalar_tensor_tensor(xn[:, t, :], xn[:, t, :], rs[:, 4 + t:5 + t], nfin, ALU.mult, ALU.mult)\
                   .then_inc(y_ready, 1)


def shape_tables():
    q = np.arange(S)
    dist = (q[:, None] - q[None, :]).astype(np.float32)
    slopes = alibi(16)
    far = np.where(dist < 0, np.float32(FAR), dist)

    def table(sl):
        out = np.zeros((P, 8, CAUSAL), np.float32)
        for h in range(8):
            b = -np.float32(sl[h]) * far
            out[:, h, 0:P] = b[0:P, 0:P]
            out[:, h, P:CAUSAL] = b[P:S, :]
        return out.reshape(P, -1)

    end = np.arange(N_CMP) * 16 + 31
    cd = (q[:, None] - end[None, :]).astype(np.float32)
    bias = np.full((P, 2, 4, 2, CMPW), -FAR, np.float32)
    mask = np.zeros((P, 2, 4, 2, CMPW), np.float32)
    for t in range(2):
        for j in range(4):
            for g in range(2):
                d = cd[t * P:(t + 1) * P]
                bias[:, t, j, g, :N_CMP] = np.where(d >= 0, -np.float32(slopes[0::2][4 * g + j]) * d, -FAR)
                mask[:, t, j, g, :N_CMP] = d >= 0
    win = np.zeros((P, 2, 512), np.float32)
    for t in range(2):
        win[:, t, S:] = np.where(np.abs(dist[t * P:(t + 1) * P]) <= 128, 0.0, -FAR)

    def rotary(n):
        inv = 10000.0 ** (-np.arange(n, dtype=np.float32) / n)
        pos = np.stack([q // 64, q % 64], 1).astype(np.float32)
        ang = (pos[:, :, None] * inv[None, None, :]).astype(np.float32)
        c, s = np.cos(ang), np.sin(ang)
        cos = np.concatenate([c, c], 2).reshape(S, 4 * n)
        sin = np.concatenate([-s, s], 2).reshape(S, 4 * n)
        return [np.concatenate([m[0:P], m[P:S]], 1) for m in (cos, sin)]

    rope = np.concatenate(rotary(16) + rotary(8), 1).astype(np.float32)
    return {
        "ident": np.eye(P, dtype=np.float32), "nsa_table": table(slopes[0::2]), "moba_table": table(slopes[1::2]),
        "cmp_bias": bias.reshape(P, -1), "cmp_mask": mask.reshape(P, -1), "window_mask": win.reshape(P, -1),
        "rope": rope, "iota": np.tile(np.arange(1, CAP + 1, dtype=np.float32), (P, 1)),
    }


def chunks(w):
    return w.reshape(-1, P, w.shape[1]).transpose(1, 0, 2)


def stream_of(a):
    w = a["w_in"][0]
    pair = np.concatenate([np.arange(64) + 64 * h for j in range(4) for h in (j, 4 + j)])
    kv = lambda i: w[:, 512 + 128 * i:640 + 128 * i]
    parts = {"W0": w[:, pair], "W1": np.concatenate([kv(0), kv(1), kv(2), kv(4)], 1),
             "W2": np.concatenate([kv(3), kv(5), w[:, 1280:1304]], 1),
             "W6": w[:, 1304:1816], "W3": w[:, 1816:2328], "W4": w[:, 2328:2840], "W5": w[:, 2840:3352],
             "W7": w[:, 3352:3864]}
    for i in range(4):
        parts[f"W{8 + i}"] = w[:, 3864 + 512 * i:4376 + 512 * i]
    w2 = a["w_in_2"][0]
    ckv, kr = w2[:, 1152:1408], w2[:, 1408:1440]
    parts |= {"C0": w2[:, 512:768], "C1": np.concatenate([ckv, kr], 1), "X0": w2[:, pair],
              "X1": np.concatenate([w2[:, 512:768], ckv], 1), "X2": np.concatenate([w2[:, 768:1152], kr], 1),
              "WA": a["w_branch_a"][0], "WB": a["w_branch_b"][0], "QU": a["w_q_up_2"][0],
              "KU0": a["w_kv_up_2"][0], "KU1": a["w_kv_up_2"][0]}
    out_rows = np.concatenate([pair, np.arange(512, D)])
    for i in range(2):
        parts[f"WO{i}"] = a["w_o"][0][:, 512 * i:512 * i + 512]
        parts[f"OUT{i}"] = a["w_out_2"][0][out_rows, 512 * i:512 * i + 512]
    flat = {n: chunks(p).reshape(P, -1) for n, p in parts.items()}
    for n, width in WIDTH.items():
        flat[n] = np.pad(chunks(parts[n]), ((0, 0), (0, 0), (0, 512 - width))).reshape(P, -1)
    for n in ("WA", "WB"):
        flat[n] = chunks(parts[n]).reshape(P, 4, 2, 512).transpose(0, 2, 1, 3).reshape(P, -1)
    flat["WC"] = np.concatenate([chunks(a[f"cmp_w1_{k}"][0].reshape(-1, P)).reshape(P, -1) for k in "kv"], 1)
    wm = chunks(a["w_mod_2"][0])
    for n in range(12):
        flat[f"M{n}"] = wm[:, 2 * (n % 4):2 * (n % 4) + 2, 2048 * (n // 4):2048 * (n // 4) + 2048].reshape(P, -1)
    out = np.zeros((len(STREAM), P, SLOT), np.float32)
    for g in range(NG):
        for m, src in (("G", "w_gate_2"), ("U", "w_up_2"), ("D", "w_down_2")):
            e = a[src][0][EG * g:EG * g + EG]
            e = e.reshape(EG, -1, P, e.shape[2]).transpose(2, 0, 1, 3)
            for i in range(4):
                flat[f"{m}{g}.{i}"] = (e[:, :, 2 * i:2 * i + 2] if m != "D" else e[:, :, i]).reshape(P, -1)
    for n, name in enumerate(STREAM):
        out[n, :, :flat[name].shape[1]] = flat[name]
    return out


def host_arrays(a):
    col = lambda v: np.ascontiguousarray(v.reshape(-1, P).T)
    pe = np.concatenate([a[f"cmp_pe_{k}_"].reshape(LP, P).T for k in "kv"], 1)
    cond = np.stack([col(a["c_2"]), col(a["c_ctx_2"])], 2).reshape(P, -1)
    mod_bias = np.zeros((4, 32, 3, 512), np.float32)
    mod_bias[:, 0:2] = a["b_mod_2"][0].reshape(3, 4, 1, 512).transpose(1, 2, 0, 3)
    return {
        "stream": stream_of(a), "x": a["x"][0], "ctx": a["ctx_2"][0],
        "norm_pre": col(a["norm_pre"][0]), "norm_post": a["norm_post"], "norm_attn": col(a["norm_attn_2"][0]),
        "norm_ffn": col(a["norm_ffn_2"][0]), "norm_final": a["norm_final_2"].reshape(1, D),
        "mod_bias": mod_bias.reshape(P, -1), "q_norm": col(a["q_norm_2"][0]),
        "kv_norm": col(a["kv_norm_2"][0]), "sink": a["sink_2"], "cond": cond, "pe": pe,
        "w2k": np.concatenate([a["cmp_w2_k"][0]] * 2, 1), "w2v": a["cmp_w2_v"][0],
        "w_router": chunks(a["w_router_2"][0]).reshape(P, -1), **shape_tables(),
    }


def kernel(**inputs):
    import concourse.bacc as bacc
    from concourse.bass_utils import run_bass_kernel_spmd

    a = {k: np.asarray(v) for k, v in inputs.items()}
    a |= {f"cmp_pe_{k}_": a[f"cmp_pe_{k}"][0] for k in "kv"}
    nc = bacc.Bacc("TRN2", target_bir_lowering=False, num_devices=1)
    arrays, args = {}, {}
    for name, v in host_arrays(a).items():
        v = np.ascontiguousarray(v)
        arrays[f"in_{name}"] = v
        args[name] = nc.dram_tensor(f"in_{name}", v.shape, mybir.dt.from_np(v.dtype), kind="ExternalInput").ap()
    y = nc.dram_tensor("out_y", (S, D), F32, kind="ExternalOutput").ap()
    build(nc, args, y)
    got = run_bass_kernel_spmd(nc, [arrays], core_ids=[0])
    return got.results[0]["out_y"].reshape(1, S, D)
```
